# Optimizing a Trainium2 kernel written in Bass

```python
import math
import jax, jax.numpy as jnp
from jax import lax
import numpy as np
import jax
import jax.numpy as jnp

D_MODEL = 1024
BATCH = 1
SEQ = 512
DEPTH = 2

GRID_W = 64
CTX_LEN = 256
N_MIXERS = 2
N_ATT_LAYERS = (DEPTH + 1) // 2
N_SSM_LAYERS = DEPTH // 2

ATT_HEADS = 16
ATT_KV_HEADS = 4
HEAD_DIM = 64
ATT_GROUP = ATT_HEADS // ATT_KV_HEADS
ATT_DIM = ATT_HEADS * HEAD_DIM
ATT_IN_DIM = ATT_DIM + 2 * ATT_KV_HEADS * HEAD_DIM
WINDOW = 128
BLOCK = 128
SPAN = BLOCK + 2 * WINDOW
ROPE_BASE = 10000.0
ROPE_AXIS_DIM = HEAD_DIM // 2

SSM_D_INNER = 2 * D_MODEL
SSM_HEAD_DIM = 64
SSM_HEADS = SSM_D_INNER // SSM_HEAD_DIM
SSM_GROUPS = 4
SSM_GROUP_HEADS = SSM_HEADS // SSM_GROUPS
SSM_STATE = 128
SSM_CONV_W = 5
SSM_CHUNK = 128
SSM_CONV_DIM = SSM_D_INNER + 2 * SSM_GROUPS * SSM_STATE
SSM_IN_DIM = SSM_D_INNER + SSM_CONV_DIM + 2 * SSM_HEADS
SSM_NORM_GROUPS = SSM_GROUPS

FF_DIM = 4 * D_MODEL
N_MOD = 6
ALPHA = (2.0 * DEPTH) ** 0.25
BETA = (8.0 * DEPTH) ** -0.25
LN_EPS = 1e-5
RMS_EPS = 1e-5
NEG_INF = -1e30


def layer_norm(x, g, b):
    xf = x.astype(jnp.float32)
    mu = jnp.mean(xf, axis=-1, keepdims=True)
    var = jnp.mean(jnp.square(xf - mu), axis=-1, keepdims=True)
    y = (xf - mu) * lax.rsqrt(var + LN_EPS) * g.astype(jnp.float32) + b.astype(jnp.float32)
    return y.astype(x.dtype)

def modulate(h, shift, scale):
    return h * (1.0 + scale) + shift

def squared_relu_mlp(h, w1, w2):
    return jnp.square(jax.nn.relu(h @ w1)) @ w2

def axial_rope_tables(rows):
    row = jnp.repeat(jnp.arange(rows), GRID_W).astype(jnp.float32)
    col = jnp.tile(jnp.arange(GRID_W), rows).astype(jnp.float32)
    inv_freq = ROPE_BASE ** (-jnp.arange(0, ROPE_AXIS_DIM, 2, dtype=jnp.float32) / ROPE_AXIS_DIM)
    ang_r = row[:, None] * inv_freq[None, :]
    ang_c = col[:, None] * inv_freq[None, :]
    return (jnp.cos(ang_r), jnp.sin(ang_r), jnp.cos(ang_c), jnp.sin(ang_c))

def rotate_half(x, cos, sin):
    x1, x2 = jnp.split(x, 2, axis=-1)
    return jnp.concatenate([x1 * cos - x2 * sin, x2 * cos + x1 * sin], axis=-1)

def apply_axial_rope(x, tables):
    cos_r, sin_r, cos_c, sin_c = tables
    bshape = (x.shape[1],) + (1,) * (x.ndim - 3) + (-1,)
    xf = x.astype(jnp.float32)
    xr = rotate_half(xf[..., :ROPE_AXIS_DIM], cos_r.reshape(bshape), sin_r.reshape(bshape))
    xc = rotate_half(xf[..., ROPE_AXIS_DIM:], cos_c.reshape(bshape), sin_c.reshape(bshape))
    return jnp.concatenate([xr, xc], axis=-1).astype(x.dtype)

def attention_mixer(u_lat, u_ctx, w_in, w_out, sink, rope, need_ctx_out):
    bsz, n, _ = u_lat.shape
    n_ctx = u_ctx.shape[1]
    nb = n // BLOCK
    scale = HEAD_DIM ** -0.5
    sink_f = sink.astype(jnp.float32).reshape(ATT_KV_HEADS, ATT_GROUP)

    def project(u):
        length = u.shape[1]
        q, k, v = jnp.split(u @ w_in, [ATT_DIM, ATT_DIM + ATT_KV_HEADS * HEAD_DIM], axis=-1)
        return (q.reshape(bsz, length, ATT_KV_HEADS, ATT_GROUP, HEAD_DIM),
                k.reshape(bsz, length, ATT_KV_HEADS, HEAD_DIM),
                v.reshape(bsz, length, ATT_KV_HEADS, HEAD_DIM))

    def sink_softmax(logits):
        s = jnp.broadcast_to(sink_f[None, :, :, None, None], logits.shape[:-1] + (1,))
        return jax.nn.softmax(jnp.concatenate([logits, s], axis=-1), axis=-1)

    q_l, k_l, v_l = project(u_lat)
    q_c, k_c, v_c = project(u_ctx)
    qr_l = apply_axial_rope(q_l, rope)
    kr_l = apply_axial_rope(k_l, rope)
    pad = ((0, 0), (WINDOW, WINDOW), (0, 0), (0, 0))
    k_pad = jnp.pad(kr_l, pad)
    v_pad = jnp.pad(v_l, pad)
    q_blocks = jnp.moveaxis(qr_l.reshape(bsz, nb, BLOCK, ATT_KV_HEADS, ATT_GROUP, HEAD_DIM), 1, 0)
    qp_blocks = jnp.moveaxis(q_l.reshape(bsz, nb, BLOCK, ATT_KV_HEADS, ATT_GROUP, HEAD_DIM), 1, 0)
    offs_q = jnp.arange(BLOCK)
    offs_k = jnp.arange(SPAN) - WINDOW

    def block_attend(args):
        blk, qb, qpb = args
        start = blk * BLOCK
        kw = lax.dynamic_slice_in_dim(k_pad, start, SPAN, axis=1)
        vw = lax.dynamic_slice_in_dim(v_pad, start, SPAN, axis=1)
        qi = start + offs_q
        kj = start + offs_k
        ok = (kj[None, :] >= 0) & (kj[None, :] < n) & (jnp.abs(qi[:, None] - kj[None, :]) <= WINDOW)
        s_win = jnp.einsum('blgrd,bsgd->bgrls', qb, kw).astype(jnp.float32) * scale
        s_win = jnp.where(ok, s_win, NEG_INF)
        s_ctx = jnp.einsum('blgrd,bsgd->bgrls', qpb, k_c).astype(jnp.float32) * scale
        p = sink_softmax(jnp.concatenate([s_win, s_ctx], axis=-1)).astype(vw.dtype)
        return (jnp.einsum('bgrls,bsgd->blgrd', p[..., :SPAN], vw)
                + jnp.einsum('bgrls,bsgd->blgrd', p[..., SPAN:SPAN + n_ctx], v_c))

    o = lax.map(block_attend, (jnp.arange(nb), q_blocks, qp_blocks))
    y_lat = jnp.moveaxis(o, 0, 1).reshape(bsz, n, ATT_DIM) @ w_out
    y_ctx = None
    if need_ctx_out:
        s = jnp.einsum('blgrd,bsgd->bgrls', q_c, k_c).astype(jnp.float32) * scale
        p = sink_softmax(s).astype(v_c.dtype)
        o_c = jnp.einsum('bgrls,bsgd->blgrd', p[..., :n_ctx], v_c)
        y_ctx = o_c.reshape(bsz, n_ctx, ATT_DIM) @ w_out
    return y_lat, y_ctx

def depthwise_conv(x, w, bias):
    ch = x.shape[-1]
    y = lax.conv_general_dilated(x, w[:, None, :].astype(x.dtype), window_strides=(1,),
                                 padding=[(SSM_CONV_W // 2, SSM_CONV_W // 2)],
                                 dimension_numbers=('NWC', 'WIO', 'NWC'), feature_group_count=ch)
    return y + bias

def segsum(a):
    t = a.shape[-1]
    a_rep = jnp.broadcast_to(a[..., None], a.shape + (t,))
    a_rep = jnp.where(jnp.tril(jnp.ones((t, t), dtype=bool), -1), a_rep, 0.0)
    cs = jnp.cumsum(a_rep, axis=-2)
    return jnp.where(jnp.tril(jnp.ones((t, t), dtype=bool)), cs, -jnp.inf)

def ssd_scan(xs, dt, a_neg, bm, cm, init_state, with_outputs):
    b, length, g, r, p = xs.shape
    n = bm.shape[-1]
    nc = length // SSM_CHUNK
    q = SSM_CHUNK
    dt4 = dt.reshape(b, length, g, r)
    x_dt = (xs.astype(jnp.float32) * dt4[..., None]).reshape(b, nc, q, g, r, p)
    a = jnp.moveaxis((dt4 * a_neg.reshape(g, r)).reshape(b, nc, q, g, r), 2, -1)
    a_cs = jnp.cumsum(a, axis=-1)
    bc = bm.astype(jnp.float32).reshape(b, nc, q, g, n)
    cc = cm.astype(jnp.float32).reshape(b, nc, q, g, n)
    decay_states = jnp.exp(a_cs[..., -1:] - a_cs)
    states = jnp.einsum('bcsgn,bcgrs,bcsgrp->bcgrpn', bc, decay_states, x_dt)
    states = jnp.concatenate([init_state[:, None], states], axis=1)
    chunk_a = jnp.pad(a_cs[..., -1], ((0, 0), (1, 0), (0, 0), (0, 0)))
    decay_chunk = jnp.exp(segsum(jnp.moveaxis(chunk_a, 1, -1)))
    new_states = jnp.einsum('bgrzc,bcgrpn->bzgrpn', decay_chunk, states)
    final_state = new_states[:, -1]
    if not with_outputs:
        return None, final_state
    prev_states = new_states[:, :-1]
    lmat = jnp.exp(segsum(a))
    cb = jnp.einsum('bclgn,bcsgn->bcgls', cc, bc)
    y_diag = jnp.einsum('bcgrls,bcsgrp->bclgrp', cb[:, :, :, None] * lmat, x_dt)
    y_off = jnp.einsum('bclgn,bcgrpn,bcgrl->bclgrp', cc, prev_states, jnp.exp(a_cs))
    return (y_diag + y_off).reshape(b, length, g, r, p), final_state

def ssm_mixer(u_lat, u_ctx, w_in, conv_w, conv_b, dt_bias, a_log, d_skip, norm_g, w_out, need_ctx_out):
    a_neg = -jnp.exp(a_log.astype(jnp.float32))
    bsz = u_lat.shape[0]

    def flip(t):
        return jnp.flip(t, axis=1)

    def prep(u):
        length = u.shape[1]
        z, xbc, dt = jnp.split(u @ w_in, [SSM_D_INNER, SSM_D_INNER + SSM_CONV_DIM], axis=-1)
        xbc = jax.nn.silu(depthwise_conv(xbc, conv_w, conv_b))
        xs, bm, cm = jnp.split(xbc, [SSM_D_INNER, SSM_D_INNER + SSM_GROUPS * SSM_STATE], axis=-1)
        xs = xs.reshape(bsz, length, SSM_GROUPS, SSM_GROUP_HEADS, SSM_HEAD_DIM)
        bm = bm.reshape(bsz, length, SSM_GROUPS, SSM_STATE)
        cm = cm.reshape(bsz, length, SSM_GROUPS, SSM_STATE)
        dt = jax.nn.softplus(dt.astype(jnp.float32).reshape(bsz, length, 2, SSM_HEADS)
                             + dt_bias.astype(jnp.float32))
        return z, xs, bm, cm, dt

    def finish(z, xs, y_f, y_b):
        length = xs.shape[1]
        y = y_f + y_b + xs.astype(jnp.float32) * d_skip.astype(jnp.float32).reshape(SSM_GROUPS, SSM_GROUP_HEADS, 1)
        y = y.reshape(bsz, length, SSM_D_INNER) * jax.nn.silu(z.astype(jnp.float32))
        y = y.reshape(bsz, length, SSM_NORM_GROUPS, -1)
        y = y * lax.rsqrt(jnp.mean(jnp.square(y), axis=-1, keepdims=True) + RMS_EPS)
        y = (y.reshape(bsz, length, SSM_D_INNER) * norm_g.astype(jnp.float32)).astype(z.dtype)
        return y @ w_out

    z_c, x_c, b_c, c_c, dt_c = prep(u_ctx)
    z_l, x_l, b_l, c_l, dt_l = prep(u_lat)
    init = jnp.zeros((bsz, SSM_GROUPS, SSM_GROUP_HEADS, SSM_HEAD_DIM, SSM_STATE), jnp.float32)
    yc_f, st_f = ssd_scan(x_c, dt_c[:, :, 0], a_neg[0], b_c, c_c, init, need_ctx_out)
    yc_b, st_b = ssd_scan(flip(x_c), flip(dt_c[:, :, 1]), a_neg[1], flip(b_c), flip(c_c), init, need_ctx_out)
    yl_f, _ = ssd_scan(x_l, dt_l[:, :, 0], a_neg[0], b_l, c_l, st_f, True)
    yl_b, _ = ssd_scan(flip(x_l), flip(dt_l[:, :, 1]), a_neg[1], flip(b_l), flip(c_l), st_b, True)
    y_lat = finish(z_l, x_l, yl_f, flip(yl_b))
    y_ctx = finish(z_c, x_c, yc_f, flip(yc_b)) if need_ctx_out else None
    return y_lat, y_ctx

def first_inputs(seed: int = 0) -> dict:
    key = jax.random.key(seed)
    ks = jax.random.split(key, 24)
    f = jnp.float32
    d = D_MODEL

    def nrm(k, shape, scale):
        return jax.random.normal(k, shape, f) * scale

    dt0 = jnp.exp(jax.random.uniform(ks[15], (N_SSM_LAYERS, 2, SSM_HEADS), f, math.log(1e-3), math.log(1e-1)))
    return {
        'x': nrm(ks[0], (BATCH, SEQ, d), 1.0),
        'c': nrm(ks[1], (BATCH, d), 1.0),
        'ctx': nrm(ks[2], (BATCH, CTX_LEN, d), 1.0),
        'c_ctx': nrm(ks[3], (d,), 1.0),
        'w_mod': nrm(ks[4], (DEPTH, d, N_MOD * d), 0.5 * d ** -0.5),
        'b_mod': nrm(ks[5], (DEPTH, N_MOD * d), 0.02),
        'ln_mix_g': 1.0 + nrm(ks[6], (DEPTH, d), 0.02),
        'ln_mix_b': nrm(ks[7], (DEPTH, d), 0.02),
        'ln_ff_g': 1.0 + nrm(ks[8], (DEPTH, d), 0.02),
        'ln_ff_b': nrm(ks[9], (DEPTH, d), 0.02),
        'att_w_in': nrm(ks[10], (N_ATT_LAYERS, d, ATT_IN_DIM), d ** -0.5),
        'att_w_out': nrm(ks[11], (N_ATT_LAYERS, ATT_DIM, d), BETA * ATT_DIM ** -0.5),
        'att_sink': nrm(ks[12], (N_ATT_LAYERS, ATT_HEADS), 0.5),
        'ssm_w_in': nrm(ks[13], (N_SSM_LAYERS, d, SSM_IN_DIM), d ** -0.5),
        'ssm_conv_w': nrm(ks[14], (N_SSM_LAYERS, SSM_CONV_W, SSM_CONV_DIM), SSM_CONV_W ** -0.5),
        'ssm_conv_b': nrm(ks[16], (N_SSM_LAYERS, SSM_CONV_DIM), 0.02),
        'ssm_dt_bias': dt0 + jnp.log(-jnp.expm1(-dt0)),
        'ssm_a_log': jnp.log(jax.random.uniform(ks[17], (N_SSM_LAYERS, 2, SSM_HEADS), f, 1.0, 16.0)),
        'ssm_d': 1.0 + nrm(ks[18], (N_SSM_LAYERS, SSM_HEADS), 0.1),
        'ssm_norm_g': 1.0 + nrm(ks[19], (N_SSM_LAYERS, SSM_D_INNER), 0.02),
        'ssm_w_out': nrm(ks[20], (N_SSM_LAYERS, SSM_D_INNER, d), BETA * SSM_D_INNER ** -0.5),
        'ff_w1': nrm(ks[21], (DEPTH, d, FF_DIM), d ** -0.5),
        'ff_w2': nrm(ks[22], (DEPTH, FF_DIM, d), BETA * FF_DIM ** -0.5),
    }

def first_block(x, c, ctx, c_ctx, w_mod, b_mod, ln_mix_g, ln_mix_b, ln_ff_g, ln_ff_b,
              att_w_in, att_w_out, att_sink, ssm_w_in, ssm_conv_w, ssm_conv_b, ssm_dt_bias,
              ssm_a_log, ssm_d, ssm_norm_g, ssm_w_out, ff_w1, ff_w2):
    rows = x.shape[1] // GRID_W
    rope = axial_rope_tables(rows)
    h_lat, h_ctx = x, ctx
    for i in range(DEPTH):
        last = i == DEPTH - 1
        j = i // N_MIXERS
        m_lat = (jax.nn.silu(c) @ w_mod[i] + b_mod[i])[:, None, :]
        m_ctx = (jax.nn.silu(c_ctx) @ w_mod[i] + b_mod[i])[None, None, :]
        sh_m_l, sc_m_l, g_m_l, sh_f_l, sc_f_l, g_f_l = jnp.split(m_lat, N_MOD, axis=-1)
        sh_m_c, sc_m_c, g_m_c, sh_f_c, sc_f_c, g_f_c = jnp.split(m_ctx, N_MOD, axis=-1)
        u_lat = modulate(h_lat, sh_m_l, sc_m_l)
        u_ctx = modulate(h_ctx, sh_m_c, sc_m_c)
        if i % N_MIXERS == 0:
            y_lat, y_ctx = attention_mixer(u_lat, u_ctx, att_w_in[j], att_w_out[j], att_sink[j], rope, not last)
        else:
            y_lat, y_ctx = ssm_mixer(u_lat, u_ctx, ssm_w_in[j], ssm_conv_w[j], ssm_conv_b[j], ssm_dt_bias[j],
                                     ssm_a_log[j], ssm_d[j], ssm_norm_g[j], ssm_w_out[j], not last)
        h_lat = layer_norm(ALPHA * h_lat + g_m_l * y_lat, ln_mix_g[i], ln_mix_b[i])
        f_lat = squared_relu_mlp(modulate(h_lat, sh_f_l, sc_f_l), ff_w1[i], ff_w2[i])
        h_lat = layer_norm(ALPHA * h_lat + g_f_l * f_lat, ln_ff_g[i], ln_ff_b[i])
        if not last:
            h_ctx = layer_norm(ALPHA * h_ctx + g_m_c * y_ctx, ln_mix_g[i], ln_mix_b[i])
            f_ctx = squared_relu_mlp(modulate(h_ctx, sh_f_c, sc_f_c), ff_w1[i], ff_w2[i])
            h_ctx = layer_norm(ALPHA * h_ctx + g_f_c * f_ctx, ln_ff_g[i], ln_ff_b[i])
    return h_lat


DEPTH_2 = 1


MIXER_DELTA = 0
MIXER_HYENA = 1
N_DELTA_LAYERS = (DEPTH_2 - MIXER_DELTA + N_MIXERS - 1) // N_MIXERS
N_HYENA_LAYERS = (DEPTH_2 - MIXER_HYENA + N_MIXERS - 1) // N_MIXERS

EPS = 1e-6

DN_HEAD_DIM = 128
DN_HEADS = D_MODEL // DN_HEAD_DIM
DN_INNER = DN_HEADS * DN_HEAD_DIM
DN_CONV = 5
DN_CHUNK = 64
DN_CHUNK_LOG2 = 6
DN_PROJ = 4 * DN_INNER + 4 * DN_HEADS

HY_WIDTH = D_MODEL
HY_SHORT = 3
HY_BANDS = 16
HY_EMB = 1 + 2 * HY_BANDS
HY_FF = 64
HY_FAST = 0.3
HY_SLOW = 1.5
HY_TARGET = 1e-2

PEER_HEADS = 8
PEER_NKEYS = 128
PEER_EXPERTS = PEER_NKEYS * PEER_NKEYS
PEER_DK = 256
PEER_TOPK = 16
PEER_BLOCK = 128


def _rmsnorm(x, g):
    xf = x.astype(jnp.float32)
    y = xf * lax.rsqrt(jnp.mean(xf * xf, axis=-1, keepdims=True) + EPS)
    return (y * g.astype(jnp.float32)).astype(x.dtype)

def _modulate(xn, shift, scale):
    return xn * (1 + scale) + shift

def _l2norm(x):
    xf = x.astype(jnp.float32)
    return xf * lax.rsqrt(jnp.sum(xf * xf, axis=-1, keepdims=True) + EPS)

def _rev(t):
    return jnp.flip(t, axis=2)

def _short_conv(x, w, n_rows):
    B, L, C = x.shape
    K = w.shape[0]
    xr = x.reshape(B * n_rows, L // n_rows, C)
    y = lax.conv_general_dilated(
        xr, w.astype(x.dtype)[:, None, :], window_strides=(1,),
        padding=[((K - 1) // 2, (K - 1) // 2)],
        dimension_numbers=('NWC', 'WIO', 'NWC'), feature_group_count=C)
    return y.reshape(B, L, C)

def _dn_inputs(hn, n_rows, w_in, conv_w, a_log, dt_bias):
    B, L, _ = hn.shape
    z = hn @ w_in
    qkv = jax.nn.silu(_short_conv(z[..., :3 * DN_INNER], conv_w, n_rows))
    gate = z[..., 3 * DN_INNER:4 * DN_INNER]
    ba = z[..., 4 * DN_INNER:].astype(jnp.float32).reshape(B, L, 2, 2, DN_HEADS)
    qkv = qkv.reshape(B, L, 3, DN_HEADS, DN_HEAD_DIM).transpose(2, 0, 3, 1, 4)
    q = _l2norm(qkv[0]) * (DN_HEAD_DIM ** -0.5)
    k = _l2norm(qkv[1])
    v = qkv[2].astype(jnp.float32)
    beta = jax.nn.sigmoid(ba[:, :, 0]).transpose(0, 2, 3, 1)
    g = (-jnp.exp(a_log.astype(jnp.float32)) *
         jax.nn.softplus(ba[:, :, 1] + dt_bias.astype(jnp.float32))).transpose(0, 2, 3, 1)
    return q, k, v, beta, g, gate

def _unit_lower_inverse(a):
    eye = jnp.eye(a.shape[-1], dtype=a.dtype)
    t = eye - a
    p = a
    for _ in range(DN_CHUNK_LOG2 - 1):
        p = p @ p
        t = t @ (eye + p)
    return t

def _gated_delta_chunked(k, v, beta, g, s0, q=None):
    f32 = jnp.float32
    with_out = q is not None
    B, H, L, DK = k.shape
    DV = v.shape[-1]
    C = DN_CHUNK
    n = L // C
    k = k.astype(f32).reshape(B, H, n, C, DK)
    v = v.astype(f32).reshape(B, H, n, C, DV)
    beta = beta.astype(f32).reshape(B, H, n, C)
    G = jnp.cumsum(g.astype(f32).reshape(B, H, n, C), axis=-1)
    incl = jnp.tril(jnp.ones((C, C), bool))
    strict = jnp.tril(jnp.ones((C, C), bool), -1)
    dmat = jnp.exp(jnp.where(incl, G[..., :, None] - G[..., None, :], -jnp.inf))
    kb = k * beta[..., None]
    a = jnp.where(strict, jnp.einsum('bhnid,bhnjd->bhnij', kb, k) * dmat, 0.0)
    t = _unit_lower_inverse(a)
    u = t @ (v * beta[..., None])
    w = t @ (kb * jnp.exp(G)[..., None])
    kd = k * jnp.exp(G[..., -1:] - G)[..., None]
    gl = jnp.exp(G[..., -1])
    xs = (jnp.moveaxis(w, 2, 0), jnp.moveaxis(u, 2, 0), jnp.moveaxis(kd, 2, 0), jnp.moveaxis(gl, 2, 0))
    if with_out:
        q = q.astype(f32).reshape(B, H, n, C, DK)
        qa = jnp.einsum('bhnid,bhnjd->bhnij', q, k) * dmat
        qg = q * jnp.exp(G)[..., None]
        xs = xs + (jnp.moveaxis(qg, 2, 0), jnp.moveaxis(qa, 2, 0))

    def step(s, inp):
        w_c, u_c, kd_c, gl_c = inp[:4]
        v_new = u_c - jnp.einsum('bhck,bhkv->bhcv', w_c, s)
        s_next = s * gl_c[..., None, None] + jnp.einsum('bhck,bhcv->bhkv', kd_c, v_new)
        if not with_out:
            return s_next, None
        qg_c, qa_c = inp[4:]
        o_c = jnp.einsum('bhck,bhkv->bhcv', qg_c, s) + jnp.einsum('bhij,bhjv->bhiv', qa_c, v_new)
        return s_next, o_c

    s_fin, o = lax.scan(step, s0.astype(f32), xs)
    if not with_out:
        return None, s_fin
    return jnp.moveaxis(o, 0, 2).reshape(B, H, L, DV), s_fin

def _gated_out(o, gate, g_norm, w_out):
    B, H, L, DV = o.shape
    o = jnp.swapaxes(o, 1, 2)
    on = o * lax.rsqrt(jnp.mean(o * o, axis=-1, keepdims=True) + EPS) * g_norm.astype(jnp.float32)
    y = on * jax.nn.silu(gate.astype(jnp.float32)).reshape(B, L, H, DV)
    return y.reshape(B, L, H * DV).astype(gate.dtype) @ w_out

def _deltanet(hn, hcn, n_rows, w_in, conv_w, a_log, dt_bias, o_norm_g, w_out, ctx_out):
    q, k, v, beta, g, gate = _dn_inputs(hn, n_rows, w_in, conv_w, a_log, dt_bias)
    qc, kc, vc, betac, gc, gatec = _dn_inputs(hcn, 1, w_in, conv_w, a_log, dt_bias)
    B = hn.shape[0]
    s0 = jnp.zeros((B, DN_HEADS, DN_HEAD_DIM, DN_HEAD_DIM), jnp.float32)
    oc_f, sc_f = _gated_delta_chunked(kc, vc, betac[:, 0], gc[:, 0], s0, qc if ctx_out else None)
    oc_b, sc_b = _gated_delta_chunked(_rev(kc), _rev(vc), _rev(betac[:, 1]), _rev(gc[:, 1]), s0,
                                      _rev(qc) if ctx_out else None)
    o_f, _ = _gated_delta_chunked(k, v, beta[:, 0], g[:, 0], sc_f, q)
    o_b, _ = _gated_delta_chunked(_rev(k), _rev(v), _rev(beta[:, 1]), _rev(g[:, 1]), sc_b, _rev(q))
    y = _gated_out(o_f + _rev(o_b), gate, o_norm_g, w_out)
    yc = _gated_out(oc_f + _rev(oc_b), gatec, o_norm_g, w_out) if ctx_out else None
    return y, yc

def _hyena_filters(L, w1, b1, w2, b2, w3, b3, w4, freq):
    f32 = jnp.float32
    D = w4.shape[-1] // 4
    pos = jnp.arange(L, dtype=f32)
    t = pos / max(L - 1, 1)
    ang = (2 * math.pi * pos / L)[:, None] * jnp.linspace(1e-4, HY_BANDS - 1, HY_BANDS, dtype=f32)[None]
    z = jnp.concatenate([t[:, None], jnp.cos(ang), -jnp.sin(ang)], axis=-1)
    fr = freq.astype(f32)
    hid = jnp.sin(fr * (z @ w1.astype(f32) + b1.astype(f32)))
    hid = jnp.sin(fr * (hid @ w2.astype(f32) + b2.astype(f32)))
    hid = jnp.sin(fr * (hid @ w3.astype(f32) + b3.astype(f32)))
    h = hid @ w4.astype(f32)
    deltas = jnp.abs(jnp.linspace(math.log(HY_TARGET) / HY_FAST, math.log(HY_TARGET) / HY_SLOW, D, dtype=f32))
    decay = jnp.exp(-t[:, None] * deltas[None])
    return (h.reshape(L, 2, 2, D) * decay[:, None, None, :]).transpose(1, 2, 0, 3)

def _long_conv(u, hf, hb, d):
    B, L, D = u.shape
    filt2 = jnp.concatenate([hf, jnp.zeros((1, D), jnp.float32), jnp.flip(hb[1:], axis=0)], axis=0)
    uf = jnp.fft.rfft(u.astype(jnp.float32), n=2 * L, axis=1)
    y = jnp.fft.irfft(uf * jnp.fft.rfft(filt2, axis=0)[None], n=2 * L, axis=1)[:, :L]
    return (y + u.astype(jnp.float32) * d.astype(jnp.float32)).astype(u.dtype)

def _hyena(hn, n_rows, w_in, conv_w, conv_b, f_w1, f_b1, f_w2, f_b2, f_w3, f_b3, f_w4, freq, skip, w_out):
    B, L, _ = hn.shape
    z = _short_conv(hn @ w_in, conv_w, n_rows) + conv_b.astype(hn.dtype)
    v, x1, x2 = jnp.split(z, 3, axis=-1)
    filt = _hyena_filters(L, f_w1, f_b1, f_w2, f_b2, f_w3, f_b3, f_w4, freq)
    z1 = x1 * _long_conv(v, filt[0, 0], filt[0, 1], skip[0])
    z2 = x2 * _long_conv(z1, filt[1, 0], filt[1, 1], skip[1])
    return z2 @ w_out

def _peer(x, w_q, sub_keys, u_tab, v_tab):
    B, L, D = x.shape
    T = B * L
    xt = x.reshape(T, D)
    q = (xt @ w_q).astype(jnp.float32).reshape(T, PEER_HEADS, 2, PEER_DK // 2)
    s = jnp.einsum('thpd,hpkd->thpk', q, sub_keys.astype(jnp.float32))
    s1, i1 = lax.top_k(s[:, :, 0], PEER_TOPK)
    s2, i2 = lax.top_k(s[:, :, 1], PEER_TOPK)
    n_cand = PEER_TOPK * PEER_TOPK
    cand_s = (s1[..., :, None] + s2[..., None, :]).reshape(T, PEER_HEADS, n_cand)
    cand_i = (i1[..., :, None] * PEER_NKEYS + i2[..., None, :]).reshape(T, PEER_HEADS, n_cand)
    top_s, pos = lax.top_k(cand_s, PEER_TOPK)
    idx = jnp.take_along_axis(cand_i, pos, axis=-1)
    gate = jax.nn.softmax(top_s, axis=-1)
    nb = T // PEER_BLOCK

    def expert_block(args):
        xb, ib, gb = args
        hid = jnp.einsum('td,thkd->thk', xb, u_tab[ib]).astype(jnp.float32)
        coef = (jax.nn.gelu(hid, approximate=False) * gb).astype(xb.dtype)
        return jnp.einsum('thk,thkd->td', coef, v_tab[ib])

    y = lax.map(expert_block, (xt.reshape(nb, PEER_BLOCK, D),
                               idx.reshape(nb, PEER_BLOCK, PEER_HEADS, PEER_TOPK),
                               gate.reshape(nb, PEER_BLOCK, PEER_HEADS, PEER_TOPK)))
    return y.reshape(B, L, D)

def second_inputs(seed: int = 0) -> dict:
    key = jax.random.key(seed)
    ks = iter(jax.random.split(key, 32))
    f32 = jnp.float32
    D = D_MODEL

    def nrm(shape, scale):
        return jax.random.normal(next(ks), shape, f32) * scale

    x = nrm((BATCH, SEQ, D), 1.0)
    c = nrm((BATCH, D), 1.0)
    ctx = nrm((BATCH, CTX_LEN, D), 1.0)
    c_ctx = nrm((D,), 1.0)
    ada_w = nrm((DEPTH_2, D, 6 * D), 0.5 * D ** -0.5)
    ada_b = nrm((DEPTH_2, 6 * D), 0.02)
    norm_g = 1.0 + nrm((DEPTH_2, 2, D), 0.02)
    dn_w_in = nrm((N_DELTA_LAYERS, D, DN_PROJ), D ** -0.5)
    dn_conv_w = nrm((N_DELTA_LAYERS, DN_CONV, 3 * DN_INNER), DN_CONV ** -0.5)
    dn_a_log = jnp.log(jax.random.uniform(next(ks), (N_DELTA_LAYERS, 2, DN_HEADS), f32, 1.0, 16.0))
    dt = jnp.exp(jax.random.uniform(next(ks), (N_DELTA_LAYERS, 2, DN_HEADS), f32,
                                    math.log(1e-3), math.log(1e-1)))
    dn_dt_bias = dt + jnp.log(-jnp.expm1(-dt))
    dn_norm_g = 1.0 + nrm((N_DELTA_LAYERS, DN_HEAD_DIM), 0.02)
    dn_w_out = nrm((N_DELTA_LAYERS, DN_INNER, D), DN_INNER ** -0.5)
    hy_w_in = nrm((N_HYENA_LAYERS, D, 3 * HY_WIDTH), D ** -0.5)
    hy_conv_w = nrm((N_HYENA_LAYERS, HY_SHORT, 3 * HY_WIDTH), HY_SHORT ** -0.5)
    hy_conv_b = nrm((N_HYENA_LAYERS, 3 * HY_WIDTH), 0.02)
    hy_f_w1 = nrm((N_HYENA_LAYERS, HY_EMB, HY_FF), HY_EMB ** -0.5)
    hy_f_b1 = nrm((N_HYENA_LAYERS, HY_FF), 0.02)
    hy_f_w2 = nrm((N_HYENA_LAYERS, HY_FF, HY_FF), HY_FF ** -0.5)
    hy_f_b2 = nrm((N_HYENA_LAYERS, HY_FF), 0.02)
    hy_f_w3 = nrm((N_HYENA_LAYERS, HY_FF, HY_FF), HY_FF ** -0.5)
    hy_f_b3 = nrm((N_HYENA_LAYERS, HY_FF), 0.02)
    hy_f_w4 = nrm((N_HYENA_LAYERS, HY_FF, 4 * HY_WIDTH), 0.02 * HY_FF ** -0.5)
    hy_freq = 1.0 + nrm((N_HYENA_LAYERS, HY_FF), 0.02)
    hy_skip = nrm((N_HYENA_LAYERS, 2, HY_WIDTH), 1.0)
    hy_w_out = nrm((N_HYENA_LAYERS, HY_WIDTH, D), HY_WIDTH ** -0.5)
    peer_w_q = nrm((DEPTH_2, D, PEER_HEADS * PEER_DK), D ** -0.5)
    peer_keys = nrm((DEPTH_2, PEER_HEADS, 2, PEER_NKEYS, PEER_DK // 2), (PEER_DK // 2) ** -0.5)
    peer_u = nrm((DEPTH_2, PEER_EXPERTS, D), D ** -0.5)
    peer_v = nrm((DEPTH_2, PEER_EXPERTS, D), PEER_HEADS ** -0.5)
    final_g = 1.0 + nrm((D,), 0.02)
    return {"x": x, "c": c, "ctx": ctx, "c_ctx": c_ctx,
            "ada_w": ada_w, "ada_b": ada_b, "norm_g": norm_g,
            "dn_w_in": dn_w_in, "dn_conv_w": dn_conv_w, "dn_a_log": dn_a_log, "dn_dt_bias": dn_dt_bias,
            "dn_norm_g": dn_norm_g, "dn_w_out": dn_w_out,
            "hy_w_in": hy_w_in, "hy_conv_w": hy_conv_w, "hy_conv_b": hy_conv_b,
            "hy_f_w1": hy_f_w1, "hy_f_b1": hy_f_b1, "hy_f_w2": hy_f_w2, "hy_f_b2": hy_f_b2,
            "hy_f_w3": hy_f_w3, "hy_f_b3": hy_f_b3, "hy_f_w4": hy_f_w4, "hy_freq": hy_freq,
            "hy_skip": hy_skip, "hy_w_out": hy_w_out,
            "peer_w_q": peer_w_q, "peer_keys": peer_keys, "peer_u": peer_u, "peer_v": peer_v,
            "final_g": final_g}

def second_block(x, c, ctx, c_ctx, ada_w, ada_b, norm_g,
              dn_w_in, dn_conv_w, dn_a_log, dn_dt_bias, dn_norm_g, dn_w_out,
              hy_w_in, hy_conv_w, hy_conv_b, hy_f_w1, hy_f_b1, hy_f_w2, hy_f_b2,
              hy_f_w3, hy_f_b3, hy_f_w4, hy_freq, hy_skip, hy_w_out,
              peer_w_q, peer_keys, peer_u, peer_v, final_g):
    f32 = jnp.float32
    B, L, D = x.shape
    rows = L // GRID_W
    silu_c = jax.nn.silu(c.astype(f32))
    silu_cc = jax.nn.silu(c_ctx.astype(f32))
    h, hc = x, ctx
    for i in range(DEPTH_2):
        kind = i % N_MIXERS
        j = i // N_MIXERS
        ctx_out = any(l % N_MIXERS == MIXER_DELTA for l in range(i + 1, DEPTH_2))
        ctx_in = kind == MIXER_DELTA or ctx_out
        w_ada = ada_w[i].astype(f32)
        b_ada = ada_b[i].astype(f32)
        mod = (silu_c @ w_ada + b_ada).astype(h.dtype).reshape(B, 6, 1, D)
        sh1, sc1, gt1, sh2, sc2, gt2 = [mod[:, m] for m in range(6)]
        hn = _modulate(_rmsnorm(h, norm_g[i, 0]), sh1, sc1)
        hcn = None
        if ctx_in:
            modc = (silu_cc @ w_ada + b_ada).astype(hc.dtype).reshape(6, D)
            hcn = _modulate(_rmsnorm(hc, norm_g[i, 0]), modc[0], modc[1])
        if kind == MIXER_DELTA:
            y, yc = _deltanet(hn, hcn, rows, dn_w_in[j], dn_conv_w[j], dn_a_log[j], dn_dt_bias[j],
                              dn_norm_g[j], dn_w_out[j], ctx_out)
        else:
            hy_args = (hy_w_in[j], hy_conv_w[j], hy_conv_b[j], hy_f_w1[j], hy_f_b1[j], hy_f_w2[j],
                       hy_f_b2[j], hy_f_w3[j], hy_f_b3[j], hy_f_w4[j], hy_freq[j], hy_skip[j], hy_w_out[j])
            y = _hyena(hn, rows, *hy_args)
            yc = _hyena(hcn, 1, *hy_args) if ctx_out else None
        h = h + gt1 * y
        peer_args = (peer_w_q[i], peer_keys[i], peer_u[i], peer_v[i])
        h = h + gt2 * _peer(_modulate(_rmsnorm(h, norm_g[i, 1]), sh2, sc2), *peer_args)
        if ctx_out:
            hc = hc + modc[2] * yc
            hc = hc + modc[5] * _peer(_modulate(_rmsnorm(hc, norm_g[i, 1]), modc[3], modc[4]), *peer_args)
    return _rmsnorm(h, final_g)


def setup_inputs(seed=0):
    out = dict(first_inputs(seed))
    for name, value in second_inputs(seed + 1).items():
        if name != "x":
            out[name + "_2"] = value
    return out


def reference(
    x, c, ctx, c_ctx, w_mod, b_mod, ln_mix_g, ln_mix_b, ln_ff_g, ln_ff_b, att_w_in, att_w_out,
    att_sink, ssm_w_in, ssm_conv_w, ssm_conv_b, ssm_dt_bias, ssm_a_log, ssm_d, ssm_norm_g,
    ssm_w_out, ff_w1, ff_w2, c_2, ctx_2, c_ctx_2, ada_w_2, ada_b_2, norm_g_2, dn_w_in_2,
    dn_conv_w_2, dn_a_log_2, dn_dt_bias_2, dn_norm_g_2, dn_w_out_2, hy_w_in_2, hy_conv_w_2,
    hy_conv_b_2, hy_f_w1_2, hy_f_b1_2, hy_f_w2_2, hy_f_b2_2, hy_f_w3_2, hy_f_b3_2, hy_f_w4_2,
    hy_freq_2, hy_skip_2, hy_w_out_2, peer_w_q_2, peer_keys_2, peer_u_2, peer_v_2, final_g_2,
):
    x = first_block(
        x, c, ctx, c_ctx, w_mod, b_mod, ln_mix_g, ln_mix_b, ln_ff_g, ln_ff_b, att_w_in,
        att_w_out, att_sink, ssm_w_in, ssm_conv_w, ssm_conv_b, ssm_dt_bias, ssm_a_log, ssm_d,
        ssm_norm_g, ssm_w_out, ff_w1, ff_w2,
    )
    return second_block(
        x, c_2, ctx_2, c_ctx_2, ada_w_2, ada_b_2, norm_g_2, dn_w_in_2, dn_conv_w_2, dn_a_log_2,
        dn_dt_bias_2, dn_norm_g_2, dn_w_out_2, hy_w_in_2, hy_conv_w_2, hy_conv_b_2, hy_f_w1_2,
        hy_f_b1_2, hy_f_w2_2, hy_f_b2_2, hy_f_w3_2, hy_f_b3_2, hy_f_w4_2, hy_freq_2, hy_skip_2,
        hy_w_out_2, peer_w_q_2, peer_keys_2, peer_u_2, peer_v_2, final_g_2,
    )


_drawn_inputs = setup_inputs


def setup_inputs(seed=0):
    import zlib

    import numpy as np

    out = dict(_drawn_inputs(seed))
    spreads = {}
    factors = {'ctx': 5.261,
     'b_mod': 2.783,
     'att_sink': 64.0,
     'ssm_conv_b': 8.0,
     'ssm_d': 7.678,
     'ssm_norm_g': 21.376,
     'ctx_2': 3.738,
     'c_ctx_2': 5.958,
     'ada_b_2': 2.944,
     'norm_g_2': 5.441,
     'dn_norm_g_2': 8.0,
     'final_g_2': 22.116}
    for name, (base, spread) in spreads.items():
        noise = np.random.default_rng([zlib.crc32(name.encode()), seed]).standard_normal(out[name].shape)
        drawn = base * np.exp(spread * noise) if base else spread * noise
        out[name] = jnp.asarray(drawn.astype(out[name].dtype))
    for name, factor in factors.items():
        out[name] = (out[name] * factor).astype(out[name].dtype)
    return out
```

```python
from contextlib import ExitStack

import concourse.bass as bass
from concourse import mybir

F32 = mybir.dt.float32
BF16 = mybir.dt.bfloat16
U32 = mybir.dt.uint32
ALU = mybir.AluOpType
ACT = mybir.ActivationFunctionType
AX = mybir.AxisListType

P = 128
D = 1024
KC = D // P
LAT, CTX = 512, 256
TOK = LAT + CTX
TB = TOK // P
LB = LAT // P
RING = 4
BANK = 512
ALPHA = 4.0 ** 0.25
LN_EPS = 1e-5
EPS_RMS = 1e-5
EPS = 1e-6
NEG = -1e30
HEADS = 16
HD = 64
SINNER = 2048
SHEADS = 32
SCONV = 3072
NMOD = 48

STREAM = [("mod0", NMOD, 1), ("mod1", NMOD, 1), ("ada", NMOD, 1),
          ("att_in", 12, 1), ("att_out", 8, 1), ("ff1_0", 32, 1), ("ff2_0", 8, 4),
          ("ssm_x", 16, 1), ("ssm_bc", 8, 1), ("ssm_z", 16, 1), ("ssm_out", 8, 2), ("ff1_1", 32, 1), ("ff2_1", 8, 4),
          ("dn_v", 8, 1), ("dn_k", 8, 1), ("dn_gate", 8, 1), ("dn_q", 8, 1), ("dn_out", 8, 1), ("w_q", 16, 1)]
EXPERT_TILES = 128
GROUP = RING
BLOCK = 64
DH = 8
PICKS = 16


def stream_starts():
    starts, at = {}, 0
    for name, chunks, per in STREAM:
        starts[name] = at
        at += chunks * per
    starts["experts"] = at
    return starts, at + 2 * EXPERT_TILES


VECTORS = [("c", 8), ("c_ctx", 8), ("c2", 8), ("c2_ctx", 8),
           ("b_mod0", 48), ("b_mod1", 48), ("b_ada", 48),
           ("mix_g0", 8), ("mix_g1", 8), ("mix_b0", 8), ("mix_b1", 8),
           ("ff_g0", 8), ("ff_g1", 8), ("ff_b0", 8), ("ff_b1", 8),
           ("norm_g0", 8), ("norm_g1", 8), ("final_g", 8),
           ("conv_w", 5 * 24), ("conv_b", 24), ("ssm_norm_g", 16), 
           ("dn_conv_w", 5 * 24), ("dn_norm_g", 1)]


def vector_columns():
    at, where = 0, {}
    for name, n in VECTORS:
        where[name] = (at, n)
        at += n
    return where, at


SQUARES = ["identity", "ones", "mean", "rope_swap", "mask_before", "mask_same",
           "mask_after", "sum_upto", "sum_from", "strict_lower", "strict_upper",
           "group_mean", "head_mean", "iota"]


class Count:

    def __init__(self, sem):
        self.sem, self.n, self.at, self.per = sem, 0, None, 0

    def mark(self, instruction, by=1):
        instruction.then_inc(self.sem, by)
        self.n += by
        return instruction

    def value(self, more=0):
        return self.n + more if self.at is None else self.at * self.per + (self.n + more)

    def enter(self, at, per):
        self.at, self.per, self.start = at, per, self.n

    def leave(self, iterations):
        assert self.n - self.start == self.per, (self.n - self.start, self.per)
        self.n = self.start + iterations * self.per
        self.at = None


def settle(engine, count):
    engine.wait_ge(count.sem, count.value())


def build(nc, ext, out):
    starts, n_tiles = stream_starts()
    columns, n_columns = vector_columns()
    gate_store = nc.dram_tensor("gate_store", (P, KC, LAT), F32, kind="Internal").ap()
    expert_gates = nc.dram_tensor("expert_gates", (LAT // BLOCK, P, P, BLOCK), F32, kind="Internal").ap()
    with ExitStack() as ctx:
        def sb(name, shape, dt=F32, stack=ctx):
            return stack.enter_context(nc.sbuf_tensor(name, shape, dt))

        def sem(name):
            return ctx.enter_context(nc.semaphore(name))

        ps = ctx.enter_context(nc.psum_tensor("ps", [P, 8, BANK], F32))

        def banks(first, width):
            return ps[:, first:first + (width + BANK - 1) // BANK, :].rearrange("p b n -> p (b n)")[:, 0:width]

        h = sb("h", [P, KC, TOK])
        x_all = sb("x_all", [P, 2, KC, TOK], BF16)
        x_hi, x_lo = x_all[:, 0], x_all[:, 1]
        w_raw = sb("w_raw", [P, RING, D])
        w_hi = sb("w_hi", [P, RING, D], BF16)
        w_lo = sb("w_lo", [P, RING, D], BF16)
        vec = sb("vec", [P, n_columns])
        sq = sb("sq", [P, len(SQUARES), P])
        mods = sb("mods", [P, 3, NMOD, 2])
        modp = sb("modp", [P, 3, NMOD, 2])
        cvec = sb("cvec", [P, 2, 2, KC, 2])
        cv = sb("cv", [P, 2, KC, 2])
        cvh = sb("cvh", [P, 2, 2, KC, 2], BF16)

        def V(name, i=0, n=1):
            return vec[:, columns[name][0] + i:columns[name][0] + i + n]

        def SQ(name):
            return sq[:, SQUARES.index(name), :]

        raw_ready = [sem(f"raw_ready{i}") for i in range(RING)]
        hi_done = sem("hi_done")
        split_done = sem("split_done")
        slot_free = sem("slot_free")
        psum_free = sem("psum_free")
        consts_ready = sem("consts_ready")
        start_done = sem("start_done")
        pe_done, act_done, dve_done, pool_done, dma_done = (
            Count(sem(n)) for n in ("pe_done", "act_done", "dve_done", "pool_done", "dma_done"))
        engines_counts = (pe_done, act_done, dve_done, pool_done, dma_done)
        chunks_before = [0]

        with nc.Block() as block:
            @block.sync
            def _(sp):
                sp.dma_start(vec[:], ext["vectors"]).then_inc(consts_ready, 16)
                sp.dma_start(sq[:], ext["squares"]).then_inc(consts_ready, 16)
                for t in range(RING):
                    sp.dma_start(w_raw[:, t], ext["weights"][t]).then_inc(raw_ready[t], 16)
                sp.dma_start(h[:], ext["tokens"]).then_inc(consts_ready, 16)

            @block.vector
            def _(dve):
                nc.vector.memset(cvec[:, 0, 0, 0, :], 0.0).then_inc(psum_free, 2)
                nc.vector.memset(cvec[:, 0, 1, 0, :], 0.0).then_inc(slot_free, RING)

            @block.scalar
            def _(act):
                act.wait_ge(consts_ready, 32 + 16)
                for b, names in enumerate((("c", "c_ctx"), ("c2", "c2_ctx"))):
                    for s, name in enumerate(names):
                        act_done.mark(nc.scalar.activation(cv[:, b, :, s], V(name, 0, KC), ACT.Silu))
                settle(act, act_done)
                act_done.mark(nc.scalar.activation(cvh[:, :, 0], cv[:], ACT.Copy))

        with nc.Block() as block:
            @block.vector
            def _(dve):
                dve_done.mark(nc.vector.tensor_tensor(cvh[:, :, 1], cv[:], cvh[:, :, 0], ALU.subtract))

        def stream_tiles(sp, t0, tiles):
            first = t0 + RING
            count = min(first + tiles, n_tiles) - first
            with sp.Fori(0, count // RING) as i:
                for j in range(RING):
                    sp.wait_ge(split_done, i * RING + (t0 + j + 1))
                    sp.dma_start(w_raw[:, j], ext["weights"][i * RING + (first + j)]).then_inc(raw_ready[j], 16)

        def split_high(act, t0, tiles):
            with act.Fori(0, tiles // RING) as i:
                for j in range(RING):
                    act.wait_ge(raw_ready[j], i * 16 + 16 * (t0 // RING + 1))
                    act.wait_ge(slot_free, i * RING + (t0 + j + 1))
                    nc.scalar.activation(w_hi[:, j], w_raw[:, j], ACT.Copy).then_inc(hi_done, 1)

        def split_low(pool, t0, tiles):
            with pool.Fori(0, tiles // RING) as i:
                for j in range(RING):
                    pool.wait_ge(hi_done, i * RING + (t0 + j + 1))
                    nc.gpsimd.tensor_tensor(w_lo[:, j], w_raw[:, j], w_hi[:, j],
                                            ALU.subtract).then_inc(split_done, 1)

        def linear(name, xh, xl, segments, evacuate, per_chunk):
            t0 = starts[name]
            chunks, per = next((c, k) for n, c, k in STREAM if n == name)
            tiles = chunks * per
            body = max(RING, 2 * per)
            in_body = body // per
            c0 = chunks_before[0]
            chunks_before[0] += chunks
            with nc.Block() as block:
                @block.sync
                def _(sp):
                    stream_tiles(sp, t0, tiles)

                @block.scalar
                def _(act):
                    split_high(act, t0, tiles)

                @block.gpsimd
                def _(pool):
                    split_low(pool, t0, tiles)

                @block.tensor
                def _(pe):
                    with pe.Fori(0, tiles // body) as i:
                        for c in range(in_body):
                            pe.wait_ge(psum_free, i * in_body + (c0 + c + 1))
                            for q in range(per):
                                slot = (c * per + q) % RING
                                pe.wait_ge(split_done, i * body + (t0 + c * per + q + 1))
                                for k in range(KC):
                                    kk = q * KC + k
                                    for part, (w, x) in enumerate(((w_hi, xh), (w_hi, xl), (w_lo, xh))):
                                        for bank, width, lo in segments:
                                            mm = nc.tensor.matmul(
                                                ps[:, 2 * (c % 2) + bank, 0:width],
                                                w[:, slot, k * P:(k + 1) * P], x(kk, lo, width),
                                                start=(kk == 0 and part == 0),
                                                stop=(kk == per * KC - 1 and part == 2))
                                mm.then_inc(slot_free, 1)

                @block.vector
                def _(dve):
                    with dve.Fori(0, tiles // body) as i:
                        dve_done.enter(i, in_body * per_chunk)
                        for c in range(in_body):
                            dve.wait_ge(slot_free, i * body + (RING + t0 + (c + 1) * per))
                            evacuate(dve, i * in_body + c, c % 2, i * in_body + (c0 + c + 3))
                        dve_done.leave(tiles // body)

        def x_parts(hi, lo):
            return (lambda k, at, width: hi[:, k, at:at + width]), (lambda k, at, width: lo[:, k, at:at + width])

        BOTH = [(0, LAT, 0), (1, CTX, LAT)]
        LATENT = [(0, LAT, 0)]

        for layer, (name, bias, b) in enumerate((("mod0", "b_mod0", 0), ("mod1", "b_mod1", 0), ("ada", "b_ada", 1))):
            def evacuate_mod(dve, c, s, freed, layer=layer, bias=bias):
                at = columns[bias][0]
                nc.vector.tensor_scalar(mods[:, layer, bass.ds(c, 1), :], ps[:, 2 * s:2 * s + 1, 0:2],
                                        vec[:, bass.ds(c + at, 1)], None, ALU.add).then_inc(psum_free, 1)

            linear(name, lambda k, lo, w, b=b: cvh[:, b, 0, k, :], lambda k, lo, w, b=b: cvh[:, b, 1, k, :],
                   [(0, 2, 0)], evacuate_mod, 0)

        with nc.Block() as block:
            @block.vector
            def _(dve):
                dve_done.mark(nc.vector.tensor_scalar(modp[:], mods[:], 1.0, None, ALU.add))
                settle(dve, dve_done)
                for m in (2, 5):
                    dve_done.mark(nc.vector.tensor_scalar(modp[:, 0:2, m * KC:(m + 1) * KC, :],
                                                          mods[:, 0:2, m * KC:(m + 1) * KC, :],
                                                          1.0 / ALPHA, None, ALU.mult))

        scratch = sb("scratch", [P, 2, TOK])

        def modulate_parts(layer, which, width, source=None):
            source = source or (lambda k, lo, w: h[:, k, lo:lo + w])
            d0, a0, p0 = dve_done.n, act_done.n, pool_done.n
            segs = [(0, LAT, 0)] + ([(1, CTX, LAT)] if width == TOK else [])
            per = len(segs)
            with nc.Block() as block:
                @block.vector
                def _(dve):
                    for k in range(KC):
                        if k >= 2:
                            dve.wait_ge(pool_done.sem, p0 + k - 1)
                        for s, w, lo in segs:
                            dve_done.mark(nc.vector.tensor_scalar(
                                scratch[:, k % 2, lo:lo + w], source(k, lo, w),
                                modp[:, layer, (which + 1) * KC + k, s:s + 1],
                                mods[:, layer, which * KC + k, s:s + 1], ALU.mult, ALU.add))

                @block.scalar
                def _(act):
                    for k in range(KC):
                        act.wait_ge(dve_done.sem, d0 + per * (k + 1))
                        act_done.mark(nc.scalar.activation(x_hi[:, k, 0:width], scratch[:, k % 2, 0:width], ACT.Copy))

                @block.gpsimd
                def _(pool):
                    for k in range(KC):
                        pool.wait_ge(act_done.sem, a0 + k + 1)
                        pool_done.mark(nc.gpsimd.tensor_tensor(x_lo[:, k, 0:width], scratch[:, k % 2, 0:width],
                                                               x_hi[:, k, 0:width], ALU.subtract))

        def normalise(width, eps, centre, gain=None, bias=None, keep=None):
            segs = [(0, LAT, 0)] + ([(1, CTX, LAT)] if width == TOK else [])
            p0, d0, a0 = pe_done.n, dve_done.n, act_done.n
            dst = keep if keep is not None else h
            with nc.Block() as block:
                @block.tensor
                def _(pe):
                    if centre:
                        for s, w, lo in segs:
                            for k in range(KC):
                                mm = nc.tensor.matmul(ps[:, s, 0:w], SQ("mean"), h[:, k, lo:lo + w],
                                                      start=(k == 0), stop=(k == KC - 1))
                        pe_done.mark(mm)
                    for k in range(KC):
                        pe.wait_ge(act_done.sem, a0 + k + 1)
                        for s, w, lo in segs:
                            mm = nc.tensor.matmul(ps[:, 2 + s, 0:w], SQ("mean"), scratch[:, k % 2, lo:lo + w],
                                                  start=(k == 0), stop=(k == KC - 1))
                        pe_done.mark(mm)

                first = 1 if centre else 0

                @block.scalar
                def _(act):
                    for k in range(KC):
                        if centre:
                            act.wait_ge(dve_done.sem, d0 + k + 1)
                        if k >= 2:
                            act.wait_ge(pe_done.sem, p0 + first + k - 1)
                        act_done.mark(nc.scalar.activation(scratch[:, k % 2, 0:width], h[:, k, 0:width], ACT.Square))
                    act.wait_ge(dve_done.sem, d0 + first * KC + 1)
                    act_done.mark(nc.scalar.activation(scratch[:, 1, 0:width], scratch[:, 0, 0:width], ACT.Sqrt))
                    if gain is not None and bias is not None:
                        for k in range(KC):
                            act.wait_ge(dve_done.sem, d0 + first * KC + 2 + k + 1)
                            act_done.mark(nc.scalar.activation(h[:, k, 0:width], h[:, k, 0:width], ACT.Identity,
                                                               bias=V(bias, k), scale=V(gain, k)))

                @block.vector
                def _(dve):
                    if centre:
                        dve.wait_ge(pe_done.sem, p0 + 1)
                        for k in range(KC):
                            dve_done.mark(nc.vector.tensor_tensor(h[:, k, 0:width], h[:, k, 0:width],
                                                                  banks(0, width), ALU.subtract))
                    dve.wait_ge(pe_done.sem, p0 + first + KC)
                    dve_done.mark(nc.vector.tensor_scalar(scratch[:, 0, 0:width], banks(2, width), eps, None, ALU.add))
                    dve.wait_ge(act_done.sem, a0 + KC + 1)
                    dve_done.mark(nc.vector.reciprocal(scratch[:, 0, 0:width], scratch[:, 1, 0:width]))
                    settle(dve, dve_done)
                    for k in range(KC):
                        if gain is not None and bias is None:
                            dve_done.mark(nc.vector.scalar_tensor_tensor(
                                out=dst[:, k, 0:width], in0=h[:, k, 0:width], scalar=V(gain, k),
                                in1=scratch[:, 0, 0:width], op0=ALU.mult, op1=ALU.mult))
                        else:
                            dve_done.mark(nc.vector.tensor_tensor(dst[:, k, 0:width], h[:, k, 0:width],
                                                                  scratch[:, 0, 0:width], ALU.mult))

        def add_to_residual(layer, which, segments, scale_of=None):
            table = scale_of if scale_of is not None else modp

            def evacuate(dve, c, s, freed):
                for n, (bank, w, lo) in enumerate(segments):
                    ins = nc.vector.scalar_tensor_tensor(
                        out=h[:, bass.ds(c, 1), lo:lo + w], in0=ps[:, 2 * s + bank:2 * s + bank + 1, 0:w],
                        scalar=table[:, layer, bass.ds(c + which * KC, 1), bank:bank + 1],
                        in1=h[:, bass.ds(c, 1), lo:lo + w], op0=ALU.mult, op1=ALU.add)
                    if n == len(segments) - 1:
                        ins.then_inc(psum_free, 1)
                    else:
                        dve_done.mark(ins)
            return evacuate

        def mlp(layer, width):
            segments = BOTH if width == TOK else LATENT
            with ExitStack() as local:
                g_hi = sb(f"g_hi{layer}", [P, 32, width], BF16, local)
                g_lo = sb(f"g_lo{layer}", [P, 32, width], BF16, local)

                def evacuate(dve, c, s, freed):
                    dve_done.mark(nc.vector.tensor_scalar(scratch[:, 0, 0:width], banks(2 * s, width), 0.0, None, ALU.max))
                    settle(dve, dve_done)
                    dve_done.mark(nc.vector.tensor_tensor(scratch[:, 1, 0:width], scratch[:, 0, 0:width], scratch[:, 0, 0:width], ALU.mult))
                    settle(dve, dve_done)
                    dve_done.mark(nc.vector.tensor_copy(g_hi[:, bass.ds(c, 1), :], scratch[:, 1:2, 0:width]))
                    settle(dve, dve_done)
                    nc.vector.tensor_tensor(g_lo[:, bass.ds(c, 1), :], scratch[:, 1:2, 0:width], g_hi[:, bass.ds(c, 1), :],
                                            ALU.subtract).then_inc(psum_free, 1)

                linear(f"ff1_{layer}", *x_parts(x_hi, x_lo), segments, evacuate, 3)
                linear(f"ff2_{layer}", *x_parts(g_hi, g_lo), segments, add_to_residual(layer, 5, segments),
                       len(segments) - 1)

        def keep_chunk(target, width):
            def evacuate(dve, c, s, freed):
                nc.vector.tensor_copy(target[:, bass.ds(c, 1), 0:width],
                                      banks(2 * s, width).unsqueeze(1)).then_inc(psum_free, 1)
            return evacuate

        def attention():
            scores_done, scores_read, max_ready, exp_done, turned, turned_read, out_done, out_read = (
                sem(n) for n in ("scores_done", "scores_read", "max_ready", "exp_done", "turned", "turned_read",
                                 "out_done", "out_read"))
            with ExitStack() as local:
                otok = sb("otok", [P, TB, D], F32, local)
                with ExitStack() as inner:
                    qkv = sb("qkv", [P, 12, TOK], F32, inner)
                    qk_rot = sb("qk_rot", [P, 10, LAT], F32, inner)
                    v_tok = sb("v_tok", [P, TB, 4 * HD], F32, inner)
                    scores = sb("scores", [P, 2, 5 * P], F32, inner)
                    probs = sb("probs", [P, 2, 5 * P], F32, inner)
                    probs_t = scratch.rearrange("p a b -> p (a b)")[:, 0:1280].rearrange("p (u n) -> p u n", u=2)
                    top = sb("top", [P, 96], F32, inner)
                    neg_max = sb("neg_max", [P, 96], F32, inner)
                    row_sum = sb("row_sum", [P, 96], F32, inner)
                    sink_exp = sb("sink_exp", [P, 96], F32, inner)
                    sinks = sb("sinks", [P, 2, HEADS], F32, inner)
                    rope = otok.rearrange("p t d -> p (t d)")[:, 0:2 * LAT].rearrange("p (a n) -> p a n", a=2)

                    linear("att_in", *x_parts(x_hi, x_lo), BOTH, keep_chunk(qkv, TOK), 0)

                    d0, p0, m0 = dve_done.n, pe_done.n, dma_done.n
                    with nc.Block() as block:
                        @block.sync
                        def _(sp):
                            dma_done.mark(sp.dma_start(rope, ext["rope"]), 16)
                            dma_done.mark(sp.dma_start(sinks[:, 0], ext["sinks"]), 16)

                        @block.tensor
                        def _(pe):
                            for c in range(10):
                                if c >= 4:
                                    pe.wait_ge(dve_done.sem, d0 + 3 * (c - 4) + 1)
                                pe_done.mark(nc.tensor.matmul(ps[:, c % 4, :], SQ("rope_swap"), qkv[:, c, 0:LAT],
                                                              start=True, stop=True))
                            for t in range(TB):
                                for c in range(2):
                                    mm = nc.tensor.transpose(ps[:, 4 + t // 2, (t % 2) * 256 + c * P:(t % 2) * 256 + (c + 1) * P],
                                                             qkv[:, 10 + c, t * P:(t + 1) * P], SQ("identity"))
                                pe_done.mark(mm)

                        @block.vector
                        def _(dve):
                            dve.wait_ge(dma_done.sem, m0 + 32)
                            for c in range(10):
                                dve.wait_ge(pe_done.sem, p0 + c + 1)
                                if c >= 1:
                                    settle(dve, dve_done)
                                dve_done.mark(nc.vector.tensor_tensor(scratch[:, 0, 0:LAT], ps[:, c % 4, :], rope[:, 1], ALU.mult))
                                dve_done.mark(nc.vector.tensor_tensor(qk_rot[:, c, :], qkv[:, c, 0:LAT], rope[:, 0], ALU.mult))
                                settle(dve, dve_done)
                                dve_done.mark(nc.vector.tensor_tensor(qk_rot[:, c, :], qk_rot[:, c, :], scratch[:, 0, 0:LAT], ALU.add))

                        @block.scalar
                        def _(act):
                            act.wait_ge(dma_done.sem, m0 + 32)
                            act_done.mark(nc.scalar.activation(sinks[:, 1], sinks[:, 0], ACT.Copy, scale=-1.0))
                            for t in range(TB):
                                act.wait_ge(pe_done.sem, p0 + 10 + (t // 2 + 1) * 2)
                                act_done.mark(nc.scalar.activation(v_tok[:, t, :], ps[:, 4 + t // 2, (t % 2) * 256:(t % 2) * 256 + 256],
                                                                   ACT.Copy))

                    units = []
                    for b in range(TB):
                        near = [t for t in (b - 1, b, b + 1) if 0 <= t < LB] if b < LB else []
                        units += [(b, j, f, near) for j in range(KC) for f in range(2)]
                    U = len(units)

                    with nc.Block() as block:
                        @block.tensor
                        def _(pe):
                            def score(u):
                                b, j, f, near = units[u]
                                rows = slice(64 * f, 64 * f + 64)
                                if u >= 2:
                                    pe.wait_ge(scores_read, u - 1)
                                if near:
                                    nc.tensor.matmul(ps[:, u % 2, 0:len(near) * P], qk_rot[rows, j, b * P:(b + 1) * P],
                                                     qk_rot[rows, 8 + j // 4, near[0] * P:(near[-1] + 1) * P],
                                                     start=True, stop=True)
                                nc.tensor.matmul(ps[:, 2 + u % 2, 0:CTX], qkv[rows, j, b * P:(b + 1) * P],
                                                 qkv[rows, 8 + j // 4, LAT:TOK], start=True, stop=True).then_inc(scores_done, 1)

                            def turn(u):
                                n = len(units[u][3]) + 2
                                pe.wait_ge(exp_done, u + 1)
                                if u >= 2:
                                    pe.wait_ge(turned_read, u - 1)
                                for t in range(n):
                                    dst = ps[:, 4 + u % 2, t * P:(t + 1) * P] if t < 4 else ps[:, 6, 0:P]
                                    if t == 4 and u >= 1:
                                        pe.wait_ge(turned_read, u)
                                    mm = nc.tensor.transpose(dst, probs[:, u % 2, t * P:(t + 1) * P], SQ("identity"))
                                mm.then_inc(turned, 1)

                            def weigh(u):
                                b, j, f, near = units[u]
                                kv = 2 * (j // 4) + f
                                pe.wait_ge(turned_read, u + 1)
                                if u % 8 == 0 and u > 0:
                                    pe.wait_ge(out_read, u // 8)
                                keys = near + [LB, LB + 1]
                                for n, t in enumerate(keys):
                                    mm = nc.tensor.matmul(ps[:, 7, (u % 8) * HD:(u % 8 + 1) * HD],
                                                          probs_t[:, u % 2, n * P:(n + 1) * P],
                                                          v_tok[:, t, kv * HD:(kv + 1) * HD],
                                                          start=(n == 0), stop=(n == len(keys) - 1))
                                mm.then_inc(out_done, 1)

                            for s in range(U + 2):
                                if s < U:
                                    score(s)
                                if 1 <= s <= U:
                                    turn(s - 1)
                                if s >= 2:
                                    weigh(s - 2)

                        @block.vector
                        def _(dve):
                            def read(u):
                                b, j, f, near = units[u]
                                n = len(near) * P
                                dve.wait_ge(scores_done, u + 1)
                                if u >= 2:
                                    dve.wait_ge(exp_done, u - 1)
                                if near:
                                    first = 0 if near[0] == b - 1 else 1
                                    mask = sq[:, SQUARES.index("mask_before"):SQUARES.index("mask_before") + 3, :]
                                    dve_done.mark(nc.vector.tensor_tensor(
                                        scores[:, u % 2, 0:n].rearrange("p (a b) -> p a b", b=P),
                                        ps[:, u % 2, 0:n].rearrange("p (a b) -> p a b", b=P),
                                        mask[:, first:first + len(near), :], ALU.add))
                                dve_done.mark(nc.vector.tensor_copy(scores[:, u % 2, n:n + CTX], ps[:, 2 + u % 2, 0:CTX]))
                                settle(dve, dve_done)
                                nc.vector.tensor_reduce(top[:, u:u + 1], scores[:, u % 2, 0:n + CTX], AX.X,
                                                        ALU.max).then_inc(scores_read, 1)
                                dve.wait_ge(scores_read, u + 1)
                                nc.vector.tensor_scalar(neg_max[:, u:u + 1], top[:, u:u + 1], -HD ** -0.5,
                                                        sinks[:, 1, 2 * j + f:2 * j + f + 1], ALU.mult,
                                                        ALU.min).then_inc(max_ready, 1)

                            def finish(g):
                                a, z = 8 * g, 8 * g + 8
                                dve.wait_ge(out_done, z)
                                dve_done.mark(nc.vector.tensor_tensor(row_sum[:, a:z], row_sum[:, a:z], sink_exp[:, a:z], ALU.add))
                                settle(dve, dve_done)
                                dve_done.mark(nc.vector.reciprocal(row_sum[:, a:z], row_sum[:, a:z]))
                                settle(dve, dve_done)
                                nc.vector.tensor_tensor(
                                    otok[:, g // 2, (g % 2) * BANK:(g % 2 + 1) * BANK].rearrange("p (h d) -> p h d", d=HD),
                                    ps[:, 7, :].rearrange("p (h d) -> p h d", d=HD),
                                    row_sum[:, a:z].unsqueeze(2).broadcast_to([P, 8, HD]), ALU.mult).then_inc(out_read, 1)

                            for s in range(U):
                                read(s)
                                if s % 8 == 1 and s > 8:
                                    finish(s // 8 - 1)
                            finish(U // 8 - 1)

                        @block.scalar
                        def _(act):
                            def exps(u):
                                b, j, f, near = units[u]
                                n = len(near) * P + CTX
                                act.wait_ge(max_ready, u + 1)
                                if u >= 2:
                                    act.wait_ge(turned, u - 1)
                                act_done.mark(nc.scalar.activation(sink_exp[:, u:u + 1], sinks[:, 0, 2 * j + f:2 * j + f + 1],
                                                                   ACT.Exp, bias=neg_max[:, u:u + 1]))
                                nc.scalar.activation(probs[:, u % 2, 0:n], scores[:, u % 2, 0:n], ACT.Exp,
                                                     bias=neg_max[:, u:u + 1], scale=HD ** -0.5,
                                                     accum_out=row_sum[:, u:u + 1]).then_inc(exp_done, 1)

                            def copy(u):
                                n = len(units[u][3]) + 2
                                act.wait_ge(turned, u + 1)
                                if u >= 2:
                                    act.wait_ge(out_done, u - 1)
                                wide = min(n, 4) * P
                                ins = nc.scalar.activation(probs_t[:, u % 2, 0:wide], ps[:, 4 + u % 2, 0:wide], ACT.Copy)
                                if n > 4:
                                    act_done.mark(ins)
                                    ins = nc.scalar.activation(probs_t[:, u % 2, 4 * P:5 * P],
                                                               ps[:, 6, 0:P], ACT.Copy)
                                ins.then_inc(turned_read, 1)

                            for s in range(U + 1):
                                if s < U:
                                    exps(s)
                                if s >= 1:
                                    copy(s - 1)

                to_feature_major(otok, TB, KC)

            linear("att_out", *x_parts(x_hi, x_lo), BOTH, add_to_residual(0, 2, BOTH), 1)

        def to_feature_major(source, blocks, chunks):
            p0, a0, d0 = pe_done.n, act_done.n, dve_done.n
            groups = [(t, c) for t in range(blocks) for c in range(0, chunks, 4)]
            with nc.Block() as block:
                @block.tensor
                def _(pe):
                    for g, (t, c) in enumerate(groups):
                        if g >= 4:
                            pe.wait_ge(dve_done.sem, d0 + g - 3)
                        for k in range(4):
                            mm = nc.tensor.transpose(ps[:, g % 4, k * P:(k + 1) * P],
                                                     source[:, t, (c + k) * P:(c + k + 1) * P], SQ("identity"))
                        pe_done.mark(mm)

                @block.scalar
                def _(act):
                    for g, (t, c) in enumerate(groups):
                        act.wait_ge(pe_done.sem, p0 + g + 1)
                        act_done.mark(nc.scalar.activation(x_hi[:, c:c + 4, t * P:(t + 1) * P],
                                                           ps[:, g % 4, :].rearrange("p (c t) -> p c t", c=4), ACT.Copy))

                @block.vector
                def _(dve):
                    for g, (t, c) in enumerate(groups):
                        dve.wait_ge(act_done.sem, a0 + g + 1)
                        dve_done.mark(nc.vector.tensor_tensor(x_lo[:, c:c + 4, t * P:(t + 1) * P],
                                                              ps[:, g % 4, :].rearrange("p (c t) -> p c t", c=4),
                                                              x_hi[:, c:c + 4, t * P:(t + 1) * P], ALU.subtract))

        def pad_layout(rows):
            at, out = 2, []
            for lo, w in rows:
                out.append((lo, w, at))
                at += w + 4
            return out, at + 2

        def convolve(pad, acc, target, layout, width, weights, n_chunks, chunk0, bias):
            w0 = columns[weights][0]
            span = width - 4

            def evacuate(dve, c, s, freed):
                n = len(layout)
                groups = []
                for lo, w, at in layout:
                    if groups and groups[-1][1] == w:
                        groups[-1][3] += 1
                    else:
                        groups.append([lo, w, at, 1])
                for lo, w, at, count in groups:
                    dst = pad[:, at:at + count * (w + 4)].rearrange("p (r n) -> p r n", r=count)[:, :, 0:w]
                    src = banks(2 * s, TOK)[:, lo:lo + count * w].rearrange("p (r n) -> p r n", r=count)
                    ins = nc.vector.tensor_copy(dst, src)
                    if lo + count * w == sum(x[1] for x in layout):
                        ins.then_inc(psum_free, 1)
                    else:
                        dve_done.mark(ins)
                settle(dve, dve_done)
                dve.wait_ge(psum_free, freed)
                for tap in range(5):
                    scalar = vec[:, bass.ds(c + (w0 + tap * n_chunks + chunk0), 1)]
                    src = pad[:, tap:tap + span]
                    if tap == 0:
                        if bias is None:
                            ins = nc.vector.tensor_scalar(acc[:, 0:span], src, scalar, None, ALU.mult)
                        else:
                            ins = nc.vector.tensor_scalar(acc[:, 0:span], src, scalar,
                                                          vec[:, bass.ds(c + (columns[bias][0] + chunk0), 1)], ALU.mult, ALU.add)
                    else:
                        ins = nc.vector.scalar_tensor_tensor(out=acc[:, 0:span], in0=src, scalar=scalar,
                                                             in1=acc[:, 0:span], op0=ALU.mult, op1=ALU.add)
                    dve_done.mark(ins)
                    settle(dve, dve_done)
                for lo, w, at, count in groups:
                    dst = target[:, bass.ds(c, 1), lo:lo + count * w].rearrange("p a (r n) -> p (a r) n", r=count)
                    dve_done.mark(nc.vector.tensor_copy(dst, acc[:, at - 2:at - 2 + count * (w + 4)].rearrange(
                        "p (r n) -> p r n", r=count)[:, :, 0:w]))
                settle(dve, dve_done)
            return evacuate

        def per_conv(groups):
            return groups - 1 + 5 + groups

        def softplus(v, tmp):
            e, u, d, r = tmp
            a0, d0 = act_done.n, dve_done.n
            with nc.Block() as block:
                @block.scalar
                def _(act):
                    act_done.mark(nc.scalar.activation(e, v, ACT.Abs))
                    settle(act, act_done)
                    act_done.mark(nc.scalar.activation(e, e, ACT.Exp, scale=-1.0))
                    act.wait_ge(dve_done.sem, d0 + 1)
                    act_done.mark(nc.scalar.activation(r, u, ACT.Ln))

                @block.vector
                def _(dve):
                    dve.wait_ge(act_done.sem, a0 + 2)
                    dve_done.mark(nc.vector.tensor_scalar(u, e, 1.0, None, ALU.add))
                    settle(dve, dve_done)
                    dve_done.mark(nc.vector.tensor_scalar(d, u, 1.0, None, ALU.subtract))
                    dve.wait_ge(act_done.sem, a0 + 3)
                    settle(dve, dve_done)
                    dve_done.mark(nc.vector.scalar_tensor_tensor(out=u, in0=d, scalar=0.0, in1=e, op0=ALU.is_equal, op1=ALU.mult))
                    dve_done.mark(nc.vector.tensor_tensor(r, r, e, ALU.mult))
                    settle(dve, dve_done)
                    dve_done.mark(nc.vector.tensor_scalar(d, d, 2.0 ** -24, None, ALU.max))
                    settle(dve, dve_done)
                    dve_done.mark(nc.vector.reciprocal(d, d))
                    settle(dve, dve_done)
                    dve_done.mark(nc.vector.tensor_tensor(r, r, d, ALU.mult))
                    settle(dve, dve_done)
                    dve_done.mark(nc.vector.tensor_tensor(r, r, u, ALU.add))
                    settle(dve, dve_done)
                    dve_done.mark(nc.vector.scalar_tensor_tensor(out=v, in0=v, scalar=0.0, in1=r, op0=ALU.max, op1=ALU.add))

        def small_product(w_ext, n, w32, wh, wl, target):
            m0, a0, d0, p0 = dma_done.n, act_done.n, dve_done.n, pe_done.n
            with nc.Block() as block:
                @block.sync
                def _(sp):
                    dma_done.mark(sp.dma_start(w32, w_ext), 16)

                @block.scalar
                def _(act):
                    act.wait_ge(dma_done.sem, m0 + 16)
                    act_done.mark(nc.scalar.activation(wh, w32, ACT.Copy))

                @block.tensor
                def _(pe):
                    pe.wait_ge(dve_done.sem, d0 + 1)
                    for t in range(TB):
                        for k in range(KC):
                            for part, (x, w) in enumerate(((x_hi, wh), (x_lo, wh), (x_hi, wl))):
                                mm = nc.tensor.matmul(ps[:, 0, t * n:(t + 1) * n], x[:, k, t * P:(t + 1) * P], w[:, k, :],
                                                      start=(k == 0 and part == 0), stop=(k == KC - 1 and part == 2))
                    pe_done.mark(mm)

                @block.vector
                def _(dve):
                    dve.wait_ge(act_done.sem, a0 + 1)
                    dve_done.mark(nc.vector.tensor_tensor(wl, w32, wh, ALU.subtract))
                    dve.wait_ge(pe_done.sem, p0 + 1)
                    dve_done.mark(nc.vector.tensor_copy(target, ps[:, 0, 0:TB * n].rearrange("p (t n) -> p t n", n=n)))

        def silu_and_turn(source, chunks, target, turned_chunks):
            a0, p0, d0 = act_done.n, pe_done.n, dve_done.n
            with nc.Block() as block:
                @block.scalar
                def _(act):
                    for c in range(chunks):
                        act_done.mark(nc.scalar.activation(source[:, c, :], source[:, c, :], ACT.Silu))

                @block.tensor
                def _(pe):
                    for c in range(turned_chunks):
                        pe.wait_ge(act_done.sem, a0 + c + 1)
                        if c >= 4:
                            pe.wait_ge(dve_done.sem, d0 + c - 3)
                        for t in range(TB):
                            mm = nc.tensor.transpose(banks(2 * (c % 4), TOK)[:, t * P:(t + 1) * P], source[:, c, t * P:(t + 1) * P], SQ("identity"))
                        pe_done.mark(mm)

                @block.vector
                def _(dve):
                    for c in range(turned_chunks):
                        dve.wait_ge(pe_done.sem, p0 + c + 1)
                        dve_done.mark(nc.vector.tensor_copy(target[:, :, c * P:(c + 1) * P],
                                                            banks(2 * (c % 4), TOK).rearrange("p (t n) -> p t n", n=P)))

        def ssm(x_tok, local):
            b_tok = sb("b_tok", [P, TB, 512], F32, local)
            with ExitStack() as first:
                x_t = sb("x_t", [P, 16, TOK], F32, first)
                layout, width = pad_layout([(0, LAT), (LAT, CTX)])
                pad = b_tok.rearrange("p t n -> p (t n)")[:, 0:width]
                acc = b_tok.rearrange("p t n -> p (t n)")[:, 1024:1024 + width]
                zero_pad(pad)
                linear("ssm_x", *x_parts(x_hi, x_lo), BOTH,
                       convolve(pad, acc, x_t, layout, width, "conv_w", 24, 0, "conv_b"), per_conv(2))
                silu_and_turn(x_t, 16, x_tok, 16)
            bc_t = sb("bc_t", [P, 8, TOK], F32, local)
            extra = sb("extra", [P, 2, 2, LAT], F32, local)
            dt = sb("dt", [P, TB, 64], F32, local)
            cum = sb("cum", [P, TB, 64], F32, local)
            tot = sb("tot", [P, TB, 64], F32, local)
            rows = sb("rows", [P, 128], F32, local)
            flat = extra.rearrange("p a b n -> p (a b n)")
            layout, width = pad_layout([(0, LAT), (LAT, CTX)])
            pad, acc = flat[:, 0:width], flat[:, 1024:1024 + width]
            zero_pad(pad)
            linear("ssm_bc", *x_parts(x_hi, x_lo), BOTH,
                   convolve(pad, acc, bc_t, layout, width, "conv_w", 24, 16, "conv_b"), per_conv(2))
            silu_and_turn(bc_t, 8, b_tok, 4)
            dtw = flat[:, 0:512].rearrange("p (k n) -> p k n", k=KC)
            dth = flat[:, 512:768].bitcast(BF16).rearrange("p (k n) -> p k n", k=KC)
            dtl = flat[:, 768:1024].bitcast(BF16).rearrange("p (k n) -> p k n", k=KC)
            small_product(ext["dt_w"], 64, dtw, dth, dtl, dt[:])
            m0 = dma_done.n
            with nc.Block() as block:
                @block.sync
                def _(sp):
                    dma_done.mark(sp.dma_start(rows[:], ext["dt_rows"]), 16)

                @block.vector
                def _(dve):
                    dve.wait_ge(dma_done.sem, m0 + 16)
                    dve_done.mark(nc.vector.tensor_tensor(dt[:], dt[:], rows[:, 0:64].unsqueeze(1).broadcast_to([P, TB, 64]), ALU.add))
            f4 = flat[:, 0:4 * 384].rearrange("p (a t n) -> p a t n", a=4, t=TB)
            softplus(dt[:], [f4[:, q] for q in range(4)])
            p0, a0, d0 = pe_done.n, act_done.n, dve_done.n
            a_of = f4[:, 0]
            with nc.Block() as block:
                @block.scalar
                def _(act):
                    act_done.mark(nc.scalar.activation(rows[:, 0:64], rows[:, 64:128], ACT.Exp))
                    act.wait_ge(dve_done.sem, d0 + 5)
                    act_done.mark(nc.scalar.activation(tot[:], tot[:], ACT.Exp))

                @block.vector
                def _(dve):
                    dve.wait_ge(act_done.sem, a0 + 1)
                    dve_done.mark(nc.vector.tensor_scalar(rows[:, 0:64], rows[:, 0:64], -1.0, None, ALU.mult))
                    settle(dve, dve_done)
                    dve_done.mark(nc.vector.tensor_tensor(a_of, dt[:], rows[:, 0:64].unsqueeze(1).broadcast_to([P, TB, 64]), ALU.mult))
                    dve.wait_ge(pe_done.sem, p0 + 1)
                    dve_done.mark(nc.vector.tensor_copy(cum[:], ps[:, 0, 0:384].rearrange("p (t n) -> p t n", n=64)))
                    dve_done.mark(nc.vector.tensor_copy(tot[:], ps[:, 1, 0:384].rearrange("p (t n) -> p t n", n=64)))
                    settle(dve, dve_done)
                    dve_done.mark(nc.vector.tensor_tensor(f4[:, 1], tot[:], cum[:], ALU.subtract))

                @block.tensor
                def _(pe):
                    pe.wait_ge(dve_done.sem, d0 + 2)
                    for t in range(TB):
                        for d, m in enumerate(("sum_upto", "sum_from")):
                            nc.tensor.matmul(ps[:, 0, t * 64 + 32 * d:t * 64 + 32 * d + 32], SQ(m), a_of[:, t, 32 * d:32 * d + 32],
                                             start=True, stop=True)
                    pe_done.mark(nc.tensor.matmul(ps[:, 1, 0:384], SQ("ones"), a_of.rearrange("p t n -> p (t n)"), start=True, stop=True))
            wgt = sb("wgt", [P, TB, 64], F32, local)
            a_keep = sb("a_keep", [P, TB, 64], F32, local)
            a1 = act_done.n
            with nc.Block() as block:
                @block.scalar
                def _(act):
                    act_done.mark(nc.scalar.activation(f4[:, 1], f4[:, 1], ACT.Exp))
                    act_done.mark(nc.scalar.activation(a_keep[:], a_of, ACT.Copy))

                @block.vector
                def _(dve):
                    dve.wait_ge(act_done.sem, a1 + 1)
                    dve_done.mark(nc.vector.tensor_tensor(wgt[:], f4[:, 1], dt[:], ALU.mult))

            x_flat = [x_hi.rearrange("p k n -> p (k n)").bitcast(F32), x_lo.rearrange("p k n -> p (k n)").bitcast(F32)]
            states = [x_flat[d][:, 0:2048].rearrange("p (c n) -> p c n", c=LB) for d in range(2)]
            carry = [x_flat[d][:, 2048:2560] for d in range(2)]
            weighted = w_hi.rearrange("p r n -> p (r n)").bitcast(F32)[:, 0:1024].rearrange("p (u n) -> p u n", u=2)
            cb = x_flat[0][:, 2560:3072]
            spread = w_hi.rearrange("p r n -> p (r n)").bitcast(F32).rearrange("p (u d n) -> p u d n", u=2, d=2)
            decay = w_lo.rearrange("p r n -> p (r n)").bitcast(F32).rearrange("p (u d n) -> p u d n", u=2, d=2)
            mixed = scratch.rearrange("p a n -> p (a n)")[:, 0:1024].rearrange("p (u n) -> p u n", u=2)
            c_scaled = extra
            for g in range(4):
                ssm_states(g, x_tok, b_tok, wgt, tot, states, carry, weighted)
                ssm_heads(g, x_tok, bc_t, dt, a_keep, cum, states, cb, spread, decay, mixed, c_scaled)

        def zero_pad(pad):
            with nc.Block() as block:
                @block.vector
                def _(dve):
                    dve_done.mark(nc.vector.memset(pad, 0.0))

        def ssm_states(g, x_tok, b_tok, wgt, tot, states, carry, weighted):
            steps = []
            for n in range(5):
                steps += [(0, (4, 5, 0, 1, 2)[n], n), (1, (5, 4, 3, 2, 1)[n], n)]
            pool0, p0, d0 = pool_done.n, pe_done.n, dve_done.n
            heads = slice(8 * g, 8 * g + 8)
            with nc.Block() as block:
                @block.gpsimd
                def _(pool):
                    for k, (d, t, n) in enumerate(steps):
                        if k >= 2:
                            pool.wait_ge(pe_done.sem, p0 + k - 1)
                        pool_done.mark(nc.gpsimd.tensor_tensor(
                            weighted[:, k % 2].rearrange("p (h n) -> p h n", h=8),
                            x_tok[:, t, g * 512:(g + 1) * 512].rearrange("p (h n) -> p h n", h=8),
                            wgt[:, t, 32 * d + 8 * g:32 * d + 8 * g + 8].unsqueeze(2).broadcast_to([P, 8, HD]), ALU.mult))

                @block.tensor
                def _(pe):
                    for k, (d, t, n) in enumerate(steps):
                        pe.wait_ge(pool_done.sem, pool0 + k + 1)
                        if k >= 2:
                            pe.wait_ge(dve_done.sem, d0 + 2 * (k - 1))
                        pe_done.mark(nc.tensor.matmul(ps[:, k % 2, :], b_tok[:, t, g * P:(g + 1) * P], weighted[:, k % 2],
                                                      start=True, stop=True))

                @block.vector
                def _(dve):
                    def slot(d, n):
                        return carry[d] if n == 0 else states[d][:, n - 1 if d == 0 else 4 - n]
                    for k, (d, t, n) in enumerate(steps):
                        now = slot(d, n)
                        if n == 0:
                            dve_done.mark(nc.vector.memset(now, 0.0))
                        else:
                            if k >= 2:
                                settle(dve, dve_done)
                            dve_done.mark(nc.vector.tensor_tensor(
                                now.rearrange("p (h n) -> p h n", h=8), slot(d, n - 1).rearrange("p (h n) -> p h n", h=8),
                                tot[:, t, 32 * d + 8 * g:32 * d + 8 * g + 8].unsqueeze(2).broadcast_to([P, 8, HD]), ALU.mult))
                        dve.wait_ge(pe_done.sem, p0 + k + 1)
                        settle(dve, dve_done)
                        dve_done.mark(nc.vector.tensor_tensor(now, now, ps[:, k % 2, :], ALU.add))

        ssm_sems = [sem(n) for n in ("sums_done", "spread_done", "diff_done", "decay_done", "mixed_done",
                                     "c_scaled_done", "y_done", "y_kept")]

        def ssm_heads(g, x_tok, bc_t, dt, a_keep, cum, states, cb, spread, decay, mixed, c_scaled):
            sums_done, spread_done, diff_done, decay_done, mixed_done, c_scaled_done, y_done, y_kept = ssm_sems
            n0 = 8 * g
            k0 = 4 * g
            p0, d0 = pe_done.n, dve_done.n
            with nc.Block() as block:
                @block.tensor
                def _(pe):
                    for t in range(LB):
                        mm = nc.tensor.matmul(ps[:, 6, t * P:(t + 1) * P], bc_t[:, g, t * P:(t + 1) * P],
                                              bc_t[:, 4 + g, t * P:(t + 1) * P], start=True, stop=True)
                    pe_done.mark(mm)

                    def sums(v):
                        if v >= 2:
                            pe.wait_ge(diff_done, n0 + v - 1)
                        for d, m in enumerate(("sum_upto", "sum_from")):
                            for t in range(LB):
                                col = 32 * d + n0 + v
                                mm = nc.tensor.matmul(ps[:, 2 * d + v % 2, t * P:(t + 1) * P],
                                                      a_keep[:, t, col:col + 1].broadcast_to([P, P]), SQ(m),
                                                      start=True, stop=True)
                        mm.then_inc(sums_done, 1)

                    def outputs(v):
                        h_ = n0 + v
                        pe.wait_ge(mixed_done, n0 + v + 1)
                        pe.wait_ge(c_scaled_done, n0 + v + 1)
                        if v >= 4 and v % 2 == 0:
                            pe.wait_ge(y_kept, k0 + v // 2 - 1)
                        rows = slice(64 * (v % 2), 64 * (v % 2) + 64)
                        for t in range(LB):
                            dst = ps[rows, 4 + v // 2 % 2, t * P:(t + 1) * P]
                            cols = slice(t * P, (t + 1) * P)
                            nc.tensor.matmul(dst, x_tok[:, t, h_ * HD:(h_ + 1) * HD], mixed[:, v % 2, cols], start=True, stop=False)
                            nc.tensor.matmul(dst, states[0][:, t, v * HD:(v + 1) * HD], c_scaled[:, v % 2, 0, cols], start=False, stop=False)
                            mm = nc.tensor.matmul(dst, states[1][:, t, v * HD:(v + 1) * HD], c_scaled[:, v % 2, 1, cols], start=False, stop=True)
                        mm.then_inc(y_done, 1)

                    for s in range(9):
                        if s < 8:
                            sums(s)
                        if s >= 1:
                            outputs(s - 1)

                @block.scalar
                def _(act):
                    def spreads(v):
                        act.wait_ge(sums_done, n0 + v + 1)
                        if v >= 2:
                            act.wait_ge(c_scaled_done, n0 + v - 1)
                        for d in range(2):
                            ins = nc.scalar.activation(spread[:, v % 2, d], ps[:, 2 * d + v % 2, :], ACT.Exp)
                            if d == 0:
                                act_done.mark(ins)
                        ins.then_inc(spread_done, 1)

                    def decays(v):
                        act.wait_ge(diff_done, n0 + v + 1)
                        nc.scalar.activation(decay[:, v % 2], decay[:, v % 2], ACT.Exp).then_inc(decay_done, 1)

                    def keep(v):
                        act.wait_ge(y_done, n0 + v + 1)
                        cc = (n0 + v) // 2
                        nc.scalar.activation(x_tok[:, 0:LB, cc * P:(cc + 1) * P],
                                             ps[:, 4 + v // 2 % 2, :].rearrange("p (t n) -> p t n", n=P),
                                             ACT.Copy).then_inc(y_kept, 1)

                    for s in range(10):
                        if s < 8:
                            spreads(s)
                        if 1 <= s <= 8:
                            decays(s - 1)
                        if s >= 2 and (s - 2) % 2 == 1:
                            keep(s - 2)

                @block.gpsimd
                def _(pool):
                    for v in range(8):
                        pool.wait_ge(spread_done, n0 + v + 1)
                        if v >= 2:
                            pool.wait_ge(y_done, n0 + v - 1)
                        for d in range(2):
                            ins = nc.gpsimd.tensor_tensor(c_scaled[:, v % 2, d], bc_t[:, 4 + g, 0:LAT], spread[:, v % 2, d], ALU.mult)
                            if d == 0:
                                pool_done.mark(ins)
                        ins.then_inc(c_scaled_done, 1)

                @block.vector
                def _(dve):
                    dve.wait_ge(pe_done.sem, p0 + 1)
                    dve_done.mark(nc.vector.tensor_copy(cb, ps[:, 6, :]))

                    def diffs(v):
                        dve.wait_ge(spread_done, n0 + v + 1)
                        if v >= 2:
                            dve.wait_ge(mixed_done, n0 + v - 1)
                        for d, m in enumerate(("mask_before", "mask_after")):
                            for t in range(LB):
                                col = 32 * d + n0 + v
                                ins = nc.vector.scalar_tensor_tensor(
                                    out=decay[:, v % 2, d, t * P:(t + 1) * P], in0=ps[:, 2 * d + v % 2, t * P:(t + 1) * P],
                                    scalar=cum[:, t, col:col + 1], in1=SQ(m), op0=ALU.subtract, op1=ALU.add)
                        ins.then_inc(diff_done, 1)

                    def mix(v):
                        dve.wait_ge(decay_done, n0 + v + 1)
                        if v >= 2:
                            dve.wait_ge(y_done, n0 + v - 1)
                        h_ = n0 + v
                        for t in range(LB):
                            cols = slice(t * P, (t + 1) * P)
                            dve_done.mark(nc.vector.tensor_scalar(mixed[:, v % 2, cols], decay[:, v % 2, 0, cols],
                                                                  dt[:, t, h_:h_ + 1], None, ALU.mult))
                        settle(dve, dve_done)
                        for t in range(LB):
                            cols = slice(t * P, (t + 1) * P)
                            dve_done.mark(nc.vector.scalar_tensor_tensor(
                                out=mixed[:, v % 2, cols], in0=decay[:, v % 2, 1, cols], scalar=dt[:, t, 32 + h_:33 + h_],
                                in1=mixed[:, v % 2, cols], op0=ALU.mult, op1=ALU.add))
                        settle(dve, dve_done)
                        dve_done.mark(nc.vector.tensor_tensor(mixed[:, v % 2], mixed[:, v % 2], cb, ALU.mult))
                        settle(dve, dve_done)
                        nc.vector.scalar_tensor_tensor(
                            out=mixed[:, v % 2].rearrange("p (t n) -> p t n", n=P),
                            in0=SQ("identity").unsqueeze(1).broadcast_to([P, LB, P]), scalar=skip[:, h_:h_ + 1],
                            in1=mixed[:, v % 2].rearrange("p (t n) -> p t n", n=P), op0=ALU.mult, op1=ALU.add).then_inc(mixed_done, 1)

                    for s in range(9):
                        if s < 8:
                            diffs(s)
                        if s >= 1:
                            mix(s - 1)

        skip = sb("skip", [P, SHEADS])
        with nc.Block() as block:
            @block.sync
            def _(sp):
                dma_done.mark(sp.dma_start(skip[:], ext["ssm_d"]), 16)
                settle(sp, dma_done)

        def ssm_finish(y_tok):
            with ExitStack() as local:
                z = sb("z", [P, 16, LAT], F32, local)
                stat = sb("stat", [P, LAT], F32, local)
                zp = z.rearrange("p c n -> p (c n)").bitcast(BF16).rearrange("p (c n) -> p c n", c=16)
                y = lambda c: y_tok[:, 0:LB, c * P:(c + 1) * P]
                r3 = lambda t: t.rearrange("p (t n) -> p t n", n=P)
                linear("ssm_z", *x_parts(x_hi, x_lo), LATENT, keep_chunk(z, LAT), 0)
                p0, a0, d0 = pe_done.n, act_done.n, dve_done.n
                with nc.Block() as block:
                    @block.scalar
                    def _(act):
                        for c in range(17):
                            if c < 16:
                                act_done.mark(nc.scalar.activation(z[:, c], z[:, c], ACT.Silu))
                            if c >= 1:
                                act.wait_ge(dve_done.sem, d0 + c)
                                if c >= 3:
                                    act.wait_ge(pe_done.sem, p0 + c - 2)
                                act_done.mark(nc.scalar.activation(r3(scratch[:, (c - 1) % 2, 0:LAT]), y(c - 1), ACT.Square))

                    @block.vector
                    def _(dve):
                        for c in range(16):
                            dve.wait_ge(act_done.sem, a0 + max(1, 2 * c))
                            dve_done.mark(nc.vector.tensor_tensor(y(c), y(c), r3(z[:, c]), ALU.mult))

                    @block.tensor
                    def _(pe):
                        for c in range(16):
                            pe.wait_ge(act_done.sem, a0 + (2 * c + 3 if c < 15 else 32))
                            pe_done.mark(nc.tensor.matmul(ps[:, c // 4, :], SQ("group_mean"), scratch[:, c % 2, 0:LAT],
                                                          start=(c % 4 == 0), stop=(c % 4 == 3)))
                a0, d0 = act_done.n, dve_done.n
                with nc.Block() as block:
                    @block.vector
                    def _(dve):
                        for g in range(4):
                            dve_done.mark(nc.vector.tensor_scalar(stat[:], ps[:, g, :], EPS_RMS, None, ALU.add))
                            dve.wait_ge(act_done.sem, a0 + 5 * g + 1)
                            dve_done.mark(nc.vector.reciprocal(stat[:], stat[:]))
                            settle(dve, dve_done)
                            for q in range(4):
                                c = 4 * g + q
                                if q >= 2:
                                    dve.wait_ge(dve_done.sem, d0 + 10 * g + 2 + 2 * (q - 2) + 2)
                                dve_done.mark(nc.vector.scalar_tensor_tensor(
                                    out=r3(scratch[:, q % 2, 0:LAT]), in0=y(c), scalar=V("ssm_norm_g", c), in1=r3(stat[:]),
                                    op0=ALU.mult, op1=ALU.mult))
                                dve.wait_ge(act_done.sem, a0 + 5 * g + 1 + q + 1)
                                dve_done.mark(nc.vector.tensor_tensor(zp[:, c, LAT:2 * LAT], scratch[:, q % 2, 0:LAT], zp[:, c, 0:LAT], ALU.subtract))

                    @block.scalar
                    def _(act):
                        for g in range(4):
                            act.wait_ge(dve_done.sem, d0 + 10 * g + 1)
                            act_done.mark(nc.scalar.activation(stat[:], stat[:], ACT.Sqrt))
                            for q in range(4):
                                act.wait_ge(dve_done.sem, d0 + 10 * g + 2 + 2 * q + 1)
                                act_done.mark(nc.scalar.activation(zp[:, 4 * g + q, 0:LAT], scratch[:, q % 2, 0:LAT], ACT.Copy))
                linear("ssm_out", lambda k, lo, w: zp[:, k, lo:lo + w], lambda k, lo, w: zp[:, k, LAT + lo:LAT + lo + w],
                       LATENT, add_to_residual(1, 2, LATENT), 0)

        def load_and_wait(pairs):
            with nc.Block() as block:
                @block.sync
                def _(sp):
                    for dst, src in pairs:
                        dma_done.mark(sp.dma_start(dst, src), 16)
                    settle(sp, dma_done)

        def unit_rows(tok, blocks, square, sums, scale):
            a0, d0 = act_done.n, dve_done.n
            with nc.Block() as block:
                @block.vector
                def _(dve):
                    for t in range(blocks):
                        settle(dve, dve_done)
                        dve_done.mark(nc.vector.tensor_tensor(square, tok[:, t], tok[:, t], ALU.mult))
                        settle(dve, dve_done)
                        dve_done.mark(nc.vector.tensor_reduce(sums[:, t], square.rearrange("p (h d) -> p h d", d=P), AX.X, ALU.add))
                    settle(dve, dve_done)
                    dve_done.mark(nc.vector.tensor_scalar(sums[:, 0:blocks], sums[:, 0:blocks], EPS, None, ALU.add))
                    dve.wait_ge(act_done.sem, a0 + 1)
                    dve_done.mark(nc.vector.reciprocal(sums[:, 0:blocks], sums[:, 0:blocks]))
                    settle(dve, dve_done)
                    dve_done.mark(nc.vector.tensor_scalar(sums[:, 0:blocks], sums[:, 0:blocks], scale, None, ALU.mult))
                    settle(dve, dve_done)
                    for t in range(blocks):
                        dve_done.mark(nc.vector.tensor_tensor(
                            tok[:, t].rearrange("p (h d) -> p h d", d=P), tok[:, t].rearrange("p (h d) -> p h d", d=P),
                            sums[:, t].unsqueeze(2).broadcast_to([P, DH, P]), ALU.mult))

                @block.scalar
                def _(act):
                    act.wait_ge(dve_done.sem, d0 + 2 * blocks + 1)
                    act_done.mark(nc.scalar.activation(sums[:, 0:blocks], sums[:, 0:blocks], ACT.Sqrt))

        def turn_back(tok, blocks, target):
            p0, a0, d0 = pe_done.n, act_done.n, dve_done.n
            groups = [(t, c) for t in range(blocks) for c in (0, 4)]
            with nc.Block() as block:
                @block.tensor
                def _(pe):
                    for g, (t, c) in enumerate(groups):
                        if g >= 4:
                            pe.wait_ge((act_done, dve_done)[g % 2].sem, (a0, d0)[g % 2] + (g - 4) // 2 + 1)
                        for k in range(4):
                            mm = nc.tensor.transpose(ps[:, g % 4, k * P:(k + 1) * P], tok[:, t, (c + k) * P:(c + k + 1) * P], SQ("identity"))
                        pe_done.mark(mm)

                def view(g):
                    t, c = groups[g]
                    return target[:, c:c + 4, t * P:(t + 1) * P], ps[:, g % 4, :].rearrange("p (c n) -> p c n", c=4)

                @block.scalar
                def _(act):
                    for g in range(0, len(groups), 2):
                        act.wait_ge(pe_done.sem, p0 + g + 1)
                        act_done.mark(nc.scalar.activation(*view(g), ACT.Copy))

                @block.vector
                def _(dve):
                    for g in range(1, len(groups), 2):
                        dve.wait_ge(pe_done.sem, p0 + g + 1)
                        dve_done.mark(nc.vector.tensor_copy(*view(g)))

        delta_sems = [sem(n) for n in ("rows_done", "gap_done", "gap_exp_done", "n_done", "strict_done", "square_done",
                                       "b_kept", "n_kept", "z_step_done", "z_done")]
        state_sems = [sem(n) for n in ("ks_done", "rest_done", "solved", "v_new_done", "v_decayed", "own_done",
                                       "own_added", "o_s_done", "s_next_done", "s_kept", "o_added")]

        def delta_inverse(n, order, qa, z, nb, k_t, q_t, gamma, beta, g_cum):
            rows_done, gap_done, gap_exp_done, n_done, strict_done, square_done, b_kept, n_kept, z_step_done, z_done = delta_sems
            latent = n >= 2
            with nc.Block() as block:
                def quad(pair, w):
                    zq = 2 * pair + w
                    d = zq // 2
                    return zq, d, order[d][n], 4 * (zq % 2)

                def pp(pair):
                    return 2 * n + pair

                @block.tensor
                def _(pe):
                    for pair in range(2):
                        for w in range(2):
                            zq, d, t, h0 = quad(pair, w)
                            if pair == 1:
                                pe.wait_ge(z_done, 12 * pp(0) + 11 + w)
                            m = "sum_upto" if d == 0 else "sum_from"
                            for q in range(4):
                                col = 8 * d + h0 + q
                                cols = slice(q * P, (q + 1) * P)
                                tok = slice(t * P, (t + 1) * P)
                                nc.tensor.matmul(ps[:, 3 * w, cols], gamma[:, t, col:col + 1].broadcast_to([P, P]), SQ(m), start=True, stop=True)
                                mm = nc.tensor.matmul(ps[:, 3 * w + 1, cols], k_t[:, h0 + q, tok], k_t[:, h0 + q, tok], start=True, stop=True)
                                if latent:
                                    mm = nc.tensor.matmul(ps[:, 3 * w + 2, cols], k_t[:, h0 + q, tok], q_t[:, h0 + q, tok], start=True, stop=True)
                            mm.then_inc(rows_done, 1)
                        for w in range(2):
                            pe.wait_ge(strict_done, 2 * pp(pair) + w + 1)
                            for q in range(4):
                                mm = nc.tensor.transpose(ps[:, 3 * w, q * P:(q + 1) * P], nb[:, w, 0, q * P:(q + 1) * P], SQ("identity"))
                            mm.then_inc(square_done, 1)
                        for l in range(1, 7):
                            for w in range(2):
                                pe.wait_ge(b_kept, 14 * pp(pair) + 2 * (l - 1) + w + 1)
                                if l > 1:
                                    pe.wait_ge(n_kept, 10 * pp(pair) + 2 * (l - 2) + w + 1)
                                for q in range(4):
                                    cols = slice(q * P, (q + 1) * P)
                                    mm = nc.tensor.matmul(ps[:, 3 * w + 1, cols], nb[:, w, 0, cols], nb[:, w, 1, cols], start=True, stop=True)
                                    if l < 6:
                                        mm = nc.tensor.matmul(ps[:, 3 * w, cols], nb[:, w, 1, cols], nb[:, w, 0, cols], start=True, stop=True)
                                mm.then_inc(square_done, 1)
                            for w in range(2):
                                zq = 2 * pair + w
                                pe.wait_ge(b_kept, 14 * pp(pair) + 2 * l + w + 1)
                                if l > 1:
                                    pe.wait_ge(z_done, 12 * pp(pair) + 2 * (l - 2) + w + 1)
                                for q in range(4):
                                    cols = slice(q * P, (q + 1) * P)
                                    mm = nc.tensor.matmul(ps[:, 3 * w + 2, cols], nb[:, w, 1, cols], z[:, zq, cols], start=True, stop=True)
                                mm.then_inc(z_step_done, 1)

                @block.scalar
                def _(act):
                    for pair in range(2):
                        for w in range(2):
                            zq = 2 * pair + w
                            act.wait_ge(gap_done, 2 * pp(pair) + w + 1)
                            nc.scalar.activation(qa[:, zq], qa[:, zq], ACT.Exp).then_inc(gap_exp_done, 1)
                        for w in range(2):
                            act.wait_ge(square_done, 14 * pp(pair) + w + 1)
                            nc.scalar.activation(nb[:, w, 1], ps[:, 3 * w, :], ACT.Copy).then_inc(b_kept, 1)
                        for l in range(1, 7):
                            for w in range(2):
                                act.wait_ge(square_done, 14 * pp(pair) + 2 * l + w + 1)
                                nc.scalar.activation(nb[:, w, 1], ps[:, 3 * w + 1, :], ACT.Copy).then_inc(b_kept, 1)

                @block.gpsimd
                def _(pool):
                    for pair in range(2):
                        for w in range(2):
                            zq, d, t, h0 = quad(pair, w)
                            pool.wait_ge(n_done, 2 * pp(pair) + w + 1)
                            strict = SQ("strict_upper" if d == 0 else "strict_lower").unsqueeze(1).broadcast_to([P, 4, P])
                            r4 = lambda x: x.rearrange("p (q n) -> p q n", q=4)
                            pool_done.mark(nc.gpsimd.tensor_tensor(r4(nb[:, w, 0]), r4(nb[:, w, 0]), strict, ALU.mult))
                            settle(pool, pool_done)
                            nc.gpsimd.tensor_tensor(r4(z[:, zq]), SQ("identity").unsqueeze(1).broadcast_to([P, 4, P]),
                                                    r4(nb[:, w, 0]), ALU.subtract).then_inc(strict_done, 1)

                @block.vector
                def _(dve):
                    for pair in range(2):
                        for w in range(2):
                            zq, d, t, h0 = quad(pair, w)
                            dve.wait_ge(rows_done, 2 * pp(pair) + w + 1)
                            mask = SQ("mask_before" if d == 0 else "mask_after")
                            for q in range(4):
                                col = 8 * d + h0 + q
                                cols = slice(q * P, (q + 1) * P)
                                ins = nc.vector.scalar_tensor_tensor(out=qa[:, zq, cols], in0=ps[:, 3 * w, cols], scalar=g_cum[:, t, col:col + 1],
                                                                     in1=mask, op0=ALU.subtract, op1=ALU.add)
                                if q < 3:
                                    dve_done.mark(ins)
                            ins.then_inc(gap_done, 1)
                        for w in range(2):
                            zq, d, t, h0 = quad(pair, w)
                            dve.wait_ge(gap_exp_done, 2 * pp(pair) + w + 1)
                            for q in range(4):
                                col = 8 * d + h0 + q
                                cols = slice(q * P, (q + 1) * P)
                                dve_done.mark(nc.vector.scalar_tensor_tensor(
                                    out=nb[:, w, 0, cols], in0=ps[:, 3 * w + 1, cols], scalar=beta[:, t, col:col + 1],
                                    in1=qa[:, zq, cols], op0=ALU.mult, op1=ALU.mult))
                            settle(dve, dve_done)
                            src = ps[:, 3 * w + 2, :] if latent else qa[:, zq]
                            nc.vector.tensor_tensor(qa[:, zq], qa[:, zq], src, ALU.mult).then_inc(n_done, 1)
                        for l in range(1, 7):
                            if l < 6:
                                for w in range(2):
                                    dve.wait_ge(square_done, 14 * pp(pair) + 2 * l + w + 1)
                                    nc.vector.tensor_copy(nb[:, w, 0], ps[:, 3 * w, :]).then_inc(n_kept, 1)
                            for w in range(2):
                                zq = 2 * pair + w
                                dve.wait_ge(z_step_done, 12 * pp(pair) + 2 * (l - 1) + w + 1)
                                nc.vector.tensor_tensor(z[:, zq], z[:, zq], ps[:, 3 * w + 2, :], ALU.add).then_inc(z_done, 1)

        def delta_states(n, order, qa, z, work, s_all, k_t, q_t, kv_tok, o_tok, small):
            ks_done, rest_done, solved, v_new_done, v_decayed, own_done, own_added, o_s_done, s_next_done, s_kept, o_added = state_sems
            beta, neg_eg, eg, e_tot, e_gap = small
            latent = n >= 2
            last = n == 5
            u0 = 4 * n
            l0 = 4 * (n - 2)
            with nc.Block() as block:
                def quad(zq):
                    d = zq // 2
                    return d, order[d][n], 4 * (zq % 2)

                @block.tensor
                def _(pe):
                    def old_state(zq):
                        d, t, h0 = quad(zq)
                        if zq >= 2:
                            pe.wait_ge(rest_done, u0 + zq - 1)
                        for q in range(4):
                            s = s_all[:, d, (h0 + q) * P:(h0 + q + 1) * P]
                            mm = nc.tensor.matmul(ps[:, zq % 2, q * P:(q + 1) * P], k_t[:, h0 + q, t * P:(t + 1) * P], s, start=True, stop=True)
                        mm.then_inc(ks_done, 1)
                        if latent:
                            if zq >= 1:
                                pe.wait_ge(o_added, l0 + zq)
                            for q in range(4):
                                s = s_all[:, d, (h0 + q) * P:(h0 + q + 1) * P]
                                mm = nc.tensor.matmul(ps[:, 4, q * P:(q + 1) * P], q_t[:, h0 + q, t * P:(t + 1) * P], s, start=True, stop=True)
                            mm.then_inc(o_s_done, 1)

                    def solve(zq):
                        pe.wait_ge(rest_done, u0 + zq + 1)
                        if zq >= 2:
                            pe.wait_ge(v_new_done, u0 + zq - 1)
                        for q in range(4):
                            cols = slice(q * P, (q + 1) * P)
                            mm = nc.tensor.matmul(ps[:, 2 + zq % 2, cols], z[:, zq, cols], work[:, zq % 2, 0, cols], start=True, stop=True)
                        mm.then_inc(solved, 1)

                    def new_state(zq):
                        d, t, h0 = quad(zq)
                        if latent:
                            pe.wait_ge(v_new_done, u0 + zq + 1)
                            if zq >= 1:
                                pe.wait_ge(own_added, l0 + zq)
                            for q in range(4):
                                cols = slice(q * P, (q + 1) * P)
                                mm = nc.tensor.matmul(ps[:, 5, cols], qa[:, zq, cols], work[:, zq % 2, 0, cols], start=True, stop=True)
                            mm.then_inc(own_done, 1)
                        if not last:
                            pe.wait_ge(v_decayed, u0 + zq + 1)
                            if zq >= 2:
                                pe.wait_ge(s_kept, u0 + zq - 1)
                            for q in range(4):
                                cols = slice(q * P, (q + 1) * P)
                                mm = nc.tensor.matmul(ps[:, 6 + zq % 2, cols], kv_tok[:, t, (h0 + q) * P:(h0 + q + 1) * P],
                                                      work[:, zq % 2, 1, cols], start=True, stop=True)
                            mm.then_inc(s_next_done, 1)

                    for s in range(6):
                        if s < 4:
                            old_state(s)
                        if 1 <= s <= 4:
                            solve(s - 1)
                        if s >= 2:
                            new_state(s - 2)

                @block.gpsimd
                def _(pool):
                    if last:
                        return
                    for zq in range(4):
                        d, t, h0 = quad(zq)
                        pool.wait_ge(v_new_done, u0 + zq + 1)
                        if zq >= 2:
                            pool.wait_ge(s_next_done, u0 + zq - 1)
                        nc.gpsimd.tensor_tensor(
                            work[:, zq % 2, 1].rearrange("p (q n) -> p q n", q=4), work[:, zq % 2, 0].rearrange("p (q n) -> p q n", q=4),
                            e_gap[:, t, 8 * d + h0:8 * d + h0 + 4].unsqueeze(2).broadcast_to([P, 4, P]), ALU.mult).then_inc(v_decayed, 1)

                @block.vector
                def _(dve):
                    def rest(zq):
                        d, t, h0 = quad(zq)
                        dve.wait_ge(ks_done, u0 + zq + 1)
                        if zq >= 2:
                            if latent:
                                dve.wait_ge(own_done, l0 + zq - 1)
                            if not last:
                                dve.wait_ge(v_decayed, u0 + zq - 1)
                        for q in range(4):
                            cols = slice(q * P, (q + 1) * P)
                            col = 8 * d + h0 + q
                            ins = nc.vector.scalar_tensor_tensor(
                                out=work[:, zq % 2, 0, cols], in0=ps[:, zq % 2, cols], scalar=neg_eg[:, t, col:col + 1],
                                in1=kv_tok[:, t, D + (h0 + q) * P:D + (h0 + q + 1) * P], op0=ALU.mult, op1=ALU.add)
                            if q < 3:
                                dve_done.mark(ins)
                        ins.then_inc(rest_done, 1)
                        if latent:
                            dve.wait_ge(o_s_done, l0 + zq + 1)
                            for q in range(4):
                                col = 8 * d + h0 + q
                                o = o_tok[:, t, (h0 + q) * P:(h0 + q + 1) * P]
                                ins = nc.vector.scalar_tensor_tensor(out=o, in0=ps[:, 4, q * P:(q + 1) * P], scalar=eg[:, t, col:col + 1],
                                                                     in1=o, op0=ALU.mult, op1=ALU.add)
                                if q < 3:
                                    dve_done.mark(ins)
                            ins.then_inc(o_added, 1)

                    def fresh(zq):
                        d, t, h0 = quad(zq)
                        dve.wait_ge(solved, u0 + zq + 1)
                        nc.vector.tensor_tensor(
                            work[:, zq % 2, 0].rearrange("p (q n) -> p q n", q=4), ps[:, 2 + zq % 2, :].rearrange("p (q n) -> p q n", q=4),
                            beta[:, t, 8 * d + h0:8 * d + h0 + 4].unsqueeze(2).broadcast_to([P, 4, P]), ALU.mult).then_inc(v_new_done, 1)

                    def add(zq):
                        d, t, h0 = quad(zq)
                        if latent:
                            dve.wait_ge(own_done, l0 + zq + 1)
                            dve.wait_ge(o_added, l0 + zq + 1)
                            o = o_tok[:, t, h0 * P:(h0 + 4) * P]
                            nc.vector.tensor_tensor(o, o, ps[:, 5, :], ALU.add).then_inc(own_added, 1)
                        if not last:
                            dve.wait_ge(s_next_done, u0 + zq + 1)
                            for q in range(4):
                                col = 8 * d + h0 + q
                                s = s_all[:, d, (h0 + q) * P:(h0 + q + 1) * P]
                                ins = nc.vector.scalar_tensor_tensor(out=s, in0=s, scalar=e_tot[:, t, col:col + 1],
                                                                     in1=ps[:, 6 + zq % 2, q * P:(q + 1) * P], op0=ALU.mult, op1=ALU.add)
                                if q < 3:
                                    dve_done.mark(ins)
                            ins.then_inc(s_kept, 1)

                    for s in range(6):
                        if s < 4:
                            rest(s)
                        if 1 <= s <= 4:
                            fresh(s - 1)
                        if s >= 2:
                            add(s - 2)

        def deltanet():
            x_words = x_all.rearrange("p a k n -> p (a k n)").bitcast(F32)
            o_tok = x_words[:, 0:4096].rearrange("p (t n) -> p t n", t=LB)
            s_all = x_words[:, 4096:6144].rearrange("p (d n) -> p d n", d=2)
            rows_kv = [(64 * r, 64) for r in range(8)]
            with ExitStack() as local:
                kv_tok = sb("kv_tok", [P, TB, 2 * D], F32, local)
                small_all = sb("small_all", [P, 8, TB, 16], F32, local)
                beta, gamma, g_cum, g_tot, eg, neg_eg, e_tot, e_gap = (small_all[:, i] for i in range(8))
                ba = sb("ba", [P, TB, 32], F32, local)
                ba_rows = sb("ba_rows", [P, 32], F32, local)
                sums = sb("sums", [P, TB, DH], F32, local)

                def project(name, target, chunk0, segments, rows):
                    layout, width = pad_layout(rows)
                    with ExitStack() as inner:
                        pad = sb(name + "_pad", [P, width], F32, inner)
                        acc = sb(name + "_acc", [P, width], F32, inner)
                        zero_pad(pad[:])
                        linear(name, *x_parts(x_hi, x_lo), segments,
                               convolve(pad, acc, target, layout, width, "dn_conv_w", 24, chunk0, None),
                               per_conv(len(segments)))

                with ExitStack() as inner:
                    v_t = sb("v_t", [P, DH, TOK], F32, inner)
                    project("dn_v", v_t, 16, BOTH, rows_kv + [(LAT, CTX)])
                    silu_and_turn(v_t, DH, kv_tok[:, :, D:], DH)
                k_t = sb("k_t", [P, DH, TOK], F32, local)
                project("dn_k", k_t, 8, BOTH, rows_kv + [(LAT, CTX)])
                silu_and_turn(k_t, DH, kv_tok[:, :, 0:D], DH)
                flat = scratch.rearrange("p a n -> p (a n)")
                square = flat[:, 0:D]
                unit_rows(kv_tok[:, :, 0:D], TB, square, sums, 1.0)
                turn_back(kv_tok[:, :, 0:D], TB, k_t)
                q_t = sb("q_t", [P, DH, LAT], F32, local)
                linear("dn_gate", *x_parts(x_hi, x_lo), LATENT, keep_chunk(q_t, LAT), 0)
                load_and_wait([(gate_store, q_t[:])])
                project("dn_q", q_t, 0, LATENT, rows_kv)
                with ExitStack() as inner:
                    q_tok = sb("q_tok", [P, LB, D], F32, inner)
                    silu_and_turn_latent(q_t, q_tok)
                    unit_rows(q_tok[:], LB, square, sums, P ** -0.5)
                    turn_back(q_tok, LB, q_t)
                wf = flat[:, 0:256].rearrange("p (k n) -> p k n", k=KC)
                wh = flat[:, 256:384].bitcast(BF16).rearrange("p (k n) -> p k n", k=KC)
                wl = flat[:, 384:512].bitcast(BF16).rearrange("p (k n) -> p k n", k=KC)
                small_product(ext["ba_w"], 32, wf, wh, wl, ba[:])
                load_and_wait([(ba_rows[:], ext["ba_rows"])])
                a0 = act_done.n
                with nc.Block() as block:
                    @block.scalar
                    def _(act):
                        act_done.mark(nc.scalar.activation(beta, ba[:, :, 0:16], ACT.Sigmoid))
                        act_done.mark(nc.scalar.activation(ba_rows[:, 16:32], ba_rows[:, 16:32], ACT.Exp))

                    @block.vector
                    def _(dve):
                        dve_done.mark(nc.vector.tensor_tensor(gamma, ba[:, :, 16:32], ba_rows[:, 0:16].unsqueeze(1).broadcast_to([P, TB, 16]), ALU.add))
                        dve.wait_ge(act_done.sem, a0 + 2)
                        dve_done.mark(nc.vector.tensor_scalar(ba_rows[:, 16:32], ba_rows[:, 16:32], -1.0, None, ALU.mult))
                softplus(gamma, [flat[:, 96 * q:96 * q + 96].rearrange("p (t n) -> p t n", n=16) for q in range(4)])
                p0, d0 = pe_done.n, dve_done.n
                with nc.Block() as block:
                    @block.vector
                    def _(dve):
                        dve_done.mark(nc.vector.tensor_tensor(gamma, gamma, ba_rows[:, 16:32].unsqueeze(1).broadcast_to([P, TB, 16]), ALU.mult))
                        dve.wait_ge(pe_done.sem, p0 + 1)
                        dve_done.mark(nc.vector.tensor_copy(g_cum, ps[:, 0, 0:96].rearrange("p (t n) -> p t n", n=16)))
                        dve_done.mark(nc.vector.tensor_copy(g_tot, ps[:, 1, 0:96].rearrange("p (t n) -> p t n", n=16)))
                        settle(dve, dve_done)
                        dve_done.mark(nc.vector.tensor_tensor(e_gap, g_tot, g_cum, ALU.subtract))
                        dve_done.mark(nc.vector.memset(o_tok, 0.0))
                        dve_done.mark(nc.vector.memset(s_all, 0.0))

                    @block.tensor
                    def _(pe):
                        pe.wait_ge(dve_done.sem, d0 + 1)
                        for t in range(TB):
                            for d, m in enumerate(("sum_upto", "sum_from")):
                                nc.tensor.matmul(ps[:, 0, t * 16 + 8 * d:t * 16 + 8 * d + 8], SQ(m), gamma[:, t, 8 * d:8 * d + 8], start=True, stop=True)
                        pe_done.mark(nc.tensor.matmul(ps[:, 1, 0:96], SQ("ones"), gamma.rearrange("p t n -> p (t n)"), start=True, stop=True))
                a0 = act_done.n
                with nc.Block() as block:
                    @block.scalar
                    def _(act):
                        act_done.mark(nc.scalar.activation(eg, g_cum, ACT.Exp))
                        act_done.mark(nc.scalar.activation(e_tot, g_tot, ACT.Exp))
                        act_done.mark(nc.scalar.activation(e_gap, e_gap, ACT.Exp))

                    @block.vector
                    def _(dve):
                        dve.wait_ge(act_done.sem, a0 + 1)
                        dve_done.mark(nc.vector.tensor_scalar(neg_eg, eg, -1.0, None, ALU.mult))

                qa = sb("qa", [P, 4, BANK], F32, local)
                z = sb("z_inv", [P, 4, BANK], F32, local)
                nb = w_hi.rearrange("p r n -> p (r n)").bitcast(F32).rearrange("p (w a n) -> p w a n", w=2, a=2)
                work = w_lo.rearrange("p r n -> p (r n)").bitcast(F32).rearrange("p (w a n) -> p w a n", w=2, a=2)
                order = ((4, 5, 0, 1, 2, 3), (5, 4, 3, 2, 1, 0))
                for n in range(6):
                    delta_inverse(n, order, qa, z, nb, k_t, q_t, gamma, beta, g_cum)
                    delta_states(n, order, qa, z, work, s_all, k_t, q_t, kv_tok, o_tok, (beta, neg_eg, eg, e_tot, e_gap))
            with ExitStack() as local:
                gate = sb("gate", [P, KC, LAT], F32, local)
                o_t = sb("o_t", [P, KC, LAT], F32, local)
                sums = sb("sums2", [P, LB, DH], F32, local)
                flat = scratch.rearrange("p a n -> p (a n)")
                rms_rows(o_tok, flat[:, 0:D], sums)
                load_and_wait([(gate[:], gate_store)])
                turn_back(o_tok, LB, o_t)
                a0, d0 = act_done.n, dve_done.n
                with nc.Block() as block:
                    @block.scalar
                    def _(act):
                        act_done.mark(nc.scalar.activation(gate[:], gate[:], ACT.Silu))
                        for k in range(KC):
                            act.wait_ge(dve_done.sem, d0 + 2 * k + 1)
                            act_done.mark(nc.scalar.activation(x_hi[:, k, 0:LAT], o_t[:, k], ACT.Copy))

                    @block.vector
                    def _(dve):
                        dve.wait_ge(act_done.sem, a0 + 1)
                        for k in range(KC):
                            dve_done.mark(nc.vector.scalar_tensor_tensor(out=o_t[:, k], in0=o_t[:, k], scalar=V("dn_norm_g"),
                                                                         in1=gate[:, k], op0=ALU.mult, op1=ALU.mult))
                            dve.wait_ge(act_done.sem, a0 + k + 2)
                            dve_done.mark(nc.vector.tensor_tensor(x_lo[:, k, 0:LAT], o_t[:, k], x_hi[:, k, 0:LAT], ALU.subtract))
            linear("dn_out", *x_parts(x_hi, x_lo), LATENT, add_to_residual(2, 2, LATENT, mods), 0)

        def rms_rows(tok, square, sums):
            a0, d0 = act_done.n, dve_done.n
            with nc.Block() as block:
                @block.vector
                def _(dve):
                    for t in range(LB):
                        settle(dve, dve_done)
                        dve_done.mark(nc.vector.tensor_tensor(square, tok[:, t], tok[:, t], ALU.mult))
                        settle(dve, dve_done)
                        dve_done.mark(nc.vector.tensor_reduce(sums[:, t], square.rearrange("p (h d) -> p h d", d=P), AX.X, ALU.add))
                    settle(dve, dve_done)
                    dve_done.mark(nc.vector.tensor_scalar(sums[:], sums[:], 1.0 / P, EPS, ALU.mult, ALU.add))
                    dve.wait_ge(act_done.sem, a0 + 1)
                    dve_done.mark(nc.vector.reciprocal(sums[:], sums[:]))
                    settle(dve, dve_done)
                    for t in range(LB):
                        r3 = tok[:, t].rearrange("p (h d) -> p h d", d=P)
                        dve_done.mark(nc.vector.tensor_tensor(r3, r3, sums[:, t].unsqueeze(2).broadcast_to([P, DH, P]), ALU.mult))

                @block.scalar
                def _(act):
                    act.wait_ge(dve_done.sem, d0 + 2 * LB + 1)
                    act_done.mark(nc.scalar.activation(sums[:], sums[:], ACT.Sqrt))

        def silu_and_turn_latent(source, target):
            a0, p0, d0 = act_done.n, pe_done.n, dve_done.n
            with nc.Block() as block:
                @block.scalar
                def _(act):
                    for c in range(DH):
                        act_done.mark(nc.scalar.activation(source[:, c, :], source[:, c, :], ACT.Silu))

                @block.tensor
                def _(pe):
                    for c in range(DH):
                        pe.wait_ge(act_done.sem, a0 + c + 1)
                        if c >= 4:
                            pe.wait_ge(dve_done.sem, d0 + c - 3)
                        for t in range(LB):
                            mm = nc.tensor.transpose(ps[:, c % 4, t * P:(t + 1) * P], source[:, c, t * P:(t + 1) * P], SQ("identity"))
                        pe_done.mark(mm)

                @block.vector
                def _(dve):
                    for c in range(DH):
                        dve.wait_ge(pe_done.sem, p0 + c + 1)
                        dve_done.mark(nc.vector.tensor_copy(target[:, :, c * P:(c + 1) * P], ps[:, c % 4, :].rearrange("p (t n) -> p t n", n=P)))

        def peer():
            with ExitStack() as local:
                normed = sb("normed2", [P, KC, LAT], F32, local)
                normalise(LAT, EPS, False, "norm_g1", None, normed)
                modulate_parts(2, 3, LAT, lambda k, lo, w: normed[:, k, lo:lo + w])
            with ExitStack() as local:
                picks = sb("picks", [P, 3, LAT], F32, local)
                with ExitStack() as inner:
                    s_tok = sb("s_tok", [P, LB, 2 * DH, P], F32, inner)
                    with ExitStack() as product:
                        keys = sb("keys", [P, 2 * DH, P], F32, product)
                        q_t = sb("pq_t", [P, 2 * DH, LAT], F32, product)
                        load_and_wait([(keys[:], ext["keys"].rearrange("d h p k -> d (h p) k"))])
                        linear("w_q", *x_parts(x_hi, x_lo), LATENT, keep_chunk(q_t, LAT), 0)
                        p0, a0 = pe_done.n, act_done.n
                        groups = [(t, c) for t in range(LB) for c in range(0, 16, 4)]
                        with nc.Block() as block:
                            @block.tensor
                            def _(pe):
                                for g, (t, c) in enumerate(groups):
                                    if g >= 4:
                                        pe.wait_ge(act_done.sem, a0 + g - 3)
                                    for q in range(4):
                                        mm = nc.tensor.matmul(ps[:, g % 4, q * P:(q + 1) * P], q_t[:, c + q, t * P:(t + 1) * P],
                                                              keys[:, c + q, :], start=True, stop=True)
                                    pe_done.mark(mm)

                            @block.scalar
                            def _(act):
                                for g, (t, c) in enumerate(groups):
                                    act.wait_ge(pe_done.sem, p0 + g + 1)
                                    act_done.mark(nc.scalar.activation(s_tok[:, t, c:c + 4, :].rearrange("p c n -> p (c n)"),
                                                                       ps[:, g % 4, :], ACT.Copy))
                    choose(inner, s_tok, picks)
                spread_gates(local, picks)
            with ExitStack() as local:
                y_sum = sb("y_sum", [P, KC, LAT], F32, local)
                experts(y_sum)
                with nc.Block() as block:
                    @block.vector
                    def _(dve):
                        for k in range(KC):
                            dve_done.mark(nc.vector.scalar_tensor_tensor(out=h[:, k, 0:LAT], in0=y_sum[:, k], scalar=mods[:, 2, 5 * KC + k, 0:1],
                                                                         in1=h[:, k, 0:LAT], op0=ALU.mult, op1=ALU.add))
            with ExitStack() as local:
                result = sb("result", [P, KC, LAT], F32, local)
                normalise(LAT, EPS, False, "final_g", None, result)
                with nc.Block() as block:
                    @block.sync
                    def _(sp):
                        dma_done.mark(sp.dma_start(out.rearrange("k p t -> p k t"), result[:]), 16)
                        settle(sp, dma_done)

        def choose(stack, s_tok, picks):
            top = sb("top16", [P, 2 * DH, PICKS], F32, stack)
            at = sb("at16", [P, 2 * DH, PICKS], U32, stack)
            at_f = sb("at16f", [P, 2 * DH, PICKS], F32, stack)
            cand = sb("cand", [P, DH, PICKS * PICKS], F32, stack)
            best = sb("best", [P, DH, PICKS], F32, stack)
            pos = sb("pos", [P, DH, PICKS], U32, stack)
            half = sb("half", [P, 2, DH, PICKS], U32, stack)
            half_f = sb("half_f", [P, 2, DH, PICKS], F32, stack)
            eq = sb("eq", [P, DH, PICKS, PICKS], F32, stack)
            three = sb("three", [P, LB, 3, P], F32, stack)
            total = sb("total", [P, DH], F32, stack)
            a0, d0, p0 = act_done.n, dve_done.n, pe_done.n
            exps = []
            with nc.Block() as block:
                @block.vector
                def _(dve):
                    def top16(values, n, out_v, out_i):
                        for lo in (0, 8):
                            for c in range(n):
                                dve_done.mark(nc.vector.max(out_v[:, c, lo:lo + 8], values[:, c, :]))
                            settle(dve, dve_done)
                            for c in range(n):
                                dve_done.mark(nc.vector.max_index(out_i[:, c, lo:lo + 8], out_v[:, c, lo:lo + 8], values[:, c, :]))
                            settle(dve, dve_done)
                            if lo == 0:
                                for c in range(n):
                                    dve_done.mark(nc.vector.match_replace(values[:, c, :], out_v[:, c, 0:8], values[:, c, :], -3e38))
                                settle(dve, dve_done)

                    for t in range(LB):
                        top16(s_tok[:, t], 2 * DH, top, at)
                        dve_done.mark(nc.vector.tensor_copy(at_f[:], at[:]))
                        by_head = top.rearrange("p (h s) j -> p h s j", s=2)
                        dve_done.mark(nc.vector.tensor_tensor(
                            cand.rearrange("p h (a b) -> p h a b", a=PICKS),
                            by_head[:, :, 0, :].unsqueeze(3).broadcast_to([P, DH, PICKS, PICKS]),
                            by_head[:, :, 1, :].unsqueeze(2).broadcast_to([P, DH, PICKS, PICKS]), ALU.add))
                        settle(dve, dve_done)
                        top16(cand, DH, best, pos)
                        g = three[:, t, 2].rearrange("p (h j) -> p h j", h=DH)
                        dve_done.mark(nc.vector.tensor_tensor(g, best[:], best[:, :, 0:1].broadcast_to([P, DH, PICKS]), ALU.subtract))
                        exps.append(dve_done.n)
                        dve_done.mark(nc.vector.tensor_scalar(half[:, 0], pos[:], 4, None, ALU.logical_shift_right))
                        dve_done.mark(nc.vector.tensor_scalar(half[:, 1], pos[:], 15, None, ALU.bitwise_and))
                        settle(dve, dve_done)
                        dve_done.mark(nc.vector.tensor_copy(half_f[:], half[:]))
                        settle(dve, dve_done)
                        for s in range(2):
                            dve_done.mark(nc.vector.tensor_tensor(
                                eq[:], half_f[:, s].unsqueeze(3).broadcast_to([P, DH, PICKS, PICKS]),
                                SQ("iota")[:, 0:PICKS].unsqueeze(1).unsqueeze(1).broadcast_to([P, DH, PICKS, PICKS]), ALU.is_equal))
                            settle(dve, dve_done)
                            dve_done.mark(nc.vector.tensor_tensor(
                                eq[:], eq[:], at_f.rearrange("p (h s) j -> p h s j", s=2)[:, :, s, :].unsqueeze(2).broadcast_to(
                                    [P, DH, PICKS, PICKS]), ALU.mult))
                            settle(dve, dve_done)
                            dve_done.mark(nc.vector.tensor_reduce(three[:, t, s].rearrange("p (h j) -> p h j", h=DH), eq[:], AX.X, ALU.add))
                            settle(dve, dve_done)
                        dve.wait_ge(act_done.sem, a0 + t + 1)
                        dve_done.mark(nc.vector.tensor_reduce(total[:], g, AX.X, ALU.add))
                        settle(dve, dve_done)
                        dve_done.mark(nc.vector.reciprocal(total[:], total[:]))
                        settle(dve, dve_done)
                        dve_done.mark(nc.vector.tensor_tensor(g, g, total[:].unsqueeze(2).broadcast_to([P, DH, PICKS]), ALU.mult))
                        settle(dve, dve_done)

                @block.scalar
                def _(act):
                    for t in range(LB):
                        act.wait_ge(dve_done.sem, exps[t])
                        act_done.mark(nc.scalar.activation(three[:, t, 2], three[:, t, 2], ACT.Exp))

            d1 = dve_done.n
            with nc.Block() as block:
                @block.tensor
                def _(pe):
                    for s in range(3):
                        for t in range(LB):
                            mm = nc.tensor.transpose(ps[:, s, t * P:(t + 1) * P], three[:, t, s, :], SQ("identity"))
                        pe_done.mark(mm)

                @block.vector
                def _(dve):
                    for s in range(3):
                        dve.wait_ge(pe_done.sem, p0 + s + 1)
                        dve_done.mark(nc.vector.tensor_copy(picks[:, s, :], ps[:, s, :]))

        def spread_gates(stack, picks):
            onehot_ready, onehot_free, bank_free, *stored = (
                sem(n) for n in ("onehot_ready", "onehot_free", "gate_bank_free", "gates_stored0", "gates_stored1"))
            k1_hot = sb("k1_hot", [P, 16, P], F32, stack)
            k2_hot = sb("k2_hot", [P, 16, P], F32, stack)
            dense = [sb(f"dense{b}", [P, P, BLOCK], F32, stack) for b in range(2)]
            per = 2 * BLOCK // 4
            bodies = LAT // (2 * BLOCK)
            with nc.Block() as block:
                @block.vector
                def _(dve):
                    nc.vector.memset(k1_hot[:, 0, 0:1], 0.0).then_inc(onehot_free, 4)
                    nc.vector.memset(k1_hot[:, 1, 0:1], 0.0).then_inc(bank_free, 4)
                    for b in range(2):
                        nc.vector.memset(k1_hot[:, 2 + b, 0:1], 0.0).then_inc(stored[b], 16)
            with nc.Block() as block:
                @block.vector
                def _(dve):
                    with dve.Fori(0, bodies) as i:
                        for g in range(per):
                            slot, t0 = 4 * (g % 4), i * (2 * BLOCK) + 4 * g
                            dve.wait_ge(onehot_free, i * per + (g + 1))
                            nc.vector.tensor_tensor(k1_hot[:, slot:slot + 4, :], SQ("iota").unsqueeze(1).broadcast_to([P, 4, P]),
                                                    picks[:, 0, bass.ds(t0, 4)].unsqueeze(2).broadcast_to([P, 4, P]),
                                                    ALU.is_equal).then_inc(onehot_ready, 1)
                            for q in range(4):
                                t = i * (2 * BLOCK) + (4 * g + q)
                                nc.vector.tensor_scalar(k2_hot[:, slot + q, :], SQ("iota"), picks[:, 1, bass.ds(t, 1)],
                                                        picks[:, 2, bass.ds(t, 1)], ALU.is_equal, ALU.mult).then_inc(onehot_ready, 1)

                @block.tensor
                def _(pe):
                    with pe.Fori(0, bodies) as i:
                        for g in range(per):
                            pe.wait_ge(onehot_ready, i * (per * 5) + (g * 5 + 5))
                            pe.wait_ge(bank_free, i * per + (g + 1))
                            for q in range(4):
                                mm = nc.tensor.matmul(ps[:, g % 4, q * P:(q + 1) * P], k1_hot[:, 4 * (g % 4) + q, :],
                                                      k2_hot[:, 4 * (g % 4) + q, :], start=True, stop=True)
                            mm.then_inc(onehot_free, 1)

                @block.scalar
                def _(act):
                    with act.Fori(0, bodies) as i:
                        for g in range(per):
                            b, at = g // (per // 2), g % (per // 2)
                            if at == 0:
                                act.wait_ge(stored[b], i * 16 + 16)
                            act.wait_ge(onehot_free, i * per + (g + 5))
                            nc.scalar.activation(dense[b][:, :, 4 * at:4 * at + 4], ps[:, g % 4, :].rearrange("p (t k) -> p k t", t=4),
                                                 ACT.Copy).then_inc(bank_free, 1)

                @block.sync
                def _(sp):
                    with sp.Fori(0, bodies) as i:
                        for b in range(2):
                            sp.wait_ge(bank_free, i * per + (4 + (b + 1) * (per // 2)))
                            sp.dma_start(expert_gates[i * 2 + b], dense[b][:]).then_inc(stored[b], 16)
                    for b in range(2):
                        sp.wait_ge(stored[b], 16 + 16 * bodies)

        def experts(y_sum):
            base = starts["experts"]
            n_groups = EXPERT_TILES // GROUP
            v_ready = [sem(f"v_ready{j}") for j in range(GROUP)]
            gates_ready = [sem(f"gates_ready{b}") for b in range(2)]
            v_hi_done, v_split, gelu_done, weighed, coef_hi_done, coef_done, y_done, y_added = (
                sem(n) for n in ("v_hi_done", "v_split", "gelu_done", "weighed", "coef_hi_done", "coef_done", "ey_done", "y_added"))
            with ExitStack() as local:
                v_raw = sb("v_raw", [P, GROUP, D], F32, local)
                v_hi = sb("v_hi", [P, GROUP, D], BF16, local)
                v_lo = sb("v_lo", [P, GROUP, D], BF16, local)
                c_hi = sb("c_hi", [P, 2, GROUP, LAT], BF16, local)
                c_lo = sb("c_lo", [P, 2, GROUP, LAT], BF16, local)
                hidden = sb("hidden", [P, 2, LAT], F32, local)
                gates = sb("gates_in", [P, 2, LAT // BLOCK, GROUP, BLOCK], F32, local)
                W = ext["weights"]
                with nc.Block() as block:
                    @block.vector
                    def _(dve):
                        dve_done.mark(nc.vector.memset(y_sum[:], 0.0))
                        nc.vector.memset(hidden[:, 0, 0:1], 0.0).then_inc(gelu_done, 4)
                        nc.vector.memset(hidden[:, 0, 1:2], 0.0).then_inc(coef_done, 2)
                        nc.vector.memset(hidden[:, 0, 2:3], 0.0).then_inc(y_done, 16)
                        nc.vector.memset(hidden[:, 0, 3:4], 0.0).then_inc(y_added, 4)

                with nc.Block() as block:
                    @block.sync
                    def _(sp):
                        def load_u(g):
                            for j in range(GROUP):
                                sp.wait_ge(split_done, (g - 1) * GROUP + (base + j + 1))
                                sp.dma_start(w_raw[:, j], W[g * (2 * GROUP) + (base + j)]).then_inc(raw_ready[j], 16)

                        def load_v(g):
                            for j in range(GROUP):
                                sp.dma_start(v_raw[:, j], W[g * (2 * GROUP) + (base + GROUP + j)]).then_inc(v_ready[j], 16)

                        def load_gates(g, b):
                            src = expert_gates[:, :, bass.ds(g * GROUP, GROUP), :].rearrange("n p k t -> p n (k t)")
                            sp.dma_start(gates[:, b].rearrange("p n k t -> p n (k t)"), src).then_inc(gates_ready[b], 16)

                        def ahead(g, b):
                            load_u(g + 1)
                            sp.wait_ge(coef_done, g * GROUP + 2)
                            load_gates(g + 1, 1 - b)
                            for j in range(GROUP):
                                sp.wait_ge(v_split, g * GROUP + (j + 1))
                                sp.dma_start(v_raw[:, j], W[g * (2 * GROUP) + (base + 3 * GROUP + j)]).then_inc(v_ready[j], 16)

                        load_gates(0, 0)
                        load_v(0)
                        with sp.Fori(0, n_groups // 2 - 1) as i:
                            for b in range(2):
                                ahead(i * 2 + b, b)
                        ahead(n_groups - 2, 0)

                    @block.scalar
                    def _(act):
                        def high_u(g, j):
                            act.wait_ge(raw_ready[j], g * 16 + 16 * (base // RING + 1))
                            act.wait_ge(slot_free, g * GROUP + (base + j + 1))
                            nc.scalar.activation(w_hi[:, j], w_raw[:, j], ACT.Copy).then_inc(hi_done, 1)

                        def group(g, b, more=True):
                            for j in range(GROUP):
                                act.wait_ge(slot_free, g * GROUP + (base + RING + j + 1))
                                act.wait_ge(coef_done, g * GROUP + (j + 1))
                                nc.scalar.activation(hidden[:, j % 2], ps[:, j, :], ACT.Gelu).then_inc(gelu_done, 1)
                                if more:
                                    high_u(g + 1, j)
                                act.wait_ge(weighed, g * GROUP + (j + 1))
                                act.wait_ge(y_done, g * KC + 8)
                                nc.scalar.activation(c_hi[:, b, j], hidden[:, j % 2], ACT.Copy).then_inc(coef_hi_done, 1)
                            for j in range(GROUP):
                                act.wait_ge(v_ready[j], g * 16 + 16)
                                act.wait_ge(y_done, g * KC + 16)
                                nc.scalar.activation(v_hi[:, j], v_raw[:, j], ACT.Copy).then_inc(v_hi_done, 1)

                        for j in range(GROUP):
                            high_u(0, j)
                        with act.Fori(0, n_groups // 2 - 1) as i:
                            for b in range(2):
                                group(i * 2 + b, b)
                        group(n_groups - 2, 0)
                        group(n_groups - 1, 1, False)

                    @block.gpsimd
                    def _(pool):
                        def low_u(g):
                            for j in range(GROUP):
                                pool.wait_ge(hi_done, g * GROUP + (base + j + 1))
                                nc.gpsimd.tensor_tensor(w_lo[:, j], w_raw[:, j], w_hi[:, j], ALU.subtract).then_inc(split_done, 1)

                        def low_v(g):
                            for j in range(GROUP):
                                pool.wait_ge(v_hi_done, g * GROUP + (j + 1))
                                nc.gpsimd.tensor_tensor(v_lo[:, j], v_raw[:, j], v_hi[:, j], ALU.subtract).then_inc(v_split, 1)

                        low_u(0)
                        with pool.Fori(0, n_groups - 1) as i:
                            low_u(i + 1)
                            low_v(i)
                        low_v(n_groups - 1)

                    @block.tensor
                    def _(pe):
                        def up(g):
                            for j in range(GROUP):
                                pe.wait_ge(split_done, g * GROUP + (base + j + 1))
                                pe.wait_ge(gelu_done, g * GROUP + (j + 1))
                                for k in range(KC):
                                    for part, (w, x) in enumerate(((w_hi, x_hi), (w_hi, x_lo), (w_lo, x_hi))):
                                        mm = nc.tensor.matmul(ps[:, j, :], w[:, j, k * P:(k + 1) * P], x[:, k, 0:LAT],
                                                              start=(k == 0 and part == 0), stop=(k == KC - 1 and part == 2))
                                mm.then_inc(slot_free, 1)

                        def down(g, b):
                            pe.wait_ge(coef_done, g * GROUP + (2 + GROUP))
                            pe.wait_ge(v_split, g * GROUP + GROUP)
                            for k in range(KC):
                                pe.wait_ge(y_added, g * KC + (k + 1))
                                for j in range(GROUP):
                                    for part, (v, c) in enumerate(((v_hi, c_hi), (v_hi, c_lo), (v_lo, c_hi))):
                                        mm = nc.tensor.matmul(ps[:, 4 + k % 4, :], v[:, j, k * P:(k + 1) * P], c[:, b, j, :],
                                                              start=(j == 0 and part == 0), stop=(j == GROUP - 1 and part == 2))
                                mm.then_inc(y_done, 1)

                        up(0)
                        with pe.Fori(0, n_groups // 2 - 1) as i:
                            up(i * 2 + 1)
                            down(i * 2, 0)
                            up(i * 2 + 2)
                            down(i * 2 + 1, 1)
                        up(n_groups - 1)
                        down(n_groups - 2, 0)
                        down(n_groups - 1, 1)

                    @block.vector
                    def _(dve):
                        def weigh(g, b, pair):
                            for j in range(GROUP):
                                if j == 0:
                                    dve.wait_ge(gates_ready[b], pair * 16 + 16)
                                dve.wait_ge(gelu_done, g * GROUP + (j + 5))
                                r3 = hidden[:, j % 2].rearrange("p (n t) -> p n t", t=BLOCK)
                                nc.vector.tensor_tensor(r3, r3, gates[:, b, :, j, :], ALU.mult).then_inc(weighed, 1)
                                dve.wait_ge(coef_hi_done, g * GROUP + (j + 1))
                                nc.vector.tensor_tensor(c_lo[:, b, j], hidden[:, j % 2], c_hi[:, b, j], ALU.subtract).then_inc(coef_done, 1)

                        def add(g):
                            dve.wait_ge(y_added, g * KC + 4)
                            for k in range(KC):
                                dve.wait_ge(y_done, g * KC + (17 + k))
                                nc.vector.tensor_tensor(y_sum[:, k], y_sum[:, k], ps[:, 4 + k % 4, :], ALU.add).then_inc(y_added, 1)

                        weigh(0, 0, 0)
                        with dve.Fori(0, n_groups // 2 - 1) as i:
                            weigh(i * 2 + 1, 1, i)
                            add(i * 2)
                            weigh(i * 2 + 2, 0, i + 1)
                            add(i * 2 + 1)
                        weigh(n_groups - 1, 1, n_groups // 2 - 1)
                        add(n_groups - 2)
                        add(n_groups - 1)

        def first_block():
            modulate_parts(0, 0, TOK)
            attention()
            normalise(TOK, LN_EPS / ALPHA ** 2, True, "mix_g0", "mix_b0")
            modulate_parts(0, 3, TOK)
            mlp(0, TOK)
            normalise(TOK, LN_EPS / ALPHA ** 2, True, "ff_g0", "ff_b0")
            modulate_parts(1, 0, TOK)
            with ExitStack() as outer:
                y_tok = sb("x_tok", [P, TB, SINNER], F32, outer)
                with ExitStack() as local:
                    ssm(y_tok, local)
                modulate_parts(1, 0, LAT)
                ssm_finish(y_tok)
            normalise(LAT, LN_EPS / ALPHA ** 2, True, "mix_g1", "mix_b1")
            modulate_parts(1, 3, LAT)
            mlp(1, LAT)
            normalise(LAT, LN_EPS / ALPHA ** 2, True, "ff_g1", "ff_b1")

        def second_block():
            load_and_wait([(h[:, :, LAT:TOK], ext["context2"])])
            with ExitStack() as local:
                normed = sb("normed", [P, KC, TOK], F32, local)
                normalise(TOK, EPS, False, "norm_g0", None, normed)
                modulate_parts(2, 0, TOK, lambda k, lo, w: normed[:, k, lo:lo + w])
            deltanet()
            peer()

        first_block()
        second_block()


def constants():
    import numpy as np
    i = np.arange(P)
    row, col = i[:, None], i[None, :]
    swap = (i // 32) * 32 + (i % 32 + 16) % 32
    table = {
        "identity": row == col, "ones": row * 0 + col * 0 + 1.0, "mean": np.full((P, P), 1.0 / D),
        "rope_swap": row == swap[None, :],
        "mask_before": np.where(col >= row, 0.0, NEG),
        "mask_same": np.zeros((P, P)),
        "mask_after": np.where(col <= row, 0.0, NEG),
        "sum_upto": row <= col, "sum_from": row >= col,
        "strict_lower": row > col, "strict_upper": row < col,
        "group_mean": np.full((P, P), 1.0 / 512), "head_mean": np.full((P, P), 1.0 / P),
        "iota": row * 0 + col,
    }
    squares = np.stack([table[n].astype(np.float32) * np.ones((P, P), np.float32) for n in SQUARES], 1)
    pos = np.arange(LAT)
    inv = (10000.0 ** (-np.arange(0, 32, 2, dtype=np.float32) / 32)).astype(np.float32)
    d = i % 64
    where = np.where(d < 32, 1, 0)[:, None] * (pos // 64)[None, :] + np.where(d >= 32, 1, 0)[:, None] * (pos % 64)[None, :]
    angle = where.astype(np.float32) * inv[d % 16][:, None]
    sign = np.where(d % 32 < 16, -1.0, 1.0)[:, None]
    rope = np.stack([np.cos(angle), sign * np.sin(angle)], 1).astype(np.float32)
    return squares, rope


def head_order():
    return [4 * (2 * (j // 4) + f) + j % 4 for j in range(8) for f in range(2)]


def tiles_of(w):
    import numpy as np
    k, n = w.shape
    return np.ascontiguousarray(w.reshape(k // D, KC, P, n // P, P).transpose(3, 0, 2, 1, 4)).reshape(-1, P, D)


def layout(inputs):
    import numpy as np

    a = {k: np.asarray(v) for k, v in inputs.items()}
    heads = head_order()
    order = np.concatenate([np.arange(HD) + HD * q for q in heads])
    w_in = a["att_w_in"][0]
    att_in = np.concatenate([w_in[:, :D][:, order], w_in[:, D:]], 1)
    u = a["peer_u_2"].reshape(P, P, D)
    u_t = np.ascontiguousarray(u.transpose(1, 2, 0)).reshape(P, KC, P, P).transpose(0, 2, 1, 3).reshape(P, P, D)
    v_t = a["peer_v_2"].reshape(P, P, D).transpose(1, 0, 2)
    experts = np.stack([u_t.reshape(-1, GROUP, P, D), v_t.reshape(-1, GROUP, P, D)], 1).reshape(-1, P, D)
    ssm_in, dn_in = a["ssm_w_in"][0], a["dn_w_in_2"][0]
    stream = {
        "mod0": a["w_mod"][0], "mod1": a["w_mod"][1], "ada": a["ada_w_2"][0],
        "att_in": att_in, "att_out": a["att_w_out"][0][order], "ff1_0": a["ff_w1"][0], "ff2_0": a["ff_w2"][0],
        "ssm_z": ssm_in[:, :SINNER], "ssm_x": ssm_in[:, SINNER:2 * SINNER], "ssm_bc": ssm_in[:, 2 * SINNER:SINNER + SCONV],
        "ssm_out": a["ssm_w_out"][0],
        "ff1_1": a["ff_w1"][1], "ff2_1": a["ff_w2"][1], "dn_q": dn_in[:, :D], "dn_k": dn_in[:, D:2 * D], "dn_v": dn_in[:, 2 * D:3 * D],
        "dn_gate": dn_in[:, 3 * D:4 * D],
        "dn_out": a["dn_w_out_2"][0], "w_q": a["peer_w_q_2"][0],
    }
    weights = np.concatenate([tiles_of(stream[n]) for n, _, _ in STREAM] + [experts], 0)

    def cols(v):
        return np.asarray(v).reshape(-1, P).T

    vectors = {
        "c": a["c"], "c_ctx": a["c_ctx"], "c2": a["c_2"], "c2_ctx": a["c_ctx_2"],
        "b_mod0": a["b_mod"][0], "b_mod1": a["b_mod"][1], "b_ada": a["ada_b_2"],
        "mix_g0": a["ln_mix_g"][0], "mix_g1": a["ln_mix_g"][1], "mix_b0": a["ln_mix_b"][0], "mix_b1": a["ln_mix_b"][1],
        "ff_g0": a["ln_ff_g"][0], "ff_g1": a["ln_ff_g"][1], "ff_b0": a["ln_ff_b"][0], "ff_b1": a["ln_ff_b"][1],
        "norm_g0": a["norm_g_2"][0, 0], "norm_g1": a["norm_g_2"][0, 1], "final_g": a["final_g_2"],
        "conv_w": a["ssm_conv_w"][0], "conv_b": a["ssm_conv_b"], "ssm_norm_g": a["ssm_norm_g"],
        "dn_conv_w": a["dn_conv_w_2"][0],
        "dn_norm_g": a["dn_norm_g_2"],
    }
    squares, rope = constants()
    tokens = np.concatenate([a["x"][0], a["ctx"][0]], 0)
    everywhere = lambda v: np.ascontiguousarray(np.broadcast_to(np.asarray(v).reshape(1, -1), (P, v.size)))
    by_chunk = lambda w: np.ascontiguousarray(w.reshape(KC, P, -1).transpose(1, 0, 2))
    return {
        "weights": weights,
        "vectors": np.ascontiguousarray(np.concatenate([cols(vectors[n]) for n, _ in VECTORS], 1)),
        "squares": squares, "rope": rope,
        "tokens": np.ascontiguousarray(tokens.T.reshape(KC, P, TOK).transpose(1, 0, 2)),
        "context2": np.ascontiguousarray(a["ctx_2"][0].T.reshape(KC, P, CTX).transpose(1, 0, 2)),
        "sinks": everywhere(a["att_sink"][0][heads]),
        "ssm_d": everywhere(a["ssm_d"][0]),
        "dt_w": by_chunk(a["ssm_w_in"][0][:, SINNER + SCONV:]),
        "dt_rows": np.concatenate([everywhere(a["ssm_dt_bias"][0]), everywhere(a["ssm_a_log"][0])], 1),
        "ba_w": by_chunk(a["dn_w_in_2"][0][:, 4 * D:]),
        "ba_rows": np.concatenate([everywhere(a["dn_dt_bias_2"][0]), everywhere(a["dn_a_log_2"][0])], 1),
        "keys": np.ascontiguousarray(a["peer_keys_2"][0].transpose(3, 0, 1, 2)),
    }


def kernel(**inputs):
    import numpy as np
    import concourse.bacc as bacc
    from concourse.bass_utils import run_bass_kernel_spmd

    arrays = layout(inputs)
    nc = bacc.Bacc("TRN2", target_bir_lowering=False, num_devices=1)
    ext = {n: nc.dram_tensor("in_" + n, v.shape, mybir.dt.from_np(v.dtype), kind="ExternalInput").ap() for n, v in arrays.items()}
    out = nc.dram_tensor("out", (KC, P, LAT), F32, kind="ExternalOutput").ap()
    build(nc, ext, out)
    r = run_bass_kernel_spmd(nc, [{"in_" + n: v for n, v in arrays.items()}], core_ids=[0])
    return np.ascontiguousarray(r.results[0]["out"].reshape(D, LAT).T).reshape(1, LAT, D)
```

```python
from contextlib import ExitStack

import concourse.bass as bass
from concourse import mybir

F32 = mybir.dt.float32
BF16 = mybir.dt.bfloat16
U32 = mybir.dt.uint32
ALU = mybir.AluOpType
ACT = mybir.ActivationFunctionType
AX = mybir.AxisListType

P = 128
D = 1024
KC = D // P
LAT, CTX = 512, 256
TOK = LAT + CTX
TB = TOK // P
LB = LAT // P
RING = 4
BANK = 512
ALPHA = 4.0 ** 0.25
LN_EPS = 1e-5
EPS_RMS = 1e-5
EPS = 1e-6
NEG = -1e30
HEADS = 16
HD = 64
SINNER = 2048
SHEADS = 32
SCONV = 3072
NMOD = 48

STREAM = [("att_in", 12, 1), ("att_out", 8, 1), ("ff1_0", 32, 1), ("ff2_0", 8, 4),
          ("ssm_x", 16, 1), ("ssm_bc", 8, 1), ("ssm_z", 16, 1), ("ssm_out", 8, 2), ("ff1_1", 32, 1), ("ff2_1", 8, 4),
          ("dn_v", 8, 1), ("dn_k", 8, 1), ("dn_gate", 8, 1), ("dn_q", 8, 1), ("dn_out", 8, 1), ("w_q", 16, 1)]
MOD_RING = 2
MOD_ALONE = 2 * KC
MOD_IN_SSM = 12
MOD_BESIDE = {"att_in": 8, "att_out": 4, "ff1_0": 4, "ff2_0": 4}
EXPERT_TILES = 128
GROUP = RING
BLOCK = 64
DH = 8
PICKS = 16


def stream_starts():
    starts, at = {}, 0
    for name, chunks, per in STREAM:
        starts[name] = at
        at += chunks * per
    starts["experts"] = at
    return starts, at + 2 * EXPERT_TILES


VECTORS = [("c", 8), ("c_ctx", 8), ("c2", 8), ("c2_ctx", 8),
           ("b_mod0", 48), ("b_mod1", 48), ("b_ada", 48),
           ("mix_g0", 8), ("mix_g1", 8), ("mix_b0", 8), ("mix_b1", 8),
           ("ff_g0", 8), ("ff_g1", 8), ("ff_b0", 8), ("ff_b1", 8),
           ("norm_g0", 8), ("norm_g1", 8), ("final_g", 8),
           ("conv_w", 5 * 24), ("conv_b", 24), ("ssm_norm_g", 16), 
           ("dn_conv_w", 5 * 24), ("dn_norm_g", 1)]


def vector_columns():
    at, where = 0, {}
    for name, n in VECTORS:
        where[name] = (at, n)
        at += n
    return where, at


SQUARES = ["identity", "ones", "mean", "rope_swap", "mask_before", "mask_same",
           "mask_after", "sum_upto", "sum_from", "strict_lower", "strict_upper",
           "group_mean", "head_mean", "iota"]


class Count:

    def __init__(self, sem):
        self.sem, self.n, self.at, self.per = sem, 0, None, 0

    def mark(self, instruction, by=1):
        instruction.then_inc(self.sem, by)
        self.n += by
        return instruction

    def value(self, more=0):
        return self.n + more if self.at is None else self.at * self.per + (self.n + more)

    def enter(self, at, per):
        self.at, self.per, self.start = at, per, self.n

    def leave(self, iterations):
        assert self.n - self.start == self.per, (self.n - self.start, self.per)
        self.n = self.start + iterations * self.per
        self.at = None


def settle(engine, count):
    engine.wait_ge(count.sem, count.value())


def build(nc, ext, out):
    starts, n_tiles = stream_starts()
    columns, n_columns = vector_columns()
    gate_store = nc.dram_tensor("gate_store", (P, KC, LAT), F32, kind="Internal").ap()
    expert_gates = nc.dram_tensor("expert_gates", (LAT // BLOCK, P, P, BLOCK), F32, kind="Internal").ap()
    with ExitStack() as ctx:
        def sb(name, shape, dt=F32, stack=ctx):
            return stack.enter_context(nc.sbuf_tensor(name, shape, dt))

        def sem(name):
            return ctx.enter_context(nc.semaphore(name))

        ps = ctx.enter_context(nc.psum_tensor("ps", [P, 8, BANK], F32))

        def banks(first, width):
            return ps[:, first:first + (width + BANK - 1) // BANK, :].rearrange("p b n -> p (b n)")[:, 0:width]

        h = sb("h", [P, KC, TOK])
        x_all = sb("x_all", [P, 2, KC, TOK], BF16)
        x_hi, x_lo = x_all[:, 0], x_all[:, 1]
        w_raw = sb("w_raw", [P, RING, D])
        w_hi = sb("w_hi", [P, RING, D], BF16)
        w_lo = sb("w_lo", [P, RING, D], BF16)
        vec = sb("vec", [P, n_columns])
        sq = sb("sq", [P, len(SQUARES), P])
        mods = sb("mods", [P, 3, NMOD, 2])
        modp = sb("modp", [P, 3, NMOD, 2])
        cv = sb("cv", [P, 2, KC, 2])

        def V(name, i=0, n=1):
            return vec[:, columns[name][0] + i:columns[name][0] + i + n]

        def SQ(name):
            return sq[:, SQUARES.index(name), :]

        raw_ready = [sem(f"raw_ready{i}") for i in range(RING)]
        hi_done = sem("hi_done")
        split_done = sem("split_done")
        slot_free = sem("slot_free")
        psum_free = sem("psum_free")
        consts_ready = sem("consts_ready")
        mod_ready = [sem(f"mod_ready{i}") for i in range(MOD_RING)]
        mod_done = sem("mod_done")
        mod_read = sem("mod_read")
        pe_done, act_done, dve_done, pool_done, dma_done = (
            Count(sem(n)) for n in ("pe_done", "act_done", "dve_done", "pool_done", "dma_done"))
        chunks_before, mods_before = [0], [0]
        scratch = sb("scratch", [P, 2, TOK])
        skip = sb("skip", [P, SHEADS])
        mod_stack = ctx.enter_context(ExitStack())
        w_mod = [sb("w_mod", [P, MOD_RING, D], F32, mod_stack)]

        with nc.Block() as block:
            @block.sync
            def _(sp):
                sp.dma_start(vec[:], ext["vectors"]).then_inc(consts_ready, 16)
                sp.dma_start(sq[:], ext["squares"]).then_inc(consts_ready, 16)
                for t in range(RING):
                    sp.dma_start(w_raw[:, t], ext["weights"][t]).then_inc(raw_ready[t], 16)
                sp.dma_start(h[:], ext["tokens"]).then_inc(consts_ready, 16)

            @block.vector
            def _(dve):
                nc.vector.memset(mods[:, 0, 0, :], 0.0).then_inc(psum_free, 2)
                nc.vector.memset(mods[:, 0, 1, :], 0.0).then_inc(slot_free, RING)
                nc.vector.memset(mods[:, 0, 2, :], 0.0).then_inc(mod_read, 2)
                nc.vector.memset(mods[:, 0, 3, :], 0.0).then_inc(mod_done, MOD_RING)

            @block.scalar
            def _(act):
                act.wait_ge(consts_ready, 32 + 16)
                for b, names in enumerate((("c", "c_ctx"), ("c2", "c2_ctx"))):
                    for s, name in enumerate(names):
                        act_done.mark(nc.scalar.activation(cv[:, b, :, s], V(name, 0, KC), ACT.Silu))

        def split_high(act, t0, tiles):
            with act.Fori(0, tiles // RING) as i:
                for j in range(RING):
                    act.wait_ge(raw_ready[j], i * 16 + 16 * (t0 // RING + 1))
                    act.wait_ge(slot_free, i * RING + (t0 + j + 1))
                    nc.scalar.activation(w_hi[:, j], w_raw[:, j], ACT.Copy).then_inc(hi_done, 1)

        def split_low(pool, t0, tiles):
            with pool.Fori(0, tiles // RING) as i:
                for j in range(RING):
                    pool.wait_ge(hi_done, i * RING + (t0 + j + 1))
                    nc.gpsimd.tensor_tensor(w_lo[:, j], w_raw[:, j], w_hi[:, j],
                                            ALU.subtract).then_inc(split_done, 1)

        def mod_load(sp, n, parity):
            sp.wait_ge(mod_done, n + 1)
            sp.dma_start(w_mod[-1][:, parity], ext["mod_weights"][n]).then_inc(mod_ready[parity], 16)

        def mod_multiply(pe, n, parity, ready, block_no, bank=4):
            pe.wait_ge(mod_ready[parity], ready)
            pe.wait_ge(mod_read, n + 1)
            for k in range(KC):
                mm = nc.tensor.matmul(ps[:, bank + parity, 0:2], w_mod[-1][:, parity, k * P:(k + 1) * P], cv[:, block_no, k, :],
                                      start=(k == 0), stop=(k == KC - 1))
            mm.then_inc(mod_done, 1)

        def mod_keep(dve, n, parity, bank=4):
            dve.wait_ge(mod_done, n + 3)
            nc.vector.tensor_scalar(mods.rearrange("p l c s -> p (l c) s")[:, bass.ds(n, 1), :],
                                    ps[:, bank + parity:bank + parity + 1, 0:2], vec[:, bass.ds(n + columns["b_mod0"][0], 1)],
                                    None, ALU.add).then_inc(mod_read, 1)

        def linear(name, xh, xl, segments, evacuate, per_chunk):
            t0 = starts[name]
            chunks, per = next((c, k) for n, c, k in STREAM if n == name)
            tiles = chunks * per
            body = max(RING, 2 * per)
            in_body = body // per
            c0 = chunks_before[0]
            chunks_before[0] += chunks
            m0, m_body = mods_before[0], MOD_BESIDE.get(name, 0)
            mods_before[0] += m_body * (tiles // body)
            block_no = m0 // (2 * NMOD)

            def beside(j):
                return range(j * m_body // body, (j + 1) * m_body // body)

            def mod_ready_count(i, m):
                return i * (8 * m_body) + 16 * ((m0 + m) // 2 + 1)

            with nc.Block() as block:
                @block.sync
                def _(sp):
                    first = t0 + RING
                    with sp.Fori(0, tiles // body) as i:
                        for j in range(body):
                            sp.wait_ge(split_done, i * body + (t0 + j + 1))
                            sp.dma_start(w_raw[:, j % RING], ext["weights"][i * body + (first + j)]).then_inc(raw_ready[j % RING], 16)
                            for m in beside(j):
                                mod_load(sp, i * m_body + (m0 + m), m % 2)

                @block.scalar
                def _(act):
                    split_high(act, t0, tiles)

                @block.gpsimd
                def _(pool):
                    split_low(pool, t0, tiles)

                @block.tensor
                def _(pe):
                    with pe.Fori(0, tiles // body) as i:
                        for c in range(in_body):
                            pe.wait_ge(psum_free, i * in_body + (c0 + c + 1))
                            for q in range(per):
                                slot = (c * per + q) % RING
                                pe.wait_ge(hi_done, i * body + (t0 + c * per + q + 1))
                                for part, (w, xs) in enumerate(((w_hi, (xh, xl)), (w_lo, (xh,)))):
                                    if part == 1:
                                        pe.wait_ge(split_done, i * body + (t0 + c * per + q + 1))
                                    for k in range(KC):
                                        kk = q * KC + k
                                        for x in xs:
                                            for bank, width, lo in segments:
                                                mm = nc.tensor.matmul(
                                                    ps[:, 2 * (c % 2) + bank, 0:width],
                                                    w[:, slot, k * P:(k + 1) * P], x(kk, lo, width),
                                                    start=(kk == 0 and part == 0 and x is xh),
                                                    stop=(kk == per * KC - 1 and part == 1))
                                mm.then_inc(slot_free, 1)
                                for m in beside(c * per + q):
                                    mod_multiply(pe, i * m_body + (m0 + m), m % 2, mod_ready_count(i, m), block_no)

                @block.vector
                def _(dve):
                    with dve.Fori(0, tiles // body) as i:
                        dve_done.enter(i, in_body * per_chunk)
                        for c in range(in_body):
                            before = [m for q in range(per - 1) for m in beside(c * per + q)]
                            for m in before:
                                mod_keep(dve, i * m_body + (m0 + m), m % 2)
                            dve.wait_ge(slot_free, i * body + (RING + t0 + (c + 1) * per))
                            evacuate(dve, i * in_body + c, c % 2, i * in_body + (c0 + c + 3))
                            for m in beside(c * per + per - 1):
                                mod_keep(dve, i * m_body + (m0 + m), m % 2)
                        dve_done.leave(tiles // body)

        def x_parts(hi, lo):
            return (lambda k, at, width: hi[:, k, at:at + width]), (lambda k, at, width: lo[:, k, at:at + width])

        BOTH = [(0, LAT, 0), (1, CTX, LAT)]
        LATENT = [(0, LAT, 0)]

        def mods_alone(n):
            m0 = mods_before[0]
            with nc.Block() as block:
                @block.sync
                def _(sp):
                    with sp.Fori(0, n // 2) as i:
                        for m in range(2):
                            mod_load(sp, i * 2 + (m0 + m), m)

                @block.tensor
                def _(pe):
                    with pe.Fori(0, n // 2) as i:
                        for m in range(2):
                            mod_multiply(pe, i * 2 + (m0 + m), m, i * 16 + (8 * m0 + 16), m0 // (2 * NMOD))

                @block.vector
                def _(dve):
                    with dve.Fori(0, n // 2) as i:
                        for m in range(2):
                            mod_keep(dve, i * 2 + (m0 + m), m)
            mods_before[0] += n

        def mods_finish(layer, first):
            last = min(mods_before[0] - layer * NMOD, NMOD)
            with nc.Block() as block:
                @block.vector
                def _(dve):
                    dve_done.mark(nc.vector.tensor_scalar(modp[:, layer, first:last], mods[:, layer, first:last], 1.0, None, ALU.add))
                    settle(dve, dve_done)
                    for m in (2 * KC, 5 * KC):
                        if layer < 2 and first <= m < last:
                            dve_done.mark(nc.vector.tensor_scalar(modp[:, layer, m:m + KC], mods[:, layer, m:m + KC],
                                                                  1.0 / ALPHA, None, ALU.mult))

        mods_alone(MOD_ALONE)
        mods_finish(0, 0)

        def modulate_parts(layer, which, width):
            d0, a0, p0 = dve_done.n, act_done.n, pool_done.n
            segs = [(0, LAT, 0)] + ([(1, CTX, LAT)] if width == TOK else [])
            per = len(segs)
            with nc.Block() as block:
                @block.vector
                def _(dve):
                    for k in range(KC):
                        if k >= 2:
                            dve.wait_ge(pool_done.sem, p0 + k - 1)
                        for s, w, lo in segs:
                            dve_done.mark(nc.vector.tensor_scalar(
                                scratch[:, k % 2, lo:lo + w], h[:, k, lo:lo + w],
                                modp[:, layer, (which + 1) * KC + k, s:s + 1],
                                mods[:, layer, which * KC + k, s:s + 1], ALU.mult, ALU.add))

                @block.scalar
                def _(act):
                    for k in range(KC):
                        act.wait_ge(dve_done.sem, d0 + per * (k + 1))
                        act_done.mark(nc.scalar.activation(x_hi[:, k, 0:width], scratch[:, k % 2, 0:width], ACT.Copy))

                @block.gpsimd
                def _(pool):
                    for k in range(KC):
                        pool.wait_ge(act_done.sem, a0 + k + 1)
                        pool_done.mark(nc.gpsimd.tensor_tensor(x_lo[:, k, 0:width], scratch[:, k % 2, 0:width],
                                                               x_hi[:, k, 0:width], ALU.subtract))

        def normalise(width, eps, centre, gain, bias=None, keep=None, then=None):
            segs = [(0, LAT, 0)] + ([(1, CTX, LAT)] if width == TOK else [])
            per = len(segs) if then else 0
            first = 1 if centre else 0
            turns = w_hi.rearrange("p r n -> p (r n)").bitcast(F32).rearrange("p (u n) -> p u n", u=2)[:, :, 0:width]
            p0, d0, a0, q0 = pe_done.n, dve_done.n, act_done.n, pool_done.n

            def target(k):
                return h[:, k, 0:width] if centre else turns[:, k % 2] if keep is None else keep[:, k, 0:width]

            def scaled(k):
                return d0 + first * KC + 2 + (k + 1) + per * max(0, k - 1)

            def modulated(k):
                return d0 + first * KC + 2 + min(k + 2, KC) + per * (k + 1)

            def affine(k):
                return a0 + KC + 1 + (k + 1) + (max(0, k - 1) if then else 0)

            def high(k):
                return a0 + KC + 1 + (min(k + 2, KC) if centre else 0) + (k + 1)

            with nc.Block() as block:
                @block.tensor
                def _(pe):
                    if centre:
                        for s, w, lo in segs:
                            mm = nc.tensor.matmul(ps[:, s, 0:w], SQ("mean"), scratch[:, 0, lo:lo + w], start=True, stop=True)
                        pe_done.mark(mm)
                    for k in range(KC):
                        pe.wait_ge(act_done.sem, a0 + k + 1)
                        for s, w, lo in segs:
                            mm = nc.tensor.matmul(ps[:, 2 + s, 0:w], SQ("mean"), scratch[:, k % 2, lo:lo + w],
                                                  start=(k == 0), stop=(k == KC - 1))
                        pe_done.mark(mm)

                @block.scalar
                def _(act):
                    for k in range(KC):
                        if centre:
                            act.wait_ge(dve_done.sem, d0 + k + 1)
                        if k >= 2:
                            act.wait_ge(pe_done.sem, p0 + first + k - 1)
                        act_done.mark(nc.scalar.activation(scratch[:, k % 2, 0:width], h[:, k, 0:width], ACT.Square))
                    act.wait_ge(dve_done.sem, d0 + first * KC + 1)
                    act_done.mark(nc.scalar.activation(scratch[:, 1, 0:width], scratch[:, 0, 0:width], ACT.Sqrt))
                    for k in range(KC + 1):
                        if centre and k < KC:
                            act.wait_ge(dve_done.sem, scaled(k))
                            act_done.mark(nc.scalar.activation(h[:, k, 0:width], h[:, k, 0:width], ACT.Identity,
                                                               bias=V(bias, k), scale=V(gain, k)))
                        if then and k >= 1:
                            act.wait_ge(dve_done.sem, modulated(k - 1))
                            act_done.mark(nc.scalar.activation(x_hi[:, k - 1, 0:width], turns[:, (k - 1) % 2], ACT.Copy))

                @block.vector
                def _(dve):
                    if centre:
                        dve.wait_ge(pe_done.sem, p0 + 1)
                        for k in range(KC):
                            dve_done.mark(nc.vector.tensor_tensor(h[:, k, 0:width], h[:, k, 0:width],
                                                                  banks(0, width), ALU.subtract))
                    dve.wait_ge(pe_done.sem, p0 + first + KC)
                    dve_done.mark(nc.vector.tensor_scalar(scratch[:, 0, 0:width], banks(2, width), eps, None, ALU.add))
                    dve.wait_ge(act_done.sem, a0 + KC + 1)
                    dve_done.mark(nc.vector.reciprocal(scratch[:, 0, 0:width], scratch[:, 1, 0:width]))
                    settle(dve, dve_done)
                    for k in range(KC + 1):
                        if k < KC:
                            if then and not centre and k >= 2:
                                dve.wait_ge(pool_done.sem, q0 + k - 1)
                            if centre:
                                dve_done.mark(nc.vector.tensor_tensor(h[:, k, 0:width], h[:, k, 0:width],
                                                                      scratch[:, 0, 0:width], ALU.mult))
                            else:
                                dve_done.mark(nc.vector.scalar_tensor_tensor(
                                    out=target(k), in0=h[:, k, 0:width], scalar=V(gain, k),
                                    in1=scratch[:, 0, 0:width], op0=ALU.mult, op1=ALU.mult))
                        if then and k >= 1:
                            layer, which = then
                            if centre:
                                dve.wait_ge(act_done.sem, affine(k - 1))
                                if k >= 3:
                                    dve.wait_ge(pool_done.sem, q0 + k - 2)
                            else:
                                dve.wait_ge(dve_done.sem, scaled(k - 1))
                            for s, w, lo in segs:
                                dve_done.mark(nc.vector.tensor_scalar(
                                    turns[:, (k - 1) % 2, lo:lo + w], target(k - 1)[:, lo:lo + w],
                                    modp[:, layer, (which + 1) * KC + k - 1, s:s + 1],
                                    mods[:, layer, which * KC + k - 1, s:s + 1], ALU.mult, ALU.add))

                @block.gpsimd
                def _(pool):
                    if then:
                        for k in range(KC):
                            pool.wait_ge(act_done.sem, high(k))
                            pool_done.mark(nc.gpsimd.tensor_tensor(x_lo[:, k, 0:width], turns[:, k % 2],
                                                                   x_hi[:, k, 0:width], ALU.subtract))

        def add_to_residual(layer, which, segments, table):
            def evacuate(dve, c, s, freed):
                width = segments[-1][1] + segments[-1][2]
                for n, (bank, w, lo) in enumerate(segments):
                    ins = nc.vector.scalar_tensor_tensor(
                        out=h[:, bass.ds(c, 1), lo:lo + w], in0=ps[:, 2 * s + bank:2 * s + bank + 1, 0:w],
                        scalar=table[:, layer, bass.ds(c + which * KC, 1), bank:bank + 1],
                        in1=h[:, bass.ds(c, 1), lo:lo + w], op0=ALU.mult, op1=ALU.add)
                    if n == len(segments) - 1:
                        ins.then_inc(psum_free, 1)
                    else:
                        dve_done.mark(ins)
                settle(dve, dve_done)
                dve.wait_ge(psum_free, freed)
                dve_done.mark(nc.vector.tensor_tensor(scratch[:, 0:1, 0:width], scratch[:, 0:1, 0:width],
                                                      h[:, bass.ds(c, 1), 0:width], ALU.add))
            return evacuate

        def residual_product(name, xh, xl, segments, layer, which, table):
            with nc.Block() as block:
                @block.vector
                def _(dve):
                    dve_done.mark(nc.vector.memset(scratch[:, 0], 0.0))
            linear(name, xh, xl, segments, add_to_residual(layer, which, segments, table), len(segments))

        def mlp(layer, width):
            segments = BOTH if width == TOK else LATENT
            with ExitStack() as local:
                g_hi = sb(f"g_hi{layer}", [P, 32, width], BF16, local)
                g_lo = sb(f"g_lo{layer}", [P, 32, width], BF16, local)

                def evacuate(dve, c, s, freed):
                    dve_done.mark(nc.vector.tensor_scalar(scratch[:, 0, 0:width], banks(2 * s, width), 0.0, None, ALU.max))
                    settle(dve, dve_done)
                    dve_done.mark(nc.vector.tensor_tensor(scratch[:, 1, 0:width], scratch[:, 0, 0:width], scratch[:, 0, 0:width], ALU.mult))
                    settle(dve, dve_done)
                    dve_done.mark(nc.vector.tensor_copy(g_hi[:, bass.ds(c, 1), :], scratch[:, 1:2, 0:width]))
                    settle(dve, dve_done)
                    nc.vector.tensor_tensor(g_lo[:, bass.ds(c, 1), :], scratch[:, 1:2, 0:width], g_hi[:, bass.ds(c, 1), :],
                                            ALU.subtract).then_inc(psum_free, 1)

                linear(f"ff1_{layer}", *x_parts(x_hi, x_lo), segments, evacuate, 3)
                residual_product(f"ff2_{layer}", *x_parts(g_hi, g_lo), segments, layer, 5, modp)

        def keep_chunk(target, width):
            def evacuate(dve, c, s, freed):
                nc.vector.tensor_copy(target[:, bass.ds(c, 1), 0:width],
                                      banks(2 * s, width).unsqueeze(1)).then_inc(psum_free, 1)
            return evacuate

        def attention():
            scores_done, scores_read, max_ready, exp_done, probs_ready, turned, turned_read, out_done, out_high, out_read = (
                sem(n) for n in ("scores_done", "scores_read", "max_ready", "exp_done", "probs_ready", "turned", "turned_read",
                                 "out_done", "out_high", "out_read"))
            with ExitStack() as local:
                with ExitStack() as inner:
                    qkv = sb("qkv", [P, 12, TOK], F32, inner)
                    qk_rot = sb("qk_rot", [P, 10, LAT], F32, inner)
                    v_tok = sb("v_tok", [P, TB, 4 * HD], F32, inner)
                    scores = sb("scores", [P, 2, 5 * P], F32, inner)
                    probs = sb("probs", [P, 2, 5 * P], F32, inner)
                    probs_t = scratch.rearrange("p a b -> p (a b)")[:, 0:1280].rearrange("p (u n) -> p u n", u=2)
                    top = sb("top", [P, 96], F32, inner)
                    neg_max = sb("neg_max", [P, 96], F32, inner)
                    row_sum = sb("row_sum", [P, 96], F32, inner)
                    sink_exp = sb("sink_exp", [P, 96], F32, inner)
                    sinks = sb("sinks", [P, 2, HEADS], F32, inner)
                    rope = sb("rope", [P, 2, LAT], F32, inner)

                    linear("att_in", *x_parts(x_hi, x_lo), BOTH, keep_chunk(qkv, TOK), 0)
                    mods_finish(0, MOD_ALONE)

                    d0, p0, m0 = dve_done.n, pe_done.n, dma_done.n
                    with nc.Block() as block:
                        @block.sync
                        def _(sp):
                            dma_done.mark(sp.dma_start(rope[:], ext["rope"]), 16)
                            dma_done.mark(sp.dma_start(sinks[:, 0], ext["sinks"]), 16)

                        @block.tensor
                        def _(pe):
                            for c in range(10):
                                if c >= 4:
                                    pe.wait_ge(dve_done.sem, d0 + 3 * (c - 4) + 1)
                                pe_done.mark(nc.tensor.matmul(ps[:, c % 4, :], SQ("rope_swap"), qkv[:, c, 0:LAT],
                                                              start=True, stop=True))
                            for t in range(TB):
                                for c in range(2):
                                    mm = nc.tensor.transpose(ps[:, 4 + t // 2, (t % 2) * 256 + c * P:(t % 2) * 256 + (c + 1) * P],
                                                             qkv[:, 10 + c, t * P:(t + 1) * P], SQ("identity"))
                                pe_done.mark(mm)

                        @block.vector
                        def _(dve):
                            dve.wait_ge(dma_done.sem, m0 + 32)
                            for c in range(10):
                                dve.wait_ge(pe_done.sem, p0 + c + 1)
                                if c >= 1:
                                    settle(dve, dve_done)
                                dve_done.mark(nc.vector.tensor_tensor(scratch[:, 0, 0:LAT], ps[:, c % 4, :], rope[:, 1], ALU.mult))
                                dve_done.mark(nc.vector.tensor_tensor(qk_rot[:, c, :], qkv[:, c, 0:LAT], rope[:, 0], ALU.mult))
                                settle(dve, dve_done)
                                dve_done.mark(nc.vector.tensor_tensor(qk_rot[:, c, :], qk_rot[:, c, :], scratch[:, 0, 0:LAT], ALU.add))

                        @block.scalar
                        def _(act):
                            act.wait_ge(dma_done.sem, m0 + 32)
                            act_done.mark(nc.scalar.activation(sinks[:, 1], sinks[:, 0], ACT.Copy, scale=-1.0))
                            for t in range(TB):
                                act.wait_ge(pe_done.sem, p0 + 10 + (t // 2 + 1) * 2)
                                act_done.mark(nc.scalar.activation(v_tok[:, t, :], ps[:, 4 + t // 2, (t % 2) * 256:(t % 2) * 256 + 256],
                                                                   ACT.Copy))

                    units = []
                    for b in range(TB):
                        near = [t for t in (b - 1, b, b + 1) if 0 <= t < LB] if b < LB else []
                        units += [(b, j, f, near) for j in range(KC) for f in range(2)]
                    U = len(units)

                    with nc.Block() as block:
                        @block.tensor
                        def _(pe):
                            def score(u):
                                b, j, f, near = units[u]
                                rows = slice(64 * f, 64 * f + 64)
                                if u >= 2:
                                    pe.wait_ge(scores_read, u - 1)
                                if near:
                                    nc.tensor.matmul(ps[:, u % 2, 0:len(near) * P], qk_rot[rows, j, b * P:(b + 1) * P],
                                                     qk_rot[rows, 8 + j // 4, near[0] * P:(near[-1] + 1) * P],
                                                     start=True, stop=True)
                                nc.tensor.matmul(ps[:, 2 + u % 2, 0:CTX], qkv[rows, j, b * P:(b + 1) * P],
                                                 qkv[rows, 8 + j // 4, LAT:TOK], start=True, stop=True).then_inc(scores_done, 1)

                            def turn(u):
                                n = len(units[u][3]) + 2
                                pe.wait_ge(probs_ready, u + 1)
                                if u >= 2:
                                    pe.wait_ge(turned_read, u - 1)
                                for t in range(n):
                                    dst = ps[:, 4 + u % 2, t * P:(t + 1) * P] if t < 4 else ps[:, 6, 0:P]
                                    if t == 4 and u >= 1:
                                        pe.wait_ge(turned_read, u)
                                    mm = nc.tensor.transpose(dst, probs[:, u % 2, t * P:(t + 1) * P], SQ("identity"))
                                mm.then_inc(turned, 1)

                            def weigh(u):
                                b, j, f, near = units[u]
                                kv = 2 * (j // 4) + f
                                pe.wait_ge(turned_read, u + 1)
                                if u % 8 == 0 and u > 0:
                                    pe.wait_ge(out_read, u // 8)
                                keys = near + [LB, LB + 1]
                                for n, t in enumerate(keys):
                                    mm = nc.tensor.matmul(ps[64 * f:64 * f + 64, 7, (j % 4) * P:(j % 4 + 1) * P],
                                                          v_tok[:, t, kv * HD:(kv + 1) * HD],
                                                          probs_t[:, u % 2, n * P:(n + 1) * P],
                                                          start=(n == 0), stop=(n == len(keys) - 1))
                                mm.then_inc(out_done, 1)

                            for s in range(U + 3):
                                if s < U:
                                    score(s)
                                if 2 <= s <= U + 1:
                                    turn(s - 2)
                                if s >= 3:
                                    weigh(s - 3)

                        @block.vector
                        def _(dve):
                            def read(u):
                                b, j, f, near = units[u]
                                n = len(near) * P
                                dve.wait_ge(scores_done, u + 1)
                                if u >= 2:
                                    dve.wait_ge(exp_done, u - 1)
                                if near:
                                    first = 0 if near[0] == b - 1 else 1
                                    mask = sq[:, SQUARES.index("mask_before"):SQUARES.index("mask_before") + 3, :]
                                    dve_done.mark(nc.vector.tensor_tensor(
                                        scores[:, u % 2, 0:n].rearrange("p (a b) -> p a b", b=P),
                                        ps[:, u % 2, 0:n].rearrange("p (a b) -> p a b", b=P),
                                        mask[:, first:first + len(near), :], ALU.add))
                                dve_done.mark(nc.vector.tensor_copy(scores[:, u % 2, n:n + CTX], ps[:, 2 + u % 2, 0:CTX]))
                                settle(dve, dve_done)
                                nc.vector.tensor_reduce(top[:, u:u + 1], scores[:, u % 2, 0:n + CTX], AX.X,
                                                        ALU.max).then_inc(scores_read, 1)
                                dve.wait_ge(scores_read, u + 1)
                                nc.vector.tensor_scalar(neg_max[:, u:u + 1], top[:, u:u + 1], -HD ** -0.5,
                                                        sinks[:, 1, 2 * j + f:2 * j + f + 1], ALU.mult,
                                                        ALU.min).then_inc(max_ready, 1)

                            def divide(u):
                                n = len(units[u][3]) * P + CTX
                                dve.wait_ge(exp_done, u + 1)
                                dve_done.mark(nc.vector.tensor_tensor(row_sum[:, u:u + 1], row_sum[:, u:u + 1], sink_exp[:, u:u + 1], ALU.add))
                                settle(dve, dve_done)
                                dve_done.mark(nc.vector.reciprocal(row_sum[:, u:u + 1], row_sum[:, u:u + 1]))
                                settle(dve, dve_done)
                                nc.vector.tensor_scalar(probs[:, u % 2, 0:n], probs[:, u % 2, 0:n], row_sum[:, u:u + 1], None,
                                                        ALU.mult).then_inc(probs_ready, 1)

                            def low(g):
                                c, b = 4 * (g % 2), g // 2
                                dve.wait_ge(out_high, g + 1)
                                nc.vector.tensor_tensor(x_lo[:, c:c + 4, b * P:(b + 1) * P], ps[:, 7, :].rearrange("p (c t) -> p c t", t=P),
                                                        x_hi[:, c:c + 4, b * P:(b + 1) * P], ALU.subtract).then_inc(out_read, 1)

                            for s in range(U + 1):
                                if s < U:
                                    read(s)
                                if s >= 1:
                                    divide(s - 1)
                                if s % 8 == 2 and s > 8:
                                    low(s // 8 - 1)
                            low(U // 8 - 1)

                        @block.scalar
                        def _(act):
                            def exps(u):
                                b, j, f, near = units[u]
                                n = len(near) * P + CTX
                                act.wait_ge(max_ready, u + 1)
                                if u >= 2:
                                    act.wait_ge(turned, u - 1)
                                act_done.mark(nc.scalar.activation(sink_exp[:, u:u + 1], sinks[:, 0, 2 * j + f:2 * j + f + 1],
                                                                   ACT.Exp, bias=neg_max[:, u:u + 1]))
                                nc.scalar.activation(probs[:, u % 2, 0:n], scores[:, u % 2, 0:n], ACT.Exp,
                                                     bias=neg_max[:, u:u + 1], scale=HD ** -0.5,
                                                     accum_out=row_sum[:, u:u + 1]).then_inc(exp_done, 1)

                            def copy(u):
                                n = len(units[u][3]) + 2
                                act.wait_ge(turned, u + 1)
                                if u >= 2:
                                    act.wait_ge(out_done, u - 1)
                                wide = min(n, 4) * P
                                ins = nc.scalar.activation(probs_t[:, u % 2, 0:wide], ps[:, 4 + u % 2, 0:wide], ACT.Copy)
                                if n > 4:
                                    act_done.mark(ins)
                                    ins = nc.scalar.activation(probs_t[:, u % 2, 4 * P:5 * P],
                                                               ps[:, 6, 0:P], ACT.Copy)
                                ins.then_inc(turned_read, 1)

                            def high(g):
                                c, b = 4 * (g % 2), g // 2
                                act.wait_ge(out_done, 8 * g + 8)
                                nc.scalar.activation(x_hi[:, c:c + 4, b * P:(b + 1) * P], ps[:, 7, :].rearrange("p (c t) -> p c t", t=P),
                                                     ACT.Copy).then_inc(out_high, 1)

                            for s in range(U + 1):
                                if s < U:
                                    exps(s)
                                if s % 8 == 2 and s > 8:
                                    high(s // 8 - 1)
                                if s >= 1:
                                    copy(s - 1)
                            high(U // 8 - 1)

            residual_product("att_out", *x_parts(x_hi, x_lo), BOTH, 0, 2, modp)
            mods_finish(0, 5 * KC)

        def pad_layout(rows):
            at, out = 2, []
            for lo, w in rows:
                out.append((lo, w, at))
                at += w + 4
            return out, at + 2

        def convolve(pad, acc, target, layout, width, weights, n_chunks, chunk0, bias):
            w0 = columns[weights][0]
            span = width - 4

            def evacuate(dve, c, s, freed):
                n = len(layout)
                groups = []
                for lo, w, at in layout:
                    if groups and groups[-1][1] == w:
                        groups[-1][3] += 1
                    else:
                        groups.append([lo, w, at, 1])
                for lo, w, at, count in groups:
                    dst = pad[:, at:at + count * (w + 4)].rearrange("p (r n) -> p r n", r=count)[:, :, 0:w]
                    src = banks(2 * s, TOK)[:, lo:lo + count * w].rearrange("p (r n) -> p r n", r=count)
                    ins = nc.vector.tensor_copy(dst, src)
                    if lo + count * w == sum(x[1] for x in layout):
                        ins.then_inc(psum_free, 1)
                    else:
                        dve_done.mark(ins)
                settle(dve, dve_done)
                dve.wait_ge(psum_free, freed)
                for tap in range(5):
                    scalar = vec[:, bass.ds(c + (w0 + tap * n_chunks + chunk0), 1)]
                    src = pad[:, tap:tap + span]
                    if tap == 0:
                        if bias is None:
                            ins = nc.vector.tensor_scalar(acc[:, 0:span], src, scalar, None, ALU.mult)
                        else:
                            ins = nc.vector.tensor_scalar(acc[:, 0:span], src, scalar,
                                                          vec[:, bass.ds(c + (columns[bias][0] + chunk0), 1)], ALU.mult, ALU.add)
                    else:
                        ins = nc.vector.scalar_tensor_tensor(out=acc[:, 0:span], in0=src, scalar=scalar,
                                                             in1=acc[:, 0:span], op0=ALU.mult, op1=ALU.add)
                    dve_done.mark(ins)
                    settle(dve, dve_done)
                for lo, w, at, count in groups:
                    dst = target[:, bass.ds(c, 1), lo:lo + count * w].rearrange("p a (r n) -> p (a r) n", r=count)
                    dve_done.mark(nc.vector.tensor_copy(dst, acc[:, at - 2:at - 2 + count * (w + 4)].rearrange(
                        "p (r n) -> p r n", r=count)[:, :, 0:w]))
                settle(dve, dve_done)
            return evacuate

        def per_conv(groups):
            return groups - 1 + 5 + groups

        def softplus(v, tmp):
            e, u, d, r = tmp
            a0, d0 = act_done.n, dve_done.n
            with nc.Block() as block:
                @block.scalar
                def _(act):
                    act_done.mark(nc.scalar.activation(e, v, ACT.Abs))
                    settle(act, act_done)
                    act_done.mark(nc.scalar.activation(e, e, ACT.Exp, scale=-1.0))
                    act.wait_ge(dve_done.sem, d0 + 1)
                    act_done.mark(nc.scalar.activation(r, u, ACT.Ln))

                @block.vector
                def _(dve):
                    dve.wait_ge(act_done.sem, a0 + 2)
                    dve_done.mark(nc.vector.tensor_scalar(u, e, 1.0, None, ALU.add))
                    settle(dve, dve_done)
                    dve_done.mark(nc.vector.tensor_scalar(d, u, 1.0, None, ALU.subtract))
                    dve.wait_ge(act_done.sem, a0 + 3)
                    settle(dve, dve_done)
                    dve_done.mark(nc.vector.scalar_tensor_tensor(out=u, in0=d, scalar=0.0, in1=e, op0=ALU.is_equal, op1=ALU.mult))
                    dve_done.mark(nc.vector.tensor_tensor(r, r, e, ALU.mult))
                    settle(dve, dve_done)
                    dve_done.mark(nc.vector.tensor_scalar(d, d, 2.0 ** -24, None, ALU.max))
                    settle(dve, dve_done)
                    dve_done.mark(nc.vector.reciprocal(d, d))
                    settle(dve, dve_done)
                    dve_done.mark(nc.vector.tensor_tensor(r, r, d, ALU.mult))
                    settle(dve, dve_done)
                    dve_done.mark(nc.vector.tensor_tensor(r, r, u, ALU.add))
                    settle(dve, dve_done)
                    dve_done.mark(nc.vector.scalar_tensor_tensor(out=v, in0=v, scalar=0.0, in1=r, op0=ALU.max, op1=ALU.add))

        def small_product(w_ext, n, w32, wh, wl, target):
            m0, a0, d0, p0 = dma_done.n, act_done.n, dve_done.n, pe_done.n
            with nc.Block() as block:
                @block.sync
                def _(sp):
                    dma_done.mark(sp.dma_start(w32, w_ext), 16)

                @block.scalar
                def _(act):
                    act.wait_ge(dma_done.sem, m0 + 16)
                    act_done.mark(nc.scalar.activation(wh, w32, ACT.Copy))

                @block.tensor
                def _(pe):
                    pe.wait_ge(dve_done.sem, d0 + 1)
                    for t in range(TB):
                        for k in range(KC):
                            for part, (x, w) in enumerate(((x_hi, wh), (x_lo, wh), (x_hi, wl))):
                                mm = nc.tensor.matmul(ps[:, 0, t * n:(t + 1) * n], x[:, k, t * P:(t + 1) * P], w[:, k, :],
                                                      start=(k == 0 and part == 0), stop=(k == KC - 1 and part == 2))
                    pe_done.mark(mm)

                @block.vector
                def _(dve):
                    dve.wait_ge(act_done.sem, a0 + 1)
                    dve_done.mark(nc.vector.tensor_tensor(wl, w32, wh, ALU.subtract))
                    dve.wait_ge(pe_done.sem, p0 + 1)
                    dve_done.mark(nc.vector.tensor_copy(target, ps[:, 0, 0:TB * n].rearrange("p (t n) -> p t n", n=n)))

        def silu_and_turn(source, chunks, target, turned_chunks):
            a0, p0, d0 = act_done.n, pe_done.n, dve_done.n
            with nc.Block() as block:
                @block.scalar
                def _(act):
                    for c in range(chunks):
                        act_done.mark(nc.scalar.activation(source[:, c, :], source[:, c, :], ACT.Silu))

                @block.tensor
                def _(pe):
                    for c in range(turned_chunks):
                        pe.wait_ge(act_done.sem, a0 + c + 1)
                        if c >= 4:
                            pe.wait_ge(dve_done.sem, d0 + c - 3)
                        for t in range(TB):
                            mm = nc.tensor.transpose(banks(2 * (c % 4), TOK)[:, t * P:(t + 1) * P], source[:, c, t * P:(t + 1) * P], SQ("identity"))
                        pe_done.mark(mm)

                @block.vector
                def _(dve):
                    for c in range(turned_chunks):
                        dve.wait_ge(pe_done.sem, p0 + c + 1)
                        dve_done.mark(nc.vector.tensor_copy(target[:, :, c * P:(c + 1) * P],
                                                            banks(2 * (c % 4), TOK).rearrange("p (t n) -> p t n", n=P)))

        def ssm(x_tok, local):
            b_tok = sb("b_tok", [P, TB, 512], F32, local)
            with ExitStack() as first:
                x_t = sb("x_t", [P, 16, TOK], F32, first)
                layout, width = pad_layout([(0, LAT), (LAT, CTX)])
                pad = b_tok.rearrange("p t n -> p (t n)")[:, 0:width]
                acc = b_tok.rearrange("p t n -> p (t n)")[:, 1024:1024 + width]
                zero_pad(pad)
                linear("ssm_x", *x_parts(x_hi, x_lo), BOTH,
                       convolve(pad, acc, x_t, layout, width, "conv_w", 24, 0, "conv_b"), per_conv(2))
                silu_and_turn(x_t, 16, x_tok, 16)
            bc_t = sb("bc_t", [P, 8, TOK], F32, local)
            extra = sb("extra", [P, 2, 2, LAT], F32, local)
            dt = sb("dt", [P, TB, 64], F32, local)
            cum = sb("cum", [P, TB, 64], F32, local)
            tot = sb("tot", [P, TB, 64], F32, local)
            rows = sb("rows", [P, 128], F32, local)
            flat = extra.rearrange("p a b n -> p (a b n)")
            layout, width = pad_layout([(0, LAT), (LAT, CTX)])
            pad, acc = flat[:, 0:width], flat[:, 1024:1024 + width]
            zero_pad(pad)
            linear("ssm_bc", *x_parts(x_hi, x_lo), BOTH,
                   convolve(pad, acc, bc_t, layout, width, "conv_w", 24, 16, "conv_b"), per_conv(2))
            silu_and_turn(bc_t, 8, b_tok, 4)
            dtw = flat[:, 0:512].rearrange("p (k n) -> p k n", k=KC)
            dth = flat[:, 512:768].bitcast(BF16).rearrange("p (k n) -> p k n", k=KC)
            dtl = flat[:, 768:1024].bitcast(BF16).rearrange("p (k n) -> p k n", k=KC)
            small_product(ext["dt_w"], 64, dtw, dth, dtl, dt[:])
            m0 = dma_done.n
            with nc.Block() as block:
                @block.sync
                def _(sp):
                    dma_done.mark(sp.dma_start(rows[:], ext["dt_rows"]), 16)

                @block.vector
                def _(dve):
                    dve.wait_ge(dma_done.sem, m0 + 16)
                    dve_done.mark(nc.vector.tensor_tensor(dt[:], dt[:], rows[:, 0:64].unsqueeze(1).broadcast_to([P, TB, 64]), ALU.add))
            f4 = flat[:, 0:4 * 384].rearrange("p (a t n) -> p a t n", a=4, t=TB)
            softplus(dt[:], [f4[:, q] for q in range(4)])
            p0, a0, d0 = pe_done.n, act_done.n, dve_done.n
            a_of = f4[:, 0]
            with nc.Block() as block:
                @block.scalar
                def _(act):
                    act_done.mark(nc.scalar.activation(rows[:, 0:64], rows[:, 64:128], ACT.Exp))
                    act.wait_ge(dve_done.sem, d0 + 5)
                    act_done.mark(nc.scalar.activation(tot[:], tot[:], ACT.Exp))

                @block.vector
                def _(dve):
                    dve.wait_ge(act_done.sem, a0 + 1)
                    dve_done.mark(nc.vector.tensor_scalar(rows[:, 0:64], rows[:, 0:64], -1.0, None, ALU.mult))
                    settle(dve, dve_done)
                    dve_done.mark(nc.vector.tensor_tensor(a_of, dt[:], rows[:, 0:64].unsqueeze(1).broadcast_to([P, TB, 64]), ALU.mult))
                    dve.wait_ge(pe_done.sem, p0 + 1)
                    dve_done.mark(nc.vector.tensor_copy(cum[:], ps[:, 0, 0:384].rearrange("p (t n) -> p t n", n=64)))
                    dve_done.mark(nc.vector.tensor_copy(tot[:], ps[:, 1, 0:384].rearrange("p (t n) -> p t n", n=64)))
                    settle(dve, dve_done)
                    dve_done.mark(nc.vector.tensor_tensor(f4[:, 1], tot[:], cum[:], ALU.subtract))

                @block.tensor
                def _(pe):
                    pe.wait_ge(dve_done.sem, d0 + 2)
                    for t in range(TB):
                        for d, m in enumerate(("sum_upto", "sum_from")):
                            nc.tensor.matmul(ps[:, 0, t * 64 + 32 * d:t * 64 + 32 * d + 32], SQ(m), a_of[:, t, 32 * d:32 * d + 32],
                                             start=True, stop=True)
                    pe_done.mark(nc.tensor.matmul(ps[:, 1, 0:384], SQ("ones"), a_of.rearrange("p t n -> p (t n)"), start=True, stop=True))
            wgt = sb("wgt", [P, TB, 64], F32, local)
            a_keep = sb("a_keep", [P, TB, 64], F32, local)
            a1 = act_done.n
            with nc.Block() as block:
                @block.scalar
                def _(act):
                    act_done.mark(nc.scalar.activation(f4[:, 1], f4[:, 1], ACT.Exp))
                    act_done.mark(nc.scalar.activation(a_keep[:], a_of, ACT.Copy))

                @block.vector
                def _(dve):
                    dve.wait_ge(act_done.sem, a1 + 1)
                    dve_done.mark(nc.vector.tensor_tensor(wgt[:], f4[:, 1], dt[:], ALU.mult))

            x_flat = [x_hi.rearrange("p k n -> p (k n)").bitcast(F32), x_lo.rearrange("p k n -> p (k n)").bitcast(F32)]
            states = [x_flat[d][:, 0:2048].rearrange("p (c n) -> p c n", c=LB) for d in range(2)]
            carry = [x_flat[d][:, 2048:2560] for d in range(2)]
            weighted = w_hi.rearrange("p r n -> p (r n)").bitcast(F32)[:, 0:1024].rearrange("p (u n) -> p u n", u=2)
            cb = x_flat[0][:, 2560:3072]
            spread = w_hi.rearrange("p r n -> p (r n)").bitcast(F32).rearrange("p (u d n) -> p u d n", u=2, d=2)
            decay = w_lo.rearrange("p r n -> p (r n)").bitcast(F32).rearrange("p (u d n) -> p u d n", u=2, d=2)
            mixed = scratch.rearrange("p a n -> p (a n)")[:, 0:1024].rearrange("p (u n) -> p u n", u=2)
            c_scaled = extra
            w_mod.append(sb("w_mod2", [P, MOD_RING, D], F32, local))
            for g in range(4):
                ssm_states(g, x_tok, b_tok, wgt, tot, states, carry, weighted)
                ssm_heads(g, x_tok, bc_t, dt, a_keep, cum, states, cb, spread, decay, mixed, c_scaled)

        def zero_pad(pad):
            with nc.Block() as block:
                @block.vector
                def _(dve):
                    dve_done.mark(nc.vector.memset(pad, 0.0))

        def ssm_states(g, x_tok, b_tok, wgt, tot, states, carry, weighted):
            steps = []
            for n in range(5):
                steps += [(0, (4, 5, 0, 1, 2)[n], n), (1, (5, 4, 3, 2, 1)[n], n)]
            pool0, p0, d0 = pool_done.n, pe_done.n, dve_done.n
            heads = slice(8 * g, 8 * g + 8)
            with nc.Block() as block:
                @block.gpsimd
                def _(pool):
                    for k, (d, t, n) in enumerate(steps):
                        if k >= 2:
                            pool.wait_ge(pe_done.sem, p0 + k - 1)
                        pool_done.mark(nc.gpsimd.tensor_tensor(
                            weighted[:, k % 2].rearrange("p (h n) -> p h n", h=8),
                            x_tok[:, t, g * 512:(g + 1) * 512].rearrange("p (h n) -> p h n", h=8),
                            wgt[:, t, 32 * d + 8 * g:32 * d + 8 * g + 8].unsqueeze(2).broadcast_to([P, 8, HD]), ALU.mult))

                @block.tensor
                def _(pe):
                    for k, (d, t, n) in enumerate(steps):
                        pe.wait_ge(pool_done.sem, pool0 + k + 1)
                        if k >= 2:
                            pe.wait_ge(dve_done.sem, d0 + 2 * (k - 1))
                        pe_done.mark(nc.tensor.matmul(ps[:, k % 2, :], b_tok[:, t, g * P:(g + 1) * P], weighted[:, k % 2],
                                                      start=True, stop=True))

                @block.vector
                def _(dve):
                    def slot(d, n):
                        return carry[d] if n == 0 else states[d][:, n - 1 if d == 0 else 4 - n]
                    for k, (d, t, n) in enumerate(steps):
                        now = slot(d, n)
                        if n == 0:
                            dve_done.mark(nc.vector.memset(now, 0.0))
                        else:
                            if k >= 2:
                                settle(dve, dve_done)
                            dve_done.mark(nc.vector.tensor_tensor(
                                now.rearrange("p (h n) -> p h n", h=8), slot(d, n - 1).rearrange("p (h n) -> p h n", h=8),
                                tot[:, t, 32 * d + 8 * g:32 * d + 8 * g + 8].unsqueeze(2).broadcast_to([P, 8, HD]), ALU.mult))
                        dve.wait_ge(pe_done.sem, p0 + k + 1)
                        settle(dve, dve_done)
                        dve_done.mark(nc.vector.tensor_tensor(now, now, ps[:, k % 2, :], ALU.add))

        ssm_sems = [sem(n) for n in ("sums_done", "spread_done", "diff_done", "decay_done", "mixed_done",
                                     "c_scaled_done", "y_done", "y_kept")]

        def ssm_heads(g, x_tok, bc_t, dt, a_keep, cum, states, cb, spread, decay, mixed, c_scaled):
            sums_done, spread_done, diff_done, decay_done, mixed_done, c_scaled_done, y_done, y_kept = ssm_sems
            n0 = 8 * g
            k0 = 4 * g
            p0, d0 = pe_done.n, dve_done.n
            m0 = mods_before[0]
            mods_before[0] += MOD_IN_SSM

            def mod_tiles(v):
                return range(m0 + MOD_IN_SSM * v // 8, m0 + MOD_IN_SSM * (v + 1) // 8)

            with nc.Block() as block:
                @block.sync
                def _(sp):
                    for m in range(m0, m0 + MOD_IN_SSM):
                        mod_load(sp, m, m % 2)

                @block.tensor
                def _(pe):
                    for t in range(LB):
                        mm = nc.tensor.matmul(ps[:, 6, t * P:(t + 1) * P], bc_t[:, g, t * P:(t + 1) * P],
                                              bc_t[:, 4 + g, t * P:(t + 1) * P], start=True, stop=True)
                    pe_done.mark(mm)

                    def sums(v):
                        if v >= 2:
                            pe.wait_ge(diff_done, n0 + v - 1)
                        for d, m in enumerate(("sum_upto", "sum_from")):
                            for t in range(LB):
                                col = 32 * d + n0 + v
                                mm = nc.tensor.matmul(ps[:, 2 * d + v % 2, t * P:(t + 1) * P],
                                                      a_keep[:, t, col:col + 1].broadcast_to([P, P]), SQ(m),
                                                      start=True, stop=True)
                        mm.then_inc(sums_done, 1)

                    def outputs(v):
                        h_ = n0 + v
                        pe.wait_ge(mixed_done, n0 + v + 1)
                        pe.wait_ge(c_scaled_done, n0 + v + 1)
                        if v >= 4 and v % 2 == 0:
                            pe.wait_ge(y_kept, k0 + v // 2 - 1)
                        rows = slice(64 * (v % 2), 64 * (v % 2) + 64)
                        for t in range(LB):
                            dst = ps[rows, 4 + v // 2 % 2, t * P:(t + 1) * P]
                            cols = slice(t * P, (t + 1) * P)
                            nc.tensor.matmul(dst, x_tok[:, t, h_ * HD:(h_ + 1) * HD], mixed[:, v % 2, cols], start=True, stop=False)
                            nc.tensor.matmul(dst, states[0][:, t, v * HD:(v + 1) * HD], c_scaled[:, v % 2, 0, cols], start=False, stop=False)
                            mm = nc.tensor.matmul(dst, states[1][:, t, v * HD:(v + 1) * HD], c_scaled[:, v % 2, 1, cols], start=False, stop=True)
                        mm.then_inc(y_done, 1)

                    for s in range(10):
                        if s < 8:
                            sums(s)
                        if s >= 2:
                            outputs(s - 2)
                        if s < 8:
                            if s == 0:
                                pe.wait_ge(dve_done.sem, d0 + 1)
                            for m in mod_tiles(s):
                                mod_multiply(pe, m, m % 2, 16 * (m // 2 + 1), m // (2 * NMOD), bank=6)

                @block.scalar
                def _(act):
                    def spreads(v):
                        act.wait_ge(sums_done, n0 + v + 1)
                        if v >= 2:
                            act.wait_ge(c_scaled_done, n0 + v - 1)
                        for d in range(2):
                            ins = nc.scalar.activation(spread[:, v % 2, d], ps[:, 2 * d + v % 2, :], ACT.Exp)
                            if d == 0:
                                act_done.mark(ins)
                        ins.then_inc(spread_done, 1)

                    def decays(v):
                        act.wait_ge(diff_done, n0 + v + 1)
                        nc.scalar.activation(decay[:, v % 2], decay[:, v % 2], ACT.Exp).then_inc(decay_done, 1)

                    def keep(v):
                        act.wait_ge(y_done, n0 + v + 1)
                        cc = (n0 + v) // 2
                        nc.scalar.activation(x_tok[:, 0:LB, cc * P:(cc + 1) * P],
                                             ps[:, 4 + v // 2 % 2, :].rearrange("p (t n) -> p t n", n=P),
                                             ACT.Copy).then_inc(y_kept, 1)

                    for s in range(11):
                        if s < 8:
                            spreads(s)
                        if 1 <= s <= 8:
                            decays(s - 1)
                        if s >= 3 and (s - 3) % 2 == 1:
                            keep(s - 3)

                @block.gpsimd
                def _(pool):
                    for v in range(8):
                        pool.wait_ge(spread_done, n0 + v + 1)
                        if v >= 2:
                            pool.wait_ge(y_done, n0 + v - 1)
                        for d in range(2):
                            ins = nc.gpsimd.tensor_tensor(c_scaled[:, v % 2, d], bc_t[:, 4 + g, 0:LAT], spread[:, v % 2, d], ALU.mult)
                            if d == 0:
                                pool_done.mark(ins)
                        ins.then_inc(c_scaled_done, 1)

                @block.vector
                def _(dve):
                    dve.wait_ge(pe_done.sem, p0 + 1)
                    dve_done.mark(nc.vector.tensor_copy(cb, ps[:, 6, :]))

                    def diffs(v):
                        dve.wait_ge(spread_done, n0 + v + 1)
                        if v >= 2:
                            dve.wait_ge(mixed_done, n0 + v - 1)
                        for d, m in enumerate(("mask_before", "mask_after")):
                            for t in range(LB):
                                col = 32 * d + n0 + v
                                ins = nc.vector.scalar_tensor_tensor(
                                    out=decay[:, v % 2, d, t * P:(t + 1) * P], in0=ps[:, 2 * d + v % 2, t * P:(t + 1) * P],
                                    scalar=cum[:, t, col:col + 1], in1=SQ(m), op0=ALU.subtract, op1=ALU.add)
                        ins.then_inc(diff_done, 1)

                    def mix(v):
                        dve.wait_ge(decay_done, n0 + v + 1)
                        if v >= 2:
                            dve.wait_ge(y_done, n0 + v - 1)
                        h_ = n0 + v
                        for t in range(LB):
                            cols = slice(t * P, (t + 1) * P)
                            dve_done.mark(nc.vector.tensor_scalar(mixed[:, v % 2, cols], decay[:, v % 2, 0, cols],
                                                                  dt[:, t, h_:h_ + 1], None, ALU.mult))
                        settle(dve, dve_done)
                        for t in range(LB):
                            cols = slice(t * P, (t + 1) * P)
                            dve_done.mark(nc.vector.scalar_tensor_tensor(
                                out=mixed[:, v % 2, cols], in0=decay[:, v % 2, 1, cols], scalar=dt[:, t, 32 + h_:33 + h_],
                                in1=mixed[:, v % 2, cols], op0=ALU.mult, op1=ALU.add))
                        settle(dve, dve_done)
                        dve_done.mark(nc.vector.tensor_tensor(mixed[:, v % 2], mixed[:, v % 2], cb, ALU.mult))
                        settle(dve, dve_done)
                        nc.vector.scalar_tensor_tensor(
                            out=mixed[:, v % 2].rearrange("p (t n) -> p t n", n=P),
                            in0=SQ("identity").unsqueeze(1).broadcast_to([P, LB, P]), scalar=skip[:, h_:h_ + 1],
                            in1=mixed[:, v % 2].rearrange("p (t n) -> p t n", n=P), op0=ALU.mult, op1=ALU.add).then_inc(mixed_done, 1)

                    for s in range(9):
                        if s < 8:
                            diffs(s)
                        if s >= 1:
                            for m in mod_tiles(s - 1):
                                mod_keep(dve, m, m % 2, bank=6)
                            mix(s - 1)

        with nc.Block() as block:
            @block.sync
            def _(sp):
                dma_done.mark(sp.dma_start(skip[:], ext["ssm_d"]), 16)
                settle(sp, dma_done)

        def ssm_finish(y_tok):
            with ExitStack() as local:
                z = sb("z", [P, 16, LAT], F32, local)
                stat = sb("stat", [P, 4 * LAT], F32, local)
                zp = z.rearrange("p c n -> p (c n)").bitcast(BF16).rearrange("p (c n) -> p c n", c=16)
                y = lambda c: y_tok[:, 0:LB, c * P:(c + 1) * P]
                r3 = lambda t: t.rearrange("p (t n) -> p t n", n=P)
                linear("ssm_z", *x_parts(x_hi, x_lo), LATENT, keep_chunk(z, LAT), 0)
                p0, a0, d0 = pe_done.n, act_done.n, dve_done.n
                with nc.Block() as block:
                    @block.scalar
                    def _(act):
                        for c in range(17):
                            if c < 16:
                                act_done.mark(nc.scalar.activation(z[:, c], z[:, c], ACT.Silu))
                            if c >= 1:
                                act.wait_ge(dve_done.sem, d0 + c)
                                if c >= 3:
                                    act.wait_ge(pe_done.sem, p0 + c - 2)
                                act_done.mark(nc.scalar.activation(r3(scratch[:, (c - 1) % 2, 0:LAT]), y(c - 1), ACT.Square))

                    @block.vector
                    def _(dve):
                        for c in range(16):
                            dve.wait_ge(act_done.sem, a0 + max(1, 2 * c))
                            dve_done.mark(nc.vector.tensor_tensor(y(c), y(c), r3(z[:, c]), ALU.mult))

                    @block.tensor
                    def _(pe):
                        for c in range(16):
                            pe.wait_ge(act_done.sem, a0 + (2 * c + 3 if c < 15 else 32))
                            pe_done.mark(nc.tensor.matmul(ps[:, c // 4, :], SQ("group_mean"), scratch[:, c % 2, 0:LAT],
                                                          start=(c % 4 == 0), stop=(c % 4 == 3)))
                a0, d0, q0 = act_done.n, dve_done.n, pool_done.n
                r2 = lambda t: t.rearrange("p (b n) -> p b n", b=4)
                turns = w_hi.rearrange("p r n -> p (r n)").bitcast(F32).rearrange("p (u n) -> p u n", u=4)
                with nc.Block() as block:
                    @block.vector
                    def _(dve):
                        dve_done.mark(nc.vector.tensor_scalar(r2(stat), ps[:, 0:4, :], EPS_RMS, None, ALU.add))
                        dve.wait_ge(act_done.sem, a0 + 1)
                        dve_done.mark(nc.vector.reciprocal(stat[:], stat[:]))
                        settle(dve, dve_done)
                        for c in range(16):
                            if c >= 4:
                                dve.wait_ge(pool_done.sem, q0 + c - 3)
                            dve_done.mark(nc.vector.scalar_tensor_tensor(
                                out=r3(turns[:, c % 4]), in0=y(c), scalar=V("ssm_norm_g", c), in1=r3(stat[:, (c // 4) * LAT:(c // 4 + 1) * LAT]),
                                op0=ALU.mult, op1=ALU.mult))

                    @block.scalar
                    def _(act):
                        act.wait_ge(dve_done.sem, d0 + 1)
                        act_done.mark(nc.scalar.activation(stat[:], stat[:], ACT.Sqrt))
                        for c in range(16):
                            act.wait_ge(dve_done.sem, d0 + 3 + c)
                            act_done.mark(nc.scalar.activation(zp[:, c, 0:LAT], turns[:, c % 4], ACT.Copy))

                    @block.gpsimd
                    def _(pool):
                        for c in range(16):
                            pool.wait_ge(act_done.sem, a0 + 2 + c)
                            pool_done.mark(nc.gpsimd.tensor_tensor(zp[:, c, LAT:2 * LAT], turns[:, c % 4], zp[:, c, 0:LAT], ALU.subtract))

                residual_product("ssm_out", lambda k, lo, w: zp[:, k, lo:lo + w], lambda k, lo, w: zp[:, k, LAT + lo:LAT + lo + w],
                                 LATENT, 1, 2, modp)

        def load_and_wait(pairs):
            with nc.Block() as block:
                @block.sync
                def _(sp):
                    for dst, src in pairs:
                        dma_done.mark(sp.dma_start(dst, src), 16)
                    settle(sp, dma_done)

        def unit_rows(tok, blocks, square, sums, scale):
            a0, d0 = act_done.n, dve_done.n
            with nc.Block() as block:
                @block.vector
                def _(dve):
                    for t in range(blocks):
                        settle(dve, dve_done)
                        dve_done.mark(nc.vector.tensor_tensor(square, tok[:, t], tok[:, t], ALU.mult))
                        settle(dve, dve_done)
                        dve_done.mark(nc.vector.tensor_reduce(sums[:, t], square.rearrange("p (h d) -> p h d", d=P), AX.X, ALU.add))
                    settle(dve, dve_done)
                    dve_done.mark(nc.vector.tensor_scalar(sums[:, 0:blocks], sums[:, 0:blocks], EPS, None, ALU.add))
                    dve.wait_ge(act_done.sem, a0 + 1)
                    dve_done.mark(nc.vector.reciprocal(sums[:, 0:blocks], sums[:, 0:blocks]))
                    settle(dve, dve_done)
                    dve_done.mark(nc.vector.tensor_scalar(sums[:, 0:blocks], sums[:, 0:blocks], scale, None, ALU.mult))
                    settle(dve, dve_done)
                    for t in range(blocks):
                        dve_done.mark(nc.vector.tensor_tensor(
                            tok[:, t].rearrange("p (h d) -> p h d", d=P), tok[:, t].rearrange("p (h d) -> p h d", d=P),
                            sums[:, t].unsqueeze(2).broadcast_to([P, DH, P]), ALU.mult))

                @block.scalar
                def _(act):
                    act.wait_ge(dve_done.sem, d0 + 2 * blocks + 1)
                    act_done.mark(nc.scalar.activation(sums[:, 0:blocks], sums[:, 0:blocks], ACT.Sqrt))

        def turn_back(tok, blocks, target):
            p0, a0, d0 = pe_done.n, act_done.n, dve_done.n
            groups = [(t, c) for t in range(blocks) for c in (0, 4)]
            with nc.Block() as block:
                @block.tensor
                def _(pe):
                    for g, (t, c) in enumerate(groups):
                        if g >= 4:
                            pe.wait_ge((act_done, dve_done)[g % 2].sem, (a0, d0)[g % 2] + (g - 4) // 2 + 1)
                        for k in range(4):
                            mm = nc.tensor.transpose(ps[:, g % 4, k * P:(k + 1) * P], tok[:, t, (c + k) * P:(c + k + 1) * P], SQ("identity"))
                        pe_done.mark(mm)

                def view(g):
                    t, c = groups[g]
                    return target[:, c:c + 4, t * P:(t + 1) * P], ps[:, g % 4, :].rearrange("p (c n) -> p c n", c=4)

                @block.scalar
                def _(act):
                    for g in range(0, len(groups), 2):
                        act.wait_ge(pe_done.sem, p0 + g + 1)
                        act_done.mark(nc.scalar.activation(*view(g), ACT.Copy))

                @block.vector
                def _(dve):
                    for g in range(1, len(groups), 2):
                        dve.wait_ge(pe_done.sem, p0 + g + 1)
                        dve_done.mark(nc.vector.tensor_copy(*view(g)))

        delta_sems = [sem(n) for n in ("rows_done", "gap_done", "gap_exp_done", "n_done", "strict_done", "z_begun",
                                       "n_turned", "nt_kept", "first_kept", "t_done", "t_kept", "u_done", "z_kept")]
        state_sems = [sem(n) for n in ("ks_done", "rest_done", "solved", "v_new_done", "v_decayed", "own_done",
                                       "own_added", "o_s_done", "s_next_done", "s_kept", "o_added")]

        def delta_inverse(n, order, qa, z, nt, work, k_t, q_t, gamma, beta, g_cum, step3):
            (rows_done, gap_done, gap_exp_done, n_done, strict_done, z_begun, n_turned, nt_kept, first_kept,
             t_done, t_kept, u_done, z_kept) = delta_sems
            latent = n >= 2
            u0 = 4 * n
            step = [scratch.rearrange("p a n -> p (a n)")[:, i * BANK:(i + 1) * BANK] for i in range(3)] + [step3]
            zt = work.rearrange("p w a n -> p (w a) n")
            masks = h[:, 0:7, LAT:TOK].rearrange("p k (d n) -> p k d n", d=2)

            def quad(zq):
                d = zq // 2
                return d, order[d][n], 4 * (zq % 2)

            def r4(x):
                return x.rearrange("p (q n) -> p q n", q=4)

            with nc.Block() as block:
                @block.tensor
                def _(pe):
                    for zq in range(4):
                        d, t, h0 = quad(zq)
                        w = zq % 2
                        if zq >= 2:
                            pe.wait_ge(n_done, u0 + zq - 1)
                        m = "sum_upto" if d == 0 else "sum_from"
                        for q in range(4):
                            col = 8 * d + h0 + q
                            cols = slice(q * P, (q + 1) * P)
                            tok = slice(t * P, (t + 1) * P)
                            nc.tensor.matmul(ps[:, 3 * w, cols], gamma[:, t, col:col + 1].broadcast_to([P, P]), SQ(m), start=True, stop=True)
                            mm = nc.tensor.matmul(ps[:, 3 * w + 1, cols], k_t[:, h0 + q, tok], k_t[:, h0 + q, tok], start=True, stop=True)
                            if latent:
                                mm = nc.tensor.matmul(ps[:, 3 * w + 2, cols], k_t[:, h0 + q, tok], q_t[:, h0 + q, tok], start=True, stop=True)
                        mm.then_inc(rows_done, 1)
                    for zq in range(4):
                        pe.wait_ge(strict_done, u0 + zq + 1)
                        if zq >= 2:
                            pe.wait_ge(nt_kept, u0 + zq - 1)
                        for q in range(4):
                            mm = nc.tensor.transpose(ps[:, 6 + zq % 2, q * P:(q + 1) * P], zt[:, zq, q * P:(q + 1) * P], SQ("identity"))
                        mm.then_inc(n_turned, 1)
                    pe.wait_ge(n_done, u0 + 4)
                    pe.wait_ge(nt_kept, u0 + 4)
                    for l in range(6):
                        base = 24 * n + 4 * l
                        for zq in range(4):
                            if l == 0:
                                pe.wait_ge(first_kept, u0 + zq + 1)
                            else:
                                pe.wait_ge(z_kept, base - 4 + zq + 1)
                            for q in range(4):
                                cols = slice(q * P, (q + 1) * P)
                                mm = nc.tensor.matmul(ps[:, zq, cols], nt[:, zq, cols], z[:, zq, cols], start=True, stop=True)
                            mm.then_inc(t_done, 1)
                        for zq in range(4):
                            pe.wait_ge(t_kept, base + zq + 1)
                            for q in range(4):
                                cols = slice(q * P, (q + 1) * P)
                                mm = nc.tensor.matmul(ps[:, 4 + zq, cols], zt[:, zq, cols], step[zq][:, cols], start=True, stop=True)
                                if l < 5:
                                    mm = nc.tensor.matmul(ps[:, zq, cols], step[zq][:, cols], zt[:, zq, cols], start=True, stop=True)
                            mm.then_inc(u_done, 1)

                @block.scalar
                def _(act):
                    for zq in range(4):
                        act.wait_ge(gap_done, u0 + zq + 1)
                        nc.scalar.activation(qa[:, zq], qa[:, zq], ACT.Exp).then_inc(gap_exp_done, 1)
                    for zq in range(4):
                        act.wait_ge(n_turned, u0 + zq + 1)
                        nc.scalar.activation(nt[:, zq], ps[:, 6 + zq % 2, :], ACT.Copy).then_inc(nt_kept, 1)

                @block.gpsimd
                def _(pool):
                    for zq in range(4):
                        d = zq // 2
                        pool.wait_ge(n_done, u0 + zq + 1)
                        strict = SQ("strict_upper" if d == 0 else "strict_lower").unsqueeze(1).broadcast_to([P, 4, P])
                        nc.gpsimd.tensor_tensor(r4(zt[:, zq]), r4(zt[:, zq]), strict, ALU.mult).then_inc(strict_done, 1)
                        pool.wait_ge(strict_done, u0 + zq + 1)
                        pairs = masks[:, 6, d].unsqueeze(1).broadcast_to([P, 4, P])
                        pool_done.mark(nc.gpsimd.tensor_tensor(r4(z[:, zq]), r4(zt[:, zq]), pairs, ALU.mult))
                        settle(pool, pool_done)
                        nc.gpsimd.tensor_tensor(r4(z[:, zq]), r4(z[:, zq]), SQ("identity").unsqueeze(1).broadcast_to([P, 4, P]),
                                                ALU.add).then_inc(z_begun, 1)
                @block.vector
                def _(dve):
                    def gaps(zq):
                        d, t, h0 = quad(zq)
                        dve.wait_ge(rows_done, u0 + zq + 1)
                        mask = SQ("mask_before" if d == 0 else "mask_after")
                        for q in range(4):
                            col = 8 * d + h0 + q
                            cols = slice(q * P, (q + 1) * P)
                            ins = nc.vector.scalar_tensor_tensor(out=qa[:, zq, cols], in0=ps[:, 3 * (zq % 2), cols], scalar=g_cum[:, t, col:col + 1],
                                                                 in1=mask, op0=ALU.subtract, op1=ALU.add)
                            if q < 3:
                                dve_done.mark(ins)
                        ins.then_inc(gap_done, 1)

                    def products(zq):
                        d, t, h0 = quad(zq)
                        dve.wait_ge(gap_exp_done, u0 + zq + 1)
                        for q in range(4):
                            col = 8 * d + h0 + q
                            cols = slice(q * P, (q + 1) * P)
                            dve_done.mark(nc.vector.scalar_tensor_tensor(
                                out=zt[:, zq, cols], in0=ps[:, 3 * (zq % 2) + 1, cols], scalar=beta[:, t, col:col + 1],
                                in1=qa[:, zq, cols], op0=ALU.mult, op1=ALU.mult))
                        settle(dve, dve_done)
                        src = ps[:, 3 * (zq % 2) + 2, :] if latent else qa[:, zq]
                        nc.vector.tensor_tensor(qa[:, zq], qa[:, zq], src, ALU.mult).then_inc(n_done, 1)

                    def first_transpose(zq):
                        d = zq // 2
                        dve.wait_ge(nt_kept, u0 + zq + 1)
                        dve.wait_ge(z_begun, u0 + zq + 1)
                        pairs = masks[:, 6, 1 - d].unsqueeze(1).broadcast_to([P, 4, P])
                        dve_done.mark(nc.vector.tensor_tensor(r4(zt[:, zq]), r4(nt[:, zq]), pairs, ALU.mult))
                        settle(dve, dve_done)
                        nc.vector.tensor_tensor(r4(zt[:, zq]), r4(zt[:, zq]), SQ("identity").unsqueeze(1).broadcast_to([P, 4, P]),
                                                ALU.add).then_inc(first_kept, 1)

                    for pair in (0, 2):
                        for zq in (pair, pair + 1):
                            gaps(zq)
                        for zq in (pair, pair + 1):
                            products(zq)
                    for zq in range(4):
                        first_transpose(zq)
                    for l in range(6):
                        base = 24 * n + 4 * l
                        for zq in range(4):
                            dve.wait_ge(t_done, base + zq + 1)
                            nc.vector.tensor_tensor(r4(step[zq]), r4(ps[:, zq, :]),
                                                    masks[:, l, zq // 2].unsqueeze(1).broadcast_to([P, 4, P]), ALU.mult).then_inc(t_kept, 1)
                        for zq in range(4):
                            dve.wait_ge(u_done, base + zq + 1)
                            if l < 5:
                                dve_done.mark(nc.vector.tensor_tensor(zt[:, zq], zt[:, zq], ps[:, zq, :], ALU.subtract))
                            nc.vector.tensor_tensor(z[:, zq], z[:, zq], ps[:, 4 + zq, :], ALU.subtract).then_inc(z_kept, 1)

        def delta_states(n, order, qa, z, work, s_all, k_t, q_t, kv_tok, o_tok, small):
            ks_done, rest_done, solved, v_new_done, v_decayed, own_done, own_added, o_s_done, s_next_done, s_kept, o_added = state_sems
            beta, neg_eg, eg, e_tot, e_gap = small
            latent = n >= 2
            last = n == 5
            u0 = 4 * n
            l0 = 4 * (n - 2)
            with nc.Block() as block:
                def quad(zq):
                    d = zq // 2
                    return d, order[d][n], 4 * (zq % 2)

                @block.tensor
                def _(pe):
                    def old_state(zq):
                        d, t, h0 = quad(zq)
                        if zq >= 2:
                            pe.wait_ge(rest_done, u0 + zq - 1)
                        for q in range(4):
                            s = s_all[:, d, (h0 + q) * P:(h0 + q + 1) * P]
                            mm = nc.tensor.matmul(ps[:, zq % 2, q * P:(q + 1) * P], k_t[:, h0 + q, t * P:(t + 1) * P], s, start=True, stop=True)
                        mm.then_inc(ks_done, 1)
                        if latent:
                            if zq >= 1:
                                pe.wait_ge(o_added, l0 + zq)
                            for q in range(4):
                                s = s_all[:, d, (h0 + q) * P:(h0 + q + 1) * P]
                                mm = nc.tensor.matmul(ps[:, 4, q * P:(q + 1) * P], q_t[:, h0 + q, t * P:(t + 1) * P], s, start=True, stop=True)
                            mm.then_inc(o_s_done, 1)

                    def solve(zq):
                        pe.wait_ge(rest_done, u0 + zq + 1)
                        if zq >= 2:
                            pe.wait_ge(v_new_done, u0 + zq - 1)
                        for q in range(4):
                            cols = slice(q * P, (q + 1) * P)
                            mm = nc.tensor.matmul(ps[:, 2 + zq % 2, cols], z[:, zq, cols], work[:, zq % 2, 0, cols], start=True, stop=True)
                        mm.then_inc(solved, 1)

                    def new_state(zq):
                        d, t, h0 = quad(zq)
                        if latent:
                            pe.wait_ge(v_new_done, u0 + zq + 1)
                            if zq >= 1:
                                pe.wait_ge(own_added, l0 + zq)
                            for q in range(4):
                                cols = slice(q * P, (q + 1) * P)
                                mm = nc.tensor.matmul(ps[:, 5, cols], qa[:, zq, cols], work[:, zq % 2, 0, cols], start=True, stop=True)
                            mm.then_inc(own_done, 1)
                        if not last:
                            pe.wait_ge(v_decayed, u0 + zq + 1)
                            if zq >= 2:
                                pe.wait_ge(s_kept, u0 + zq - 1)
                            for q in range(4):
                                cols = slice(q * P, (q + 1) * P)
                                mm = nc.tensor.matmul(ps[:, 6 + zq % 2, cols], kv_tok[:, t, (h0 + q) * P:(h0 + q + 1) * P],
                                                      work[:, zq % 2, 1, cols], start=True, stop=True)
                            mm.then_inc(s_next_done, 1)

                    for s in range(6):
                        if s < 4:
                            old_state(s)
                        if 1 <= s <= 4:
                            solve(s - 1)
                        if s >= 2:
                            new_state(s - 2)

                @block.gpsimd
                def _(pool):
                    if last:
                        return
                    for zq in range(4):
                        d, t, h0 = quad(zq)
                        pool.wait_ge(v_new_done, u0 + zq + 1)
                        if zq >= 2:
                            pool.wait_ge(s_next_done, u0 + zq - 1)
                        nc.gpsimd.tensor_tensor(
                            work[:, zq % 2, 1].rearrange("p (q n) -> p q n", q=4), work[:, zq % 2, 0].rearrange("p (q n) -> p q n", q=4),
                            e_gap[:, t, 8 * d + h0:8 * d + h0 + 4].unsqueeze(2).broadcast_to([P, 4, P]), ALU.mult).then_inc(v_decayed, 1)

                @block.vector
                def _(dve):
                    def rest(zq):
                        d, t, h0 = quad(zq)
                        dve.wait_ge(ks_done, u0 + zq + 1)
                        if zq >= 2:
                            if latent:
                                dve.wait_ge(own_done, l0 + zq - 1)
                            if not last:
                                dve.wait_ge(v_decayed, u0 + zq - 1)
                        for q in range(4):
                            cols = slice(q * P, (q + 1) * P)
                            col = 8 * d + h0 + q
                            ins = nc.vector.scalar_tensor_tensor(
                                out=work[:, zq % 2, 0, cols], in0=ps[:, zq % 2, cols], scalar=neg_eg[:, t, col:col + 1],
                                in1=kv_tok[:, t, D + (h0 + q) * P:D + (h0 + q + 1) * P], op0=ALU.mult, op1=ALU.add)
                            if q < 3:
                                dve_done.mark(ins)
                        ins.then_inc(rest_done, 1)
                        if latent:
                            dve.wait_ge(o_s_done, l0 + zq + 1)
                            for q in range(4):
                                col = 8 * d + h0 + q
                                o = o_tok[:, t, (h0 + q) * P:(h0 + q + 1) * P]
                                ins = nc.vector.scalar_tensor_tensor(out=o, in0=ps[:, 4, q * P:(q + 1) * P], scalar=eg[:, t, col:col + 1],
                                                                     in1=o, op0=ALU.mult, op1=ALU.add)
                                if q < 3:
                                    dve_done.mark(ins)
                            ins.then_inc(o_added, 1)

                    def fresh(zq):
                        d, t, h0 = quad(zq)
                        dve.wait_ge(solved, u0 + zq + 1)
                        nc.vector.tensor_tensor(
                            work[:, zq % 2, 0].rearrange("p (q n) -> p q n", q=4), ps[:, 2 + zq % 2, :].rearrange("p (q n) -> p q n", q=4),
                            beta[:, t, 8 * d + h0:8 * d + h0 + 4].unsqueeze(2).broadcast_to([P, 4, P]), ALU.mult).then_inc(v_new_done, 1)

                    def add(zq):
                        d, t, h0 = quad(zq)
                        if latent:
                            dve.wait_ge(own_done, l0 + zq + 1)
                            dve.wait_ge(o_added, l0 + zq + 1)
                            o = o_tok[:, t, h0 * P:(h0 + 4) * P]
                            nc.vector.tensor_tensor(o, o, ps[:, 5, :], ALU.add).then_inc(own_added, 1)
                        if not last:
                            dve.wait_ge(s_next_done, u0 + zq + 1)
                            for q in range(4):
                                col = 8 * d + h0 + q
                                s = s_all[:, d, (h0 + q) * P:(h0 + q + 1) * P]
                                ins = nc.vector.scalar_tensor_tensor(out=s, in0=s, scalar=e_tot[:, t, col:col + 1],
                                                                     in1=ps[:, 6 + zq % 2, q * P:(q + 1) * P], op0=ALU.mult, op1=ALU.add)
                                if q < 3:
                                    dve_done.mark(ins)
                            ins.then_inc(s_kept, 1)

                    for s in range(6):
                        if s < 4:
                            rest(s)
                        if 1 <= s <= 4:
                            fresh(s - 1)
                        if s >= 2:
                            add(s - 2)

        def deltanet():
            x_words = x_all.rearrange("p a k n -> p (a k n)").bitcast(F32)
            o_tok = x_words[:, 0:4096].rearrange("p (t n) -> p t n", t=LB)
            s_all = x_words[:, 4096:6144].rearrange("p (d n) -> p d n", d=2)
            rows_kv = [(64 * r, 64) for r in range(8)]
            with ExitStack() as local:
                kv_tok = sb("kv_tok", [P, TB, 2 * D], F32, local)
                small_all = sb("small_all", [P, 8, TB, 16], F32, local)
                beta, gamma, g_cum, g_tot, eg, neg_eg, e_tot, e_gap = (small_all[:, i] for i in range(8))
                ba = sb("ba", [P, TB, 32], F32, local)
                ba_rows = sb("ba_rows", [P, 32], F32, local)
                sums = sb("sums", [P, TB, DH], F32, local)

                def project(name, target, chunk0, segments, rows):
                    layout, width = pad_layout(rows)
                    with ExitStack() as inner:
                        pad = sb(name + "_pad", [P, width], F32, inner)
                        acc = sb(name + "_acc", [P, width], F32, inner)
                        zero_pad(pad[:])
                        linear(name, *x_parts(x_hi, x_lo), segments,
                               convolve(pad, acc, target, layout, width, "dn_conv_w", 24, chunk0, None),
                               per_conv(len(segments)))

                with ExitStack() as inner:
                    v_t = sb("v_t", [P, DH, TOK], F32, inner)
                    project("dn_v", v_t, 16, BOTH, rows_kv + [(LAT, CTX)])
                    silu_and_turn(v_t, DH, kv_tok[:, :, D:], DH)
                k_t = sb("k_t", [P, DH, TOK], F32, local)
                project("dn_k", k_t, 8, BOTH, rows_kv + [(LAT, CTX)])
                silu_and_turn(k_t, DH, kv_tok[:, :, 0:D], DH)
                flat = scratch.rearrange("p a n -> p (a n)")
                square = flat[:, 0:D]
                unit_rows(kv_tok[:, :, 0:D], TB, square, sums, 1.0)
                turn_back(kv_tok[:, :, 0:D], TB, k_t)
                q_t = sb("q_t", [P, DH, LAT], F32, local)
                linear("dn_gate", *x_parts(x_hi, x_lo), LATENT, keep_chunk(q_t, LAT), 0)
                load_and_wait([(gate_store, q_t[:])])
                project("dn_q", q_t, 0, LATENT, rows_kv)
                with ExitStack() as inner:
                    q_tok = sb("q_tok", [P, LB, D], F32, inner)
                    silu_and_turn_latent(q_t, q_tok)
                    unit_rows(q_tok[:], LB, square, sums, P ** -0.5)
                    turn_back(q_tok, LB, q_t)
                wf = flat[:, 0:256].rearrange("p (k n) -> p k n", k=KC)
                wh = flat[:, 256:384].bitcast(BF16).rearrange("p (k n) -> p k n", k=KC)
                wl = flat[:, 384:512].bitcast(BF16).rearrange("p (k n) -> p k n", k=KC)
                small_product(ext["ba_w"], 32, wf, wh, wl, ba[:])
                load_and_wait([(ba_rows[:], ext["ba_rows"])])
                a0 = act_done.n
                with nc.Block() as block:
                    @block.scalar
                    def _(act):
                        act_done.mark(nc.scalar.activation(beta, ba[:, :, 0:16], ACT.Sigmoid))
                        act_done.mark(nc.scalar.activation(ba_rows[:, 16:32], ba_rows[:, 16:32], ACT.Exp))

                    @block.vector
                    def _(dve):
                        dve_done.mark(nc.vector.tensor_tensor(gamma, ba[:, :, 16:32], ba_rows[:, 0:16].unsqueeze(1).broadcast_to([P, TB, 16]), ALU.add))
                        dve.wait_ge(act_done.sem, a0 + 2)
                        dve_done.mark(nc.vector.tensor_scalar(ba_rows[:, 16:32], ba_rows[:, 16:32], -1.0, None, ALU.mult))
                softplus(gamma, [flat[:, 96 * q:96 * q + 96].rearrange("p (t n) -> p t n", n=16) for q in range(4)])
                p0, d0 = pe_done.n, dve_done.n
                with nc.Block() as block:
                    @block.vector
                    def _(dve):
                        dve_done.mark(nc.vector.tensor_tensor(gamma, gamma, ba_rows[:, 16:32].unsqueeze(1).broadcast_to([P, TB, 16]), ALU.mult))
                        dve.wait_ge(pe_done.sem, p0 + 1)
                        dve_done.mark(nc.vector.tensor_copy(g_cum, ps[:, 0, 0:96].rearrange("p (t n) -> p t n", n=16)))
                        dve_done.mark(nc.vector.tensor_copy(g_tot, ps[:, 1, 0:96].rearrange("p (t n) -> p t n", n=16)))
                        settle(dve, dve_done)
                        dve_done.mark(nc.vector.tensor_tensor(e_gap, g_tot, g_cum, ALU.subtract))
                        dve_done.mark(nc.vector.memset(o_tok, 0.0))
                        dve_done.mark(nc.vector.memset(s_all, 0.0))

                    @block.tensor
                    def _(pe):
                        pe.wait_ge(dve_done.sem, d0 + 1)
                        for t in range(TB):
                            for d, m in enumerate(("sum_upto", "sum_from")):
                                nc.tensor.matmul(ps[:, 0, t * 16 + 8 * d:t * 16 + 8 * d + 8], SQ(m), gamma[:, t, 8 * d:8 * d + 8], start=True, stop=True)
                        pe_done.mark(nc.tensor.matmul(ps[:, 1, 0:96], SQ("ones"), gamma.rearrange("p t n -> p (t n)"), start=True, stop=True))
                a0 = act_done.n
                with nc.Block() as block:
                    @block.scalar
                    def _(act):
                        act_done.mark(nc.scalar.activation(eg, g_cum, ACT.Exp))
                        act_done.mark(nc.scalar.activation(e_tot, g_tot, ACT.Exp))
                        act_done.mark(nc.scalar.activation(e_gap, e_gap, ACT.Exp))

                    @block.vector
                    def _(dve):
                        dve.wait_ge(act_done.sem, a0 + 1)
                        dve_done.mark(nc.vector.tensor_scalar(neg_eg, eg, -1.0, None, ALU.mult))

                qa = sb("qa", [P, 4, BANK], F32, local)
                z = sb("z_inv", [P, 4, BANK], F32, local)
                nt = w_hi.rearrange("p r n -> p (r n)").bitcast(F32).rearrange("p (u n) -> p u n", u=4)
                work = w_lo.rearrange("p r n -> p (r n)").bitcast(F32).rearrange("p (w a n) -> p w a n", w=2, a=2)
                order = ((4, 5, 0, 1, 2, 3), (5, 4, 3, 2, 1, 0))
                load_and_wait([(h[:, 0:7, LAT:TOK], ext["level_masks"])])
                step3 = sb("step3", [P, BANK], F32, local)
                for n in range(6):
                    delta_inverse(n, order, qa, z, nt, work, k_t, q_t, gamma, beta, g_cum, step3[:])
                    delta_states(n, order, qa, z, work, s_all, k_t, q_t, kv_tok, o_tok, (beta, neg_eg, eg, e_tot, e_gap))
            with ExitStack() as local:
                gate = sb("gate", [P, KC, LAT], F32, local)
                o_t = sb("o_t", [P, KC, LAT], F32, local)
                sums = sb("sums2", [P, LB, DH], F32, local)
                flat = scratch.rearrange("p a n -> p (a n)")
                rms_rows(o_tok, flat[:, 0:D], sums)
                load_and_wait([(gate[:], gate_store)])
                turn_back(o_tok, LB, o_t)
                a0, d0 = act_done.n, dve_done.n
                with nc.Block() as block:
                    @block.scalar
                    def _(act):
                        act_done.mark(nc.scalar.activation(gate[:], gate[:], ACT.Silu))
                        for k in range(KC):
                            act.wait_ge(dve_done.sem, d0 + 2 * k + 1)
                            act_done.mark(nc.scalar.activation(x_hi[:, k, 0:LAT], o_t[:, k], ACT.Copy))

                    @block.vector
                    def _(dve):
                        dve.wait_ge(act_done.sem, a0 + 1)
                        for k in range(KC):
                            dve_done.mark(nc.vector.scalar_tensor_tensor(out=o_t[:, k], in0=o_t[:, k], scalar=V("dn_norm_g"),
                                                                         in1=gate[:, k], op0=ALU.mult, op1=ALU.mult))
                            dve.wait_ge(act_done.sem, a0 + k + 2)
                            dve_done.mark(nc.vector.tensor_tensor(x_lo[:, k, 0:LAT], o_t[:, k], x_hi[:, k, 0:LAT], ALU.subtract))
            residual_product("dn_out", *x_parts(x_hi, x_lo), LATENT, 2, 2, mods)

        def rms_rows(tok, square, sums):
            a0, d0 = act_done.n, dve_done.n
            with nc.Block() as block:
                @block.vector
                def _(dve):
                    for t in range(LB):
                        settle(dve, dve_done)
                        dve_done.mark(nc.vector.tensor_tensor(square, tok[:, t], tok[:, t], ALU.mult))
                        settle(dve, dve_done)
                        dve_done.mark(nc.vector.tensor_reduce(sums[:, t], square.rearrange("p (h d) -> p h d", d=P), AX.X, ALU.add))
                    settle(dve, dve_done)
                    dve_done.mark(nc.vector.tensor_scalar(sums[:], sums[:], 1.0 / P, EPS, ALU.mult, ALU.add))
                    dve.wait_ge(act_done.sem, a0 + 1)
                    dve_done.mark(nc.vector.reciprocal(sums[:], sums[:]))
                    settle(dve, dve_done)
                    for t in range(LB):
                        r3 = tok[:, t].rearrange("p (h d) -> p h d", d=P)
                        dve_done.mark(nc.vector.tensor_tensor(r3, r3, sums[:, t].unsqueeze(2).broadcast_to([P, DH, P]), ALU.mult))

                @block.scalar
                def _(act):
                    act.wait_ge(dve_done.sem, d0 + 2 * LB + 1)
                    act_done.mark(nc.scalar.activation(sums[:], sums[:], ACT.Sqrt))

        def silu_and_turn_latent(source, target):
            a0, p0, d0 = act_done.n, pe_done.n, dve_done.n
            with nc.Block() as block:
                @block.scalar
                def _(act):
                    for c in range(DH):
                        act_done.mark(nc.scalar.activation(source[:, c, :], source[:, c, :], ACT.Silu))

                @block.tensor
                def _(pe):
                    for c in range(DH):
                        pe.wait_ge(act_done.sem, a0 + c + 1)
                        if c >= 4:
                            pe.wait_ge(dve_done.sem, d0 + c - 3)
                        for t in range(LB):
                            mm = nc.tensor.transpose(ps[:, c % 4, t * P:(t + 1) * P], source[:, c, t * P:(t + 1) * P], SQ("identity"))
                        pe_done.mark(mm)

                @block.vector
                def _(dve):
                    for c in range(DH):
                        dve.wait_ge(pe_done.sem, p0 + c + 1)
                        dve_done.mark(nc.vector.tensor_copy(target[:, :, c * P:(c + 1) * P], ps[:, c % 4, :].rearrange("p (t n) -> p t n", n=P)))

        def peer():
            normalise(LAT, EPS, False, "norm_g1", then=(2, 3))
            with ExitStack() as local:
                picks = sb("picks", [P, 3, LAT], F32, local)
                with ExitStack() as inner:
                    s_tok = sb("s_tok", [P, LB, 2 * DH, P], F32, inner)
                    with ExitStack() as product:
                        keys = sb("keys", [P, 2 * DH, P], F32, product)
                        q_t = sb("pq_t", [P, 2 * DH, LAT], F32, product)
                        load_and_wait([(keys[:], ext["keys"].rearrange("d h p k -> d (h p) k"))])
                        linear("w_q", *x_parts(x_hi, x_lo), LATENT, keep_chunk(q_t, LAT), 0)
                        p0, a0 = pe_done.n, act_done.n
                        groups = [(t, c) for t in range(LB) for c in range(0, 16, 4)]
                        with nc.Block() as block:
                            @block.tensor
                            def _(pe):
                                for g, (t, c) in enumerate(groups):
                                    if g >= 4:
                                        pe.wait_ge(act_done.sem, a0 + g - 3)
                                    for q in range(4):
                                        mm = nc.tensor.matmul(ps[:, g % 4, q * P:(q + 1) * P], q_t[:, c + q, t * P:(t + 1) * P],
                                                              keys[:, c + q, :], start=True, stop=True)
                                    pe_done.mark(mm)

                            @block.scalar
                            def _(act):
                                for g, (t, c) in enumerate(groups):
                                    act.wait_ge(pe_done.sem, p0 + g + 1)
                                    act_done.mark(nc.scalar.activation(s_tok[:, t, c:c + 4, :].rearrange("p c n -> p (c n)"),
                                                                       ps[:, g % 4, :], ACT.Copy))
                    choose(inner, s_tok, picks)
                spread_gates(local, picks)
            with ExitStack() as local:
                y_sum = sb("y_sum", [P, KC, LAT], F32, local)
                experts(y_sum)
                with nc.Block() as block:
                    @block.vector
                    def _(dve):
                        for k in range(KC):
                            dve_done.mark(nc.vector.scalar_tensor_tensor(out=h[:, k, 0:LAT], in0=y_sum[:, k], scalar=mods[:, 2, 5 * KC + k, 0:1],
                                                                         in1=h[:, k, 0:LAT], op0=ALU.mult, op1=ALU.add))
            with ExitStack() as local:
                result = sb("result", [P, KC, LAT], F32, local)
                normalise(LAT, EPS, False, "final_g", keep=result)
                with nc.Block() as block:
                    @block.sync
                    def _(sp):
                        dma_done.mark(sp.dma_start(out.rearrange("k p t -> p k t"), result[:]), 16)
                        settle(sp, dma_done)

        def choose(stack, s_tok, picks):
            top = sb("top16", [P, 2 * DH, PICKS], F32, stack)
            at = sb("at16", [P, 2 * DH, PICKS], U32, stack)
            at_f = sb("at16f", [P, 2 * DH, PICKS], F32, stack)
            cand = sb("cand", [P, DH, PICKS * PICKS], F32, stack)
            best = sb("best", [P, DH, PICKS], F32, stack)
            pos = sb("pos", [P, DH, PICKS], U32, stack)
            half = sb("half", [P, 2, DH, PICKS], U32, stack)
            half_f = sb("half_f", [P, 2, DH, PICKS], F32, stack)
            eq = sb("eq", [P, 2, DH, PICKS, PICKS], F32, stack)
            three = sb("three", [P, LB, 3, P], F32, stack)
            total = sb("total", [P, DH], F32, stack)
            a0, d0, p0, q0 = act_done.n, dve_done.n, pe_done.n, pool_done.n
            exps, matches = [], []
            with nc.Block() as block:
                @block.vector
                def _(dve):
                    def top16(values, n, out_v, out_i):
                        for lo in (0, 8):
                            for c in range(n):
                                dve_done.mark(nc.vector.max(out_v[:, c, lo:lo + 8], values[:, c, :]))
                            settle(dve, dve_done)
                            for c in range(n):
                                dve_done.mark(nc.vector.max_index(out_i[:, c, lo:lo + 8], out_v[:, c, lo:lo + 8], values[:, c, :]))
                            settle(dve, dve_done)
                            if lo == 0:
                                for c in range(n):
                                    dve_done.mark(nc.vector.match_replace(values[:, c, :], out_v[:, c, 0:8], values[:, c, :], -3e38))
                                settle(dve, dve_done)

                    def keep_indices(t):
                        for s in range(2):
                            dve.wait_ge(pool_done.sem, q0 + 2 * t + s + 1)
                            dve_done.mark(nc.vector.tensor_reduce(three[:, t, s].rearrange("p (h j) -> p h j", h=DH), eq[:, s], AX.X, ALU.add))

                    for t in range(LB):
                        top16(s_tok[:, t], 2 * DH, top, at)
                        if t > 0:
                            keep_indices(t - 1)
                            settle(dve, dve_done)
                        dve_done.mark(nc.vector.tensor_copy(at_f[:], at[:]))
                        by_head = top.rearrange("p (h s) j -> p h s j", s=2)
                        dve_done.mark(nc.vector.tensor_tensor(
                            cand.rearrange("p h (a b) -> p h a b", a=PICKS),
                            by_head[:, :, 0, :].unsqueeze(3).broadcast_to([P, DH, PICKS, PICKS]),
                            by_head[:, :, 1, :].unsqueeze(2).broadcast_to([P, DH, PICKS, PICKS]), ALU.add))
                        settle(dve, dve_done)
                        top16(cand, DH, best, pos)
                        g = three[:, t, 2].rearrange("p (h j) -> p h j", h=DH)
                        dve_done.mark(nc.vector.tensor_tensor(g, best[:], best[:, :, 0:1].broadcast_to([P, DH, PICKS]), ALU.subtract))
                        exps.append(dve_done.n)
                        dve_done.mark(nc.vector.tensor_scalar(half[:, 0], pos[:], 4, None, ALU.logical_shift_right))
                        dve_done.mark(nc.vector.tensor_scalar(half[:, 1], pos[:], 15, None, ALU.bitwise_and))
                        settle(dve, dve_done)
                        dve_done.mark(nc.vector.tensor_copy(half_f[:], half[:]))
                        settle(dve, dve_done)
                        for s in range(2):
                            dve_done.mark(nc.vector.tensor_tensor(
                                eq[:, s], half_f[:, s].unsqueeze(3).broadcast_to([P, DH, PICKS, PICKS]),
                                SQ("iota")[:, 0:PICKS].unsqueeze(1).unsqueeze(1).broadcast_to([P, DH, PICKS, PICKS]), ALU.is_equal))
                            matches.append(dve_done.n)
                        dve.wait_ge(act_done.sem, a0 + t + 1)
                        dve_done.mark(nc.vector.tensor_reduce(total[:], g, AX.X, ALU.add))
                        settle(dve, dve_done)
                        dve_done.mark(nc.vector.reciprocal(total[:], total[:]))
                        settle(dve, dve_done)
                        dve_done.mark(nc.vector.tensor_tensor(g, g, total[:].unsqueeze(2).broadcast_to([P, DH, PICKS]), ALU.mult))
                        settle(dve, dve_done)
                    keep_indices(LB - 1)

                @block.gpsimd
                def _(pool):
                    for t in range(LB):
                        for s in range(2):
                            pool.wait_ge(dve_done.sem, matches[2 * t + s])
                            pool_done.mark(nc.gpsimd.tensor_tensor(
                                eq[:, s], eq[:, s], at_f.rearrange("p (h s) j -> p h s j", s=2)[:, :, s, :].unsqueeze(2).broadcast_to(
                                    [P, DH, PICKS, PICKS]), ALU.mult))

                @block.scalar
                def _(act):
                    for t in range(LB):
                        act.wait_ge(dve_done.sem, exps[t])
                        act_done.mark(nc.scalar.activation(three[:, t, 2], three[:, t, 2], ACT.Exp))

            d1 = dve_done.n
            with nc.Block() as block:
                @block.tensor
                def _(pe):
                    for s in range(3):
                        for t in range(LB):
                            mm = nc.tensor.transpose(ps[:, s, t * P:(t + 1) * P], three[:, t, s, :], SQ("identity"))
                        pe_done.mark(mm)

                @block.vector
                def _(dve):
                    for s in range(3):
                        dve.wait_ge(pe_done.sem, p0 + s + 1)
                        dve_done.mark(nc.vector.tensor_copy(picks[:, s, :], ps[:, s, :]))

        def spread_gates(stack, picks):
            onehot_ready, gated, onehot_free, bank_free, *stored = (
                sem(n) for n in ("onehot_ready", "rows_gated", "onehot_free", "gate_bank_free", "gates_stored0", "gates_stored1"))
            hot = sb("hot", [P, 2, 16, P], F32, stack)
            k1_hot, k2_hot = hot[:, 0], hot[:, 1]
            dense = [sb(f"dense{b}", [P, P, BLOCK], F32, stack) for b in range(2)]
            per = 2 * BLOCK // 4
            bodies = LAT // (2 * BLOCK)
            with nc.Block() as block:
                @block.vector
                def _(dve):
                    nc.vector.memset(k1_hot[:, 0, 0:1], 0.0).then_inc(onehot_free, 4)
                    nc.vector.memset(k1_hot[:, 1, 0:1], 0.0).then_inc(bank_free, 4)
                    for b in range(2):
                        nc.vector.memset(k1_hot[:, 2 + b, 0:1], 0.0).then_inc(stored[b], 16)
            with nc.Block() as block:
                @block.vector
                def _(dve):
                    with dve.Fori(0, bodies) as i:
                        for g in range(per):
                            slot, t0 = 4 * (g % 4), i * (2 * BLOCK) + 4 * g
                            dve.wait_ge(onehot_free, i * per + (g + 1))
                            for e in range(2):
                                nc.vector.tensor_tensor(hot[:, e, slot:slot + 4, :], SQ("iota").unsqueeze(1).broadcast_to([P, 4, P]),
                                                        picks[:, e, bass.ds(t0, 4)].unsqueeze(2).broadcast_to([P, 4, P]),
                                                        ALU.is_equal).then_inc(onehot_ready, 1)

                @block.gpsimd
                def _(pool):
                    with pool.Fori(0, bodies) as i:
                        for g in range(per):
                            slot, t0 = 4 * (g % 4), i * (2 * BLOCK) + 4 * g
                            pool.wait_ge(onehot_ready, i * (per * 2) + (g * 2 + 2))
                            nc.gpsimd.tensor_tensor(k2_hot[:, slot:slot + 4, :], k2_hot[:, slot:slot + 4, :],
                                                    picks[:, 2, bass.ds(t0, 4)].unsqueeze(2).broadcast_to([P, 4, P]),
                                                    ALU.mult).then_inc(gated, 1)

                @block.tensor
                def _(pe):
                    with pe.Fori(0, bodies) as i:
                        for g in range(per):
                            pe.wait_ge(gated, i * per + (g + 1))
                            pe.wait_ge(bank_free, i * per + (g + 1))
                            for q in range(4):
                                mm = nc.tensor.matmul(ps[:, g % 4, q * P:(q + 1) * P], k1_hot[:, 4 * (g % 4) + q, :],
                                                      k2_hot[:, 4 * (g % 4) + q, :], start=True, stop=True)
                            mm.then_inc(onehot_free, 1)

                @block.scalar
                def _(act):
                    with act.Fori(0, bodies) as i:
                        for g in range(per):
                            b, at = g // (per // 2), g % (per // 2)
                            if at == 0:
                                act.wait_ge(stored[b], i * 16 + 16)
                            act.wait_ge(onehot_free, i * per + (g + 5))
                            nc.scalar.activation(dense[b][:, :, 4 * at:4 * at + 4], ps[:, g % 4, :].rearrange("p (t k) -> p k t", t=4),
                                                 ACT.Copy).then_inc(bank_free, 1)

                @block.sync
                def _(sp):
                    with sp.Fori(0, bodies) as i:
                        for b in range(2):
                            sp.wait_ge(bank_free, i * per + (4 + (b + 1) * (per // 2)))
                            sp.dma_start(expert_gates[i * 2 + b], dense[b][:]).then_inc(stored[b], 16)
                    for b in range(2):
                        sp.wait_ge(stored[b], 16 + 16 * bodies)

        def experts(y_sum):
            base = starts["experts"]
            n_groups = EXPERT_TILES // GROUP
            v_ready = [sem(f"v_ready{j}") for j in range(GROUP)]
            gates_ready = [sem(f"gates_ready{b}") for b in range(2)]
            v_hi_done, v_split, gelu_done, weighed, coef_hi_done, coef_done, y_done, y_added = (
                sem(n) for n in ("v_hi_done", "v_split", "gelu_done", "weighed", "coef_hi_done", "coef_done", "ey_done", "y_added"))
            with ExitStack() as local:
                v_raw = sb("v_raw", [P, GROUP, D], F32, local)
                v_hi = sb("v_hi", [P, GROUP, D], BF16, local)
                v_lo = sb("v_lo", [P, GROUP, D], BF16, local)
                c_hi = sb("c_hi", [P, 2, GROUP, LAT], BF16, local)
                c_lo = sb("c_lo", [P, 2, GROUP, LAT], BF16, local)
                hidden = sb("hidden", [P, 2, LAT], F32, local)
                gates = sb("gates_in", [P, 2, LAT // BLOCK, GROUP, BLOCK], F32, local)
                W = ext["weights"]
                with nc.Block() as block:
                    @block.vector
                    def _(dve):
                        dve_done.mark(nc.vector.memset(y_sum[:], 0.0))
                        nc.vector.memset(hidden[:, 0, 0:1], 0.0).then_inc(gelu_done, 4)
                        nc.vector.memset(hidden[:, 0, 1:2], 0.0).then_inc(coef_done, 2)
                        nc.vector.memset(hidden[:, 0, 2:3], 0.0).then_inc(y_done, 16)
                        nc.vector.memset(hidden[:, 0, 3:4], 0.0).then_inc(y_added, 4)

                with nc.Block() as block:
                    @block.sync
                    def _(sp):
                        def load_u(g):
                            for j in range(GROUP):
                                sp.wait_ge(split_done, (g - 1) * GROUP + (base + j + 1))
                                sp.dma_start(w_raw[:, j], W[g * (2 * GROUP) + (base + j)]).then_inc(raw_ready[j], 16)

                        def load_v(g):
                            for j in range(GROUP):
                                sp.dma_start(v_raw[:, j], W[g * (2 * GROUP) + (base + GROUP + j)]).then_inc(v_ready[j], 16)

                        def load_gates(g, b):
                            src = expert_gates[:, :, bass.ds(g * GROUP, GROUP), :].rearrange("n p k t -> p n (k t)")
                            sp.dma_start(gates[:, b].rearrange("p n k t -> p n (k t)"), src).then_inc(gates_ready[b], 16)

                        def ahead(g, b):
                            load_u(g + 1)
                            sp.wait_ge(coef_done, g * GROUP + 2)
                            load_gates(g + 1, 1 - b)
                            for j in range(GROUP):
                                sp.wait_ge(v_split, g * GROUP + (j + 1))
                                sp.dma_start(v_raw[:, j], W[g * (2 * GROUP) + (base + 3 * GROUP + j)]).then_inc(v_ready[j], 16)

                        load_gates(0, 0)
                        load_v(0)
                        with sp.Fori(0, n_groups // 2 - 1) as i:
                            for b in range(2):
                                ahead(i * 2 + b, b)
                        ahead(n_groups - 2, 0)

                    @block.scalar
                    def _(act):
                        def high_u(g, j):
                            act.wait_ge(raw_ready[j], g * 16 + 16 * (base // RING + 1))
                            act.wait_ge(slot_free, g * GROUP + (base + j + 1))
                            nc.scalar.activation(w_hi[:, j], w_raw[:, j], ACT.Copy).then_inc(hi_done, 1)

                        def group(g, b, more=True):
                            for j in range(GROUP):
                                act.wait_ge(slot_free, g * GROUP + (base + RING + j + 1))
                                act.wait_ge(coef_done, g * GROUP + (j + 1))
                                nc.scalar.activation(hidden[:, j % 2], ps[:, j, :], ACT.Gelu).then_inc(gelu_done, 1)
                                if more:
                                    high_u(g + 1, j)
                                act.wait_ge(weighed, g * GROUP + (j + 1))
                                act.wait_ge(y_done, g * KC + 8)
                                nc.scalar.activation(c_hi[:, b, j], hidden[:, j % 2], ACT.Copy).then_inc(coef_hi_done, 1)
                            for j in range(GROUP):
                                act.wait_ge(v_ready[j], g * 16 + 16)
                                act.wait_ge(y_done, g * KC + 16)
                                nc.scalar.activation(v_hi[:, j], v_raw[:, j], ACT.Copy).then_inc(v_hi_done, 1)

                        for j in range(GROUP):
                            high_u(0, j)
                        with act.Fori(0, n_groups // 2 - 1) as i:
                            for b in range(2):
                                group(i * 2 + b, b)
                        group(n_groups - 2, 0)
                        group(n_groups - 1, 1, False)

                    @block.gpsimd
                    def _(pool):
                        def low_u(g):
                            for j in range(GROUP):
                                pool.wait_ge(hi_done, g * GROUP + (base + j + 1))
                                nc.gpsimd.tensor_tensor(w_lo[:, j], w_raw[:, j], w_hi[:, j], ALU.subtract).then_inc(split_done, 1)

                        def low_v(g):
                            for j in range(GROUP):
                                pool.wait_ge(v_hi_done, g * GROUP + (j + 1))
                                nc.gpsimd.tensor_tensor(v_lo[:, j], v_raw[:, j], v_hi[:, j], ALU.subtract).then_inc(v_split, 1)

                        low_u(0)
                        with pool.Fori(0, n_groups - 1) as i:
                            low_u(i + 1)
                            low_v(i)
                        low_v(n_groups - 1)

                    @block.tensor
                    def _(pe):
                        def up(g):
                            for j in range(GROUP):
                                pe.wait_ge(split_done, g * GROUP + (base + j + 1))
                                pe.wait_ge(gelu_done, g * GROUP + (j + 1))
                                for k in range(KC):
                                    for part, (w, x) in enumerate(((w_hi, x_hi), (w_hi, x_lo), (w_lo, x_hi))):
                                        mm = nc.tensor.matmul(ps[:, j, :], w[:, j, k * P:(k + 1) * P], x[:, k, 0:LAT],
                                                              start=(k == 0 and part == 0), stop=(k == KC - 1 and part == 2))
                                mm.then_inc(slot_free, 1)

                        def down(g, b):
                            pe.wait_ge(coef_done, g * GROUP + (2 + GROUP))
                            pe.wait_ge(v_split, g * GROUP + GROUP)
                            for k in range(KC):
                                pe.wait_ge(y_added, g * KC + (k + 1))
                                for j in range(GROUP):
                                    for part, (v, c) in enumerate(((v_hi, c_hi), (v_hi, c_lo), (v_lo, c_hi))):
                                        mm = nc.tensor.matmul(ps[:, 4 + k % 4, :], v[:, j, k * P:(k + 1) * P], c[:, b, j, :],
                                                              start=(j == 0 and part == 0), stop=(j == GROUP - 1 and part == 2))
                                mm.then_inc(y_done, 1)

                        up(0)
                        with pe.Fori(0, n_groups // 2 - 1) as i:
                            up(i * 2 + 1)
                            down(i * 2, 0)
                            up(i * 2 + 2)
                            down(i * 2 + 1, 1)
                        up(n_groups - 1)
                        down(n_groups - 2, 0)
                        down(n_groups - 1, 1)

                    @block.vector
                    def _(dve):
                        def weigh(g, b, pair):
                            for j in range(GROUP):
                                if j == 0:
                                    dve.wait_ge(gates_ready[b], pair * 16 + 16)
                                dve.wait_ge(gelu_done, g * GROUP + (j + 5))
                                r3 = hidden[:, j % 2].rearrange("p (n t) -> p n t", t=BLOCK)
                                nc.vector.tensor_tensor(r3, r3, gates[:, b, :, j, :], ALU.mult).then_inc(weighed, 1)
                                dve.wait_ge(coef_hi_done, g * GROUP + (j + 1))
                                nc.vector.tensor_tensor(c_lo[:, b, j], hidden[:, j % 2], c_hi[:, b, j], ALU.subtract).then_inc(coef_done, 1)

                        def add(g):
                            dve.wait_ge(y_added, g * KC + 4)
                            for k in range(KC):
                                dve.wait_ge(y_done, g * KC + (17 + k))
                                nc.vector.tensor_tensor(y_sum[:, k], y_sum[:, k], ps[:, 4 + k % 4, :], ALU.add).then_inc(y_added, 1)

                        weigh(0, 0, 0)
                        with dve.Fori(0, n_groups // 2 - 1) as i:
                            weigh(i * 2 + 1, 1, i)
                            add(i * 2)
                            weigh(i * 2 + 2, 0, i + 1)
                            add(i * 2 + 1)
                        weigh(n_groups - 1, 1, n_groups // 2 - 1)
                        add(n_groups - 2)
                        add(n_groups - 1)

        def first_block():
            modulate_parts(0, 0, TOK)
            attention()
            normalise(TOK, LN_EPS / ALPHA ** 2, True, "mix_g0", "mix_b0", then=(0, 3))
            mlp(0, TOK)
            mods_finish(1, 0)
            mod_stack.close()
            normalise(TOK, LN_EPS / ALPHA ** 2, True, "ff_g0", "ff_b0", then=(1, 0))
            with ExitStack() as outer:
                y_tok = sb("x_tok", [P, TB, SINNER], F32, outer)
                with ExitStack() as local:
                    ssm(y_tok, local)
                mods_finish(2, 0)
                modulate_parts(1, 0, LAT)
                ssm_finish(y_tok)
            normalise(LAT, LN_EPS / ALPHA ** 2, True, "mix_g1", "mix_b1", then=(1, 3))
            mlp(1, LAT)
            normalise(LAT, LN_EPS / ALPHA ** 2, True, "ff_g1", "ff_b1")

        def second_block():
            load_and_wait([(h[:, :, LAT:TOK], ext["context2"])])
            normalise(TOK, EPS, False, "norm_g0", then=(2, 0))
            deltanet()
            peer()

        first_block()
        second_block()


def constants():
    import numpy as np
    i = np.arange(P)
    row, col = i[:, None], i[None, :]
    swap = (i // 32) * 32 + (i % 32 + 16) % 32
    table = {
        "identity": row == col, "ones": row * 0 + col * 0 + 1.0, "mean": np.full((P, P), 1.0 / D),
        "rope_swap": row == swap[None, :],
        "mask_before": np.where(col >= row, 0.0, NEG),
        "mask_same": np.zeros((P, P)),
        "mask_after": np.where(col <= row, 0.0, NEG),
        "sum_upto": row <= col, "sum_from": row >= col,
        "strict_lower": row > col, "strict_upper": row < col,
        "group_mean": np.full((P, P), 1.0 / 512), "head_mean": np.full((P, P), 1.0 / P),
        "iota": row * 0 + col,
    }
    squares = np.stack([table[n].astype(np.float32) * np.ones((P, P), np.float32) for n in SQUARES], 1)
    levels = np.zeros((P, 7, 2 * P), np.float32)
    for l in range(6):
        size = 2 << l
        for d in range(2):
            levels[:, l, d * P:(d + 1) * P] = ((row // (2 * size) == col // (2 * size)) & (row // size % 2 == d)
                                               & (col // size % 2 == 1 - d))
    levels[:, 6, 0:P] = -1.0 * ((row % 2 == 0) & (col == row + 1))
    levels[:, 6, P:] = -1.0 * ((row % 2 == 1) & (col == row - 1))
    pos = np.arange(LAT)
    inv = (10000.0 ** (-np.arange(0, 32, 2, dtype=np.float32) / 32)).astype(np.float32)
    d = i % 64
    where = np.where(d < 32, 1, 0)[:, None] * (pos // 64)[None, :] + np.where(d >= 32, 1, 0)[:, None] * (pos % 64)[None, :]
    angle = where.astype(np.float32) * inv[d % 16][:, None]
    sign = np.where(d % 32 < 16, -1.0, 1.0)[:, None]
    rope = np.stack([np.cos(angle), sign * np.sin(angle)], 1).astype(np.float32)
    return squares, rope, levels


def head_order():
    return [4 * (2 * (j // 4) + f) + j % 4 for j in range(8) for f in range(2)]


def tiles_of(w):
    import numpy as np
    k, n = w.shape
    return np.ascontiguousarray(w.reshape(k // D, KC, P, n // P, P).transpose(3, 0, 2, 1, 4)).reshape(-1, P, D)


def layout(inputs):
    import numpy as np

    a = {k: np.asarray(v) for k, v in inputs.items()}
    heads = head_order()
    order = np.concatenate([np.arange(HD) + HD * q for q in heads])
    w_in = a["att_w_in"][0]
    att_in = np.concatenate([w_in[:, :D][:, order], w_in[:, D:]], 1)
    u = a["peer_u_2"].reshape(P, P, D)
    u_t = np.ascontiguousarray(u.transpose(1, 2, 0)).reshape(P, KC, P, P).transpose(0, 2, 1, 3).reshape(P, P, D)
    v_t = a["peer_v_2"].reshape(P, P, D).transpose(1, 0, 2)
    experts = np.stack([u_t.reshape(-1, GROUP, P, D), v_t.reshape(-1, GROUP, P, D)], 1).reshape(-1, P, D)
    ssm_in, dn_in = a["ssm_w_in"][0], a["dn_w_in_2"][0]
    stream = {
        "att_in": att_in, "att_out": a["att_w_out"][0][order], "ff1_0": a["ff_w1"][0], "ff2_0": a["ff_w2"][0],
        "ssm_z": ssm_in[:, :SINNER], "ssm_x": ssm_in[:, SINNER:2 * SINNER], "ssm_bc": ssm_in[:, 2 * SINNER:SINNER + SCONV],
        "ssm_out": a["ssm_w_out"][0],
        "ff1_1": a["ff_w1"][1], "ff2_1": a["ff_w2"][1], "dn_q": dn_in[:, :D], "dn_k": dn_in[:, D:2 * D], "dn_v": dn_in[:, 2 * D:3 * D],
        "dn_gate": dn_in[:, 3 * D:4 * D],
        "dn_out": a["dn_w_out_2"][0], "w_q": a["peer_w_q_2"][0],
    }
    weights = np.concatenate([tiles_of(stream[n]) for n, _, _ in STREAM] + [experts], 0)

    def cols(v):
        return np.asarray(v).reshape(-1, P).T

    vectors = {
        "c": a["c"], "c_ctx": a["c_ctx"], "c2": a["c_2"], "c2_ctx": a["c_ctx_2"],
        "b_mod0": a["b_mod"][0], "b_mod1": a["b_mod"][1], "b_ada": a["ada_b_2"],
        "mix_g0": a["ln_mix_g"][0], "mix_g1": a["ln_mix_g"][1], "mix_b0": a["ln_mix_b"][0], "mix_b1": a["ln_mix_b"][1],
        "ff_g0": a["ln_ff_g"][0], "ff_g1": a["ln_ff_g"][1], "ff_b0": a["ln_ff_b"][0], "ff_b1": a["ln_ff_b"][1],
        "norm_g0": a["norm_g_2"][0, 0], "norm_g1": a["norm_g_2"][0, 1], "final_g": a["final_g_2"],
        "conv_w": a["ssm_conv_w"][0], "conv_b": a["ssm_conv_b"], "ssm_norm_g": a["ssm_norm_g"],
        "dn_conv_w": a["dn_conv_w_2"][0],
        "dn_norm_g": a["dn_norm_g_2"],
    }
    squares, rope, levels = constants()
    tokens = np.concatenate([a["x"][0], a["ctx"][0]], 0)
    everywhere = lambda v: np.ascontiguousarray(np.broadcast_to(np.asarray(v).reshape(1, -1), (P, v.size)))
    by_chunk = lambda w: np.ascontiguousarray(w.reshape(KC, P, -1).transpose(1, 0, 2))
    return {
        "weights": weights,
        "mod_weights": np.concatenate([tiles_of(w) for w in (a["w_mod"][0], a["w_mod"][1], a["ada_w_2"][0])], 0),
        "vectors": np.ascontiguousarray(np.concatenate([cols(vectors[n]) for n, _ in VECTORS], 1)),
        "squares": squares, "rope": rope, "level_masks": levels,
        "tokens": np.ascontiguousarray(tokens.T.reshape(KC, P, TOK).transpose(1, 0, 2)),
        "context2": np.ascontiguousarray(a["ctx_2"][0].T.reshape(KC, P, CTX).transpose(1, 0, 2)),
        "sinks": everywhere(a["att_sink"][0][heads]),
        "ssm_d": everywhere(a["ssm_d"][0]),
        "dt_w": by_chunk(a["ssm_w_in"][0][:, SINNER + SCONV:]),
        "dt_rows": np.concatenate([everywhere(a["ssm_dt_bias"][0]), everywhere(a["ssm_a_log"][0])], 1),
        "ba_w": by_chunk(a["dn_w_in_2"][0][:, 4 * D:]),
        "ba_rows": np.concatenate([everywhere(a["dn_dt_bias_2"][0]), everywhere(a["dn_a_log_2"][0])], 1),
        "keys": np.ascontiguousarray(a["peer_keys_2"][0].transpose(3, 0, 1, 2)),
    }


def kernel(**inputs):
    import numpy as np
    import concourse.bacc as bacc
    from concourse.bass_utils import run_bass_kernel_spmd

    arrays = layout(inputs)
    nc = bacc.Bacc("TRN2", target_bir_lowering=False, num_devices=1)
    ext = {n: nc.dram_tensor("in_" + n, v.shape, mybir.dt.from_np(v.dtype), kind="ExternalInput").ap() for n, v in arrays.items()}
    out = nc.dram_tensor("out", (KC, P, LAT), F32, kind="ExternalOutput").ap()
    build(nc, ext, out)
    r = run_bass_kernel_spmd(nc, [{"in_" + n: v for n, v in arrays.items()}], core_ids=[0])
    return np.ascontiguousarray(r.results[0]["out"].reshape(D, LAT).T).reshape(1, LAT, D)
```
